# Optimizing a Trainium2 kernel written in Bass

```python
import math
import numpy as np
import jax
import jax.numpy as jnp
from jax import lax
import math, functools
import jax, jax.numpy as jnp

D_MODEL = 1024
BATCH = 1
SEQ = 256
DEPTH = 2

D_MIX = D_MODEL
SSD_WIDTH = D_MIX // 2
SSD_HEAD_DIM = 64
SSD_HEADS = SSD_WIDTH // SSD_HEAD_DIM
SSD_GROUPS = 2
SSD_STATE = 64
SSD_CONV = 4
SSD_CONV_DIM = SSD_WIDTH + 2 * SSD_GROUPS * SSD_STATE
SSD_CHUNK = 128
DT_MIN = 0.001
DT_MAX = 0.1
HGRN_WIDTH = D_MIX // 4
HGRN_HEAD_DIM = 64
HGRN_HEADS = HGRN_WIDTH // HGRN_HEAD_DIM
HGRN_CHUNK = 16
GATE_FLOOR = 1e-30
RET_WIDTH = D_MIX // 4
RET_HEAD_DIM = 64
RET_HEADS = RET_WIDTH // RET_HEAD_DIM
RET_CHUNK = 128
ROPE_BASE = 10000.0
IN_WIDTHS = (SSD_WIDTH, SSD_CONV_DIM, SSD_HEADS,
             HGRN_WIDTH, HGRN_WIDTH, HGRN_WIDTH, HGRN_WIDTH,
             RET_WIDTH, RET_WIDTH, RET_WIDTH, RET_WIDTH)
D_IN = SSD_WIDTH + SSD_CONV_DIM + SSD_HEADS + 4 * HGRN_WIDTH + 4 * RET_WIDTH
N_GROUPS = 4
EXPERTS_PER_GROUP = 8
N_EXPERTS = N_GROUPS * EXPERTS_PER_GROUP
TOP_K = 2
D_EXPERT = D_MODEL // 4
ADA_SCALE = 0.5
EPS = 1e-6


def rms(x):
    xf = x.astype(jnp.float32)
    return xf * lax.rsqrt(jnp.mean(xf * xf, axis=-1, keepdims=True) + EPS)

def rmsnorm(x, g):
    return rms(x) * g

def causal_depthwise_conv(x, w, bias):
    width, ch = w.shape
    out = lax.conv_general_dilated(
        x, w[:, None, :].astype(x.dtype), window_strides=(1,), padding=[(width - 1, 0)],
        dimension_numbers=('NWC', 'WIO', 'NWC'), feature_group_count=ch)
    return out + bias

def rotary(x, pos):
    half = x.shape[-1] // 2
    inv_freq = ROPE_BASE ** (-jnp.arange(half, dtype=jnp.float32) / half)
    ang = pos[:, None] * inv_freq[None, :]
    cos = jnp.cos(ang)[None, :, None, :]
    sin = jnp.sin(ang)[None, :, None, :]
    x1 = x[..., :half].astype(jnp.float32)
    x2 = x[..., half:].astype(jnp.float32)
    return jnp.concatenate([x1 * cos - x2 * sin, x1 * sin + x2 * cos], axis=-1)

def chunked_linear_recurrence(q, k, v, log_a, chunk):
    b, l, h, dk = q.shape
    dv = v.shape[-1]
    nc = l // chunk
    q, k, v, log_a = (t.astype(jnp.float32).reshape(b, nc, chunk, h, t.shape[-1])
                      for t in (q, k, v, log_a))
    cum = jnp.cumsum(log_a, axis=2)
    causal = jnp.tril(jnp.ones((chunk, chunk), dtype=bool))
    if log_a.shape[-1] == 1:
        cs = jnp.moveaxis(cum[..., 0], 2, 3)
        diff = cs[..., :, None] - cs[..., None, :]
        decay = jnp.where(causal, jnp.exp(jnp.where(causal, diff, 0.0)), 0.0)
        scores = jnp.einsum('bcthk,bcshk->bchts', q, k) * decay
    else:
        diff = cum[:, :, :, None] - cum[:, :, None]
        m = causal[:, :, None, None]
        decay = jnp.where(m, jnp.exp(jnp.where(m, diff, 0.0)), 0.0)
        scores = jnp.einsum('bcthk,bcshk,bctshk->bchts', q, k, decay)
    o_intra = jnp.einsum('bchts,bcshv->bcthv', scores, v)
    k_end = k * jnp.exp(cum[:, :, -1:] - cum)
    chunk_states = jnp.einsum('bcshk,bcshv->bchkv', k_end, v)
    chunk_decay = jnp.exp(cum[:, :, -1])

    def carry_state(s, inp):
        a, s_c = inp
        return a[..., None] * s + s_c, s

    _, s_prev = lax.scan(carry_state, jnp.zeros((b, h, dk, dv), jnp.float32),
                         (jnp.moveaxis(chunk_decay, 1, 0), jnp.moveaxis(chunk_states, 1, 0)))
    s_prev = jnp.moveaxis(s_prev, 0, 1)
    o_inter = jnp.einsum('bcthk,bchkv->bcthv', q * jnp.exp(cum), s_prev)
    return (o_intra + o_inter).reshape(b, l, h, dv)

def token_mixer(h, w_in, conv_w, conv_b, dt_bias, a_log, d_skip, ssd_norm_g,
                lower_bound, hgrn_norm_g, w_out):
    b, l, _ = h.shape
    proj = h @ w_in
    offsets = np.cumsum(IN_WIDTHS)[:-1].tolist()
    z, xbc, dt, hq, hf, hi, hg, rq, rk, rv, rg = jnp.split(proj, offsets, axis=-1)

    def heads(t, n):
        return t.reshape(b, l, n, -1)

    xbc = jax.nn.silu(causal_depthwise_conv(xbc, conv_w, conv_b))
    xs, bm, cm = jnp.split(xbc, [SSD_WIDTH, SSD_WIDTH + SSD_GROUPS * SSD_STATE], axis=-1)
    rep = SSD_HEADS // SSD_GROUPS
    xs = heads(xs, SSD_HEADS)
    bm = jnp.repeat(heads(bm, SSD_GROUPS), rep, axis=2)
    cm = jnp.repeat(heads(cm, SSD_GROUPS), rep, axis=2)
    dt = jax.nn.softplus(dt.astype(jnp.float32) + dt_bias)
    log_a = (dt * -jnp.exp(a_log.astype(jnp.float32)))[..., None]
    y = chunked_linear_recurrence(cm, bm, xs * dt[..., None], log_a, SSD_CHUNK)
    y = y + d_skip[:, None] * xs
    y = y * jax.nn.silu(heads(z, SSD_HEADS).astype(jnp.float32))
    y_ssd = rmsnorm(y.reshape(b, l, SSD_GROUPS, -1),
                    ssd_norm_g.reshape(SSD_GROUPS, -1)).reshape(b, l, SSD_WIDTH)

    raw = hf.astype(jnp.float32)
    forget = lower_bound + (1.0 - lower_bound) * jax.nn.sigmoid(raw)
    log_f = jnp.log(jnp.maximum(forget, GATE_FLOOR))
    k_in = 1.0 - forget
    o = chunked_linear_recurrence(heads(hq, HGRN_HEADS), heads(k_in, HGRN_HEADS),
                                  heads(hi, HGRN_HEADS), heads(log_f, HGRN_HEADS), HGRN_CHUNK)
    o = rmsnorm(o, hgrn_norm_g.reshape(HGRN_HEADS, HGRN_HEAD_DIM))
    o_hgrn = (o * jax.nn.sigmoid(heads(hg, HGRN_HEADS).astype(jnp.float32))).reshape(b, l, HGRN_WIDTH)

    pos = jnp.arange(l, dtype=jnp.float32)
    q_r = rotary(heads(rq, RET_HEADS), pos)
    k_r = rotary(heads(rk, RET_HEADS), pos) * RET_HEAD_DIM ** -0.5
    log_gamma = jnp.log1p(-jnp.exp2(-5.0 - jnp.arange(RET_HEADS, dtype=jnp.float32)))
    log_g = jnp.broadcast_to(log_gamma[:, None], (b, l, RET_HEADS, 1))
    o = chunked_linear_recurrence(q_r, k_r, heads(rv, RET_HEADS), log_g, RET_CHUNK)
    o_ret = (rms(o) * jax.nn.silu(heads(rg, RET_HEADS).astype(jnp.float32))).reshape(b, l, RET_WIDTH)

    mixed = jnp.concatenate([y_ssd, o_hgrn, o_ret], axis=-1).astype(h.dtype)
    return mixed @ w_out

def hierarchical_moe(h, w_grp, b_grp, w_exp, b_exp, w_gate, w_up, w_down):
    b, l, d = h.shape
    t = h.reshape(b * l, d)
    grp_logits = (t @ w_grp + b_grp).astype(jnp.float32)
    grp_prob = jax.nn.softmax(grp_logits, axis=-1)
    g_idx = jnp.argmax(grp_logits, axis=-1)
    p_grp = jnp.max(grp_prob, axis=-1, keepdims=True)
    exp_logits = (t @ w_exp + b_exp).astype(jnp.float32).reshape(-1, N_GROUPS, EXPERTS_PER_GROUP)
    in_grp = jnp.einsum('tg,tge->te', jax.nn.one_hot(g_idx, N_GROUPS, dtype=jnp.float32), exp_logits)
    top_logit, top_idx = lax.top_k(in_grp, TOP_K)
    weights = jax.nn.softmax(top_logit, axis=-1) * p_grp
    expert_id = g_idx[:, None] * EXPERTS_PER_GROUP + top_idx
    combine = jnp.einsum('tk,tke->te', weights,
                         jax.nn.one_hot(expert_id, N_EXPERTS, dtype=jnp.float32)).astype(t.dtype)
    y = jnp.zeros_like(t)
    for gi in range(N_GROUPS):
        sl = slice(gi * EXPERTS_PER_GROUP, (gi + 1) * EXPERTS_PER_GROUP)
        hid = jax.nn.silu(jnp.einsum('td,edf->tef', t, w_gate[sl])) * jnp.einsum('td,edf->tef', t, w_up[sl])
        y = y + jnp.einsum('tef,efd->td', hid * combine[:, sl, None], w_down[sl])
    return y.reshape(b, l, d)

def first_inputs(seed: int = 0) -> dict:
    key = jax.random.key(seed)
    ks = jax.random.split(key, 24)
    f32 = jnp.float32

    def nrm(k, shape, scale):
        return scale * jax.random.normal(k, shape, f32)

    dt0 = jnp.exp(jax.random.uniform(ks[9], (DEPTH, SSD_HEADS), f32, math.log(DT_MIN), math.log(DT_MAX)))
    return {
        'x': nrm(ks[0], (BATCH, SEQ, D_MODEL), 1.0),
        'c': nrm(ks[1], (BATCH, D_MODEL), 1.0),
        'norm_mix_g': 1.0 + nrm(ks[2], (DEPTH, D_MODEL), 0.02),
        'norm_ffn_g': 1.0 + nrm(ks[3], (DEPTH, D_MODEL), 0.02),
        'final_norm_g': 1.0 + nrm(ks[4], (D_MODEL,), 0.02),
        'w_ada': nrm(ks[5], (DEPTH, D_MODEL, 6 * D_MODEL), ADA_SCALE * D_MODEL ** -0.5),
        'b_ada': nrm(ks[6], (DEPTH, 6 * D_MODEL), 0.02),
        'w_in': nrm(ks[7], (DEPTH, D_MODEL, D_IN), D_MODEL ** -0.5),
        'conv_w': nrm(ks[8], (DEPTH, SSD_CONV, SSD_CONV_DIM), SSD_CONV ** -0.5),
        'conv_b': nrm(ks[10], (DEPTH, SSD_CONV_DIM), 0.02),
        'ssd_dt_bias': dt0 + jnp.log(-jnp.expm1(-dt0)),
        'ssd_a_log': jnp.log(jax.random.uniform(ks[11], (DEPTH, SSD_HEADS), f32, 1.0, 16.0)),
        'ssd_d': 1.0 + nrm(ks[12], (DEPTH, SSD_HEADS), 0.1),
        'ssd_norm_g': 1.0 + nrm(ks[13], (DEPTH, SSD_WIDTH), 0.02),
        'hgrn_lower_bounds': nrm(ks[14], (DEPTH, HGRN_WIDTH), 0.1),
        'hgrn_norm_g': 1.0 + nrm(ks[15], (DEPTH, HGRN_WIDTH), 0.02),
        'w_out': nrm(ks[16], (DEPTH, D_MIX, D_MODEL), D_MIX ** -0.5),
        'w_grp': nrm(ks[17], (DEPTH, D_MODEL, N_GROUPS), D_MODEL ** -0.5),
        'b_grp': nrm(ks[18], (DEPTH, N_GROUPS), 0.01),
        'w_exp': nrm(ks[19], (DEPTH, D_MODEL, N_EXPERTS), D_MODEL ** -0.5),
        'b_exp': nrm(ks[20], (DEPTH, N_EXPERTS), 0.01),
        'w_gate': nrm(ks[21], (DEPTH, N_EXPERTS, D_MODEL, D_EXPERT), D_MODEL ** -0.5),
        'w_up': nrm(ks[22], (DEPTH, N_EXPERTS, D_MODEL, D_EXPERT), D_MODEL ** -0.5),
        'w_down': nrm(ks[23], (DEPTH, N_EXPERTS, D_EXPERT, D_MODEL), D_EXPERT ** -0.5),
    }

def first_block(x, c, norm_mix_g, norm_ffn_g, final_norm_g, w_ada, b_ada, w_in, conv_w, conv_b,
              ssd_dt_bias, ssd_a_log, ssd_d, ssd_norm_g, hgrn_lower_bounds, hgrn_norm_g, w_out,
              w_grp, b_grp, w_exp, b_exp, w_gate, w_up, w_down):
    lb_soft = jax.nn.softmax(hgrn_lower_bounds.astype(jnp.float32), axis=0)
    lower_bound = jnp.cumsum(lb_soft, axis=0) - lb_soft[0]
    c_act = jax.nn.silu(c)
    for layer in range(DEPTH):
        mod = c_act @ w_ada[layer] + b_ada[layer]
        sh_mix, sc_mix, g_mix, sh_ffn, sc_ffn, g_ffn = jnp.split(mod[:, None, :], 6, axis=-1)
        h = (rmsnorm(x, norm_mix_g[layer]) * (1.0 + sc_mix) + sh_mix).astype(x.dtype)
        mixed = token_mixer(h, w_in[layer], conv_w[layer], conv_b[layer], ssd_dt_bias[layer],
                            ssd_a_log[layer], ssd_d[layer], ssd_norm_g[layer], lower_bound[layer],
                            hgrn_norm_g[layer], w_out[layer])
        x = x + (g_mix * mixed).astype(x.dtype)
        h = (rmsnorm(x, norm_ffn_g[layer]) * (1.0 + sc_ffn) + sh_ffn).astype(x.dtype)
        moe = hierarchical_moe(h, w_grp[layer], b_grp[layer], w_exp[layer], b_exp[layer],
                               w_gate[layer], w_up[layer], w_down[layer])
        x = x + (g_ffn * moe).astype(x.dtype)
    return rmsnorm(x, final_norm_g).astype(x.dtype)


N_MIXERS = 2
N_A = (DEPTH + 1) // 2
N_B = DEPTH // 2
D_RNN = D_MODEL
RG_BLOCKS = 4
RG_BLOCK = D_RNN // RG_BLOCKS
RG_CONV = 4
RG_C = 8.0
GLA_HEADS = 4
GLA_DK = D_MODEL // 2 // GLA_HEADS
GLA_DV = D_MODEL // GLA_HEADS
GLA_RANK = 16
GLA_TAU = 16.0
GLA_CHUNK = 64
GLA_QK = GLA_HEADS * GLA_DK
GLA_IN = 2 * GLA_QK + 2 * D_MODEL + GLA_RANK
D_FF = ((8 * D_MODEL // 3 + 127) // 128) * 128
FFN_CONV = 3


def rmsnorm_2(x, g):
    x32 = x.astype(jnp.float32)
    y = x32 * lax.rsqrt(jnp.mean(x32 * x32, axis=-1, keepdims=True) + EPS)
    return (y * g.astype(jnp.float32)).astype(x.dtype)

def causal_dwconv(x, w, b):
    k_width = w.shape[0]
    s = x.shape[1]
    xp = jnp.pad(x, ((0, 0), (k_width - 1, 0), (0, 0)))
    y = b
    for k in range(k_width):
        y = y + xp[:, k:k + s] * w[k]
    return y

def _lru_combine(left, right):
    a1, b1 = left
    a2, b2 = right
    return a1 * a2, a2 * b1 + b2

def rglru_mixer(h, w_in, conv_w, conv_b, wa, ba, wx, bx, lam, w_out):
    bsz, s, _ = h.shape
    gate_br, x_br = jnp.split(h @ w_in, 2, axis=-1)
    x_br = causal_dwconv(x_br, conv_w, conv_b)
    xb = x_br.reshape(bsz, s, RG_BLOCKS, RG_BLOCK)
    r = jax.nn.sigmoid(jnp.einsum('bsgi,gij->bsgj', xb, wa).reshape(bsz, s, D_RNN) + ba)
    i_g = jax.nn.sigmoid(jnp.einsum('bsgi,gij->bsgj', xb, wx).reshape(bsz, s, D_RNN) + bx)
    log_a = -RG_C * r.astype(jnp.float32) * jax.nn.softplus(-lam.astype(jnp.float32))
    a = jnp.exp(log_a)
    mult = jnp.sqrt(-jnp.expm1(2.0 * log_a))
    u = mult * (i_g * x_br).astype(jnp.float32)
    _, hs = lax.associative_scan(_lru_combine, (a, u), axis=1)
    y = jax.nn.gelu(gate_br) * hs.astype(h.dtype)
    return y @ w_out

def gla_chunk_scan(q, k, v, g):
    n_c, bsz, nh, cl, dk = q.shape
    dv = v.shape[-1]
    mask = jnp.tril(jnp.ones((cl, cl), dtype=bool))[:, :, None]

    def step(state, inp):
        qc, kc, vc, gc = inp
        big_g = jnp.cumsum(gc, axis=2)
        o_inter = jnp.einsum('bhcd,bhde->bhce', qc * jnp.exp(big_g), state)
        diff = big_g[:, :, :, None, :] - big_g[:, :, None, :, :]
        decay = jnp.exp(jnp.where(mask, diff, -jnp.inf))
        attn = jnp.einsum('bhid,bhjd,bhijd->bhij', qc, kc, decay)
        o_intra = jnp.einsum('bhij,bhje->bhie', attn, vc)
        g_last = big_g[:, :, -1:, :]
        state = jnp.exp(g_last[:, :, 0, :])[..., None] * state + jnp.einsum(
            'bhjd,bhje->bhde', kc * jnp.exp(g_last - big_g), vc)
        return state, o_inter + o_intra

    state0 = jnp.zeros((bsz, nh, dk, dv), jnp.float32)
    _, o = lax.scan(step, state0, (q, k, v, g))
    return o

def gla_mixer(h, w_in, w_alpha, b_alpha, norm_g, w_out):
    bsz, s, _ = h.shape
    proj = h @ w_in
    q, k, v, r, z = jnp.split(proj, [GLA_QK, 2 * GLA_QK, 2 * GLA_QK + D_MODEL,
                                     2 * GLA_QK + 2 * D_MODEL], axis=-1)
    log_alpha = jax.nn.log_sigmoid((z @ w_alpha + b_alpha).astype(jnp.float32)) / GLA_TAU
    n_c = s // GLA_CHUNK

    def to_chunks(t, d):
        return t.reshape(bsz, n_c, GLA_CHUNK, GLA_HEADS, d).transpose(1, 0, 3, 2, 4).astype(jnp.float32)

    o = gla_chunk_scan(to_chunks(q * (GLA_DK ** -0.5), GLA_DK), to_chunks(k, GLA_DK),
                       to_chunks(v, GLA_DV), to_chunks(log_alpha, GLA_DK))
    o = o.transpose(1, 0, 3, 2, 4).reshape(bsz, s, GLA_HEADS, GLA_DV)
    o = rmsnorm_2(o, norm_g).reshape(bsz, s, D_MODEL).astype(h.dtype)
    return (o * jax.nn.silu(r)) @ w_out

def conv_ffn(h, w_up, conv_w, conv_b, w_down):
    u = causal_dwconv(h @ w_up, conv_w, conv_b)
    g, val = jnp.split(u, 2, axis=-1)
    return (jax.nn.gelu(g) * val) @ w_down

def second_inputs(seed: int = 0) -> dict:
    key = jax.random.key(seed)
    ks = iter(jax.random.split(key, 32))

    def nrm(shape, scale):
        return jax.random.normal(next(ks), shape, jnp.float32) * scale

    d = D_MODEL
    x = nrm((BATCH, SEQ, d), 1.0)
    c = nrm((BATCH, d), 1.0)
    ada_w = nrm((DEPTH, d, 6 * d), d ** -0.5)
    ada_b = nrm((DEPTH, 6 * d), 0.01)
    norm_g = 1.0 + nrm((DEPTH, 4, d), 0.05)
    ffn_w_up = nrm((DEPTH, d, 2 * D_FF), d ** -0.5)
    ffn_conv_w = nrm((DEPTH, FFN_CONV, 2 * D_FF), FFN_CONV ** -0.5)
    ffn_conv_b = nrm((DEPTH, 2 * D_FF), 0.01)
    ffn_w_down = nrm((DEPTH, D_FF, d), D_FF ** -0.5)
    rg_w_in = nrm((N_A, d, 2 * D_RNN), d ** -0.5)
    rg_conv_w = nrm((N_A, RG_CONV, D_RNN), RG_CONV ** -0.5)
    rg_conv_b = nrm((N_A, D_RNN), 0.01)
    rg_wa = nrm((N_A, RG_BLOCKS, RG_BLOCK, RG_BLOCK), RG_BLOCK ** -0.5)
    rg_ba = nrm((N_A, D_RNN), 0.01)
    rg_wx = nrm((N_A, RG_BLOCKS, RG_BLOCK, RG_BLOCK), RG_BLOCK ** -0.5)
    rg_bx = nrm((N_A, D_RNN), 0.01)
    a_pow = jax.random.uniform(next(ks), (N_A, D_RNN), jnp.float32, 0.9, 0.999)
    a_base = a_pow ** (1.0 / RG_C)
    rg_lambda = jnp.log(a_base) - jnp.log1p(-a_base)
    rg_w_out = nrm((N_A, D_RNN, d), D_RNN ** -0.5)
    gla_w_in = nrm((N_B, d, GLA_IN), d ** -0.5)
    gla_w_alpha = nrm((N_B, GLA_RANK, GLA_QK), GLA_RANK ** -0.5)
    gla_b_alpha = nrm((N_B, GLA_QK), 0.01)
    gla_norm_g = 1.0 + nrm((N_B, GLA_DV), 0.05)
    gla_w_out = nrm((N_B, d, d), d ** -0.5)
    return {"x": x, "c": c, "ada_w": ada_w, "ada_b": ada_b, "norm_g": norm_g,
            "ffn_w_up": ffn_w_up, "ffn_conv_w": ffn_conv_w, "ffn_conv_b": ffn_conv_b,
            "ffn_w_down": ffn_w_down, "rg_w_in": rg_w_in, "rg_conv_w": rg_conv_w,
            "rg_conv_b": rg_conv_b, "rg_wa": rg_wa, "rg_ba": rg_ba, "rg_wx": rg_wx,
            "rg_bx": rg_bx, "rg_lambda": rg_lambda, "rg_w_out": rg_w_out,
            "gla_w_in": gla_w_in, "gla_w_alpha": gla_w_alpha, "gla_b_alpha": gla_b_alpha,
            "gla_norm_g": gla_norm_g, "gla_w_out": gla_w_out}

def second_block(x, c, ada_w, ada_b, norm_g, ffn_w_up, ffn_conv_w, ffn_conv_b, ffn_w_down,
              rg_w_in, rg_conv_w, rg_conv_b, rg_wa, rg_ba, rg_wx, rg_bx, rg_lambda, rg_w_out,
              gla_w_in, gla_w_alpha, gla_b_alpha, gla_norm_g, gla_w_out):
    c_act = jax.nn.silu(c)
    for i in range(DEPTH):
        mod = (c_act @ ada_w[i] + ada_b[i])[:, None, :]
        sh_m, sc_m, gt_m, sh_f, sc_f, gt_f = jnp.split(mod, 6, axis=-1)
        j = i // N_MIXERS
        h = rmsnorm_2(x, norm_g[i, 0]) * (1.0 + sc_m) + sh_m
        if i % N_MIXERS == 0:
            y = rglru_mixer(h, rg_w_in[j], rg_conv_w[j], rg_conv_b[j], rg_wa[j], rg_ba[j],
                            rg_wx[j], rg_bx[j], rg_lambda[j], rg_w_out[j])
        else:
            y = gla_mixer(h, gla_w_in[j], gla_w_alpha[j], gla_b_alpha[j], gla_norm_g[j], gla_w_out[j])
        x = x + gt_m * rmsnorm_2(y, norm_g[i, 1])
        h = rmsnorm_2(x, norm_g[i, 2]) * (1.0 + sc_f) + sh_f
        y = conv_ffn(h, ffn_w_up[i], ffn_conv_w[i], ffn_conv_b[i], ffn_w_down[i])
        x = x + gt_f * rmsnorm_2(y, norm_g[i, 3])
    return x


def setup_inputs(seed=0):
    out = dict(first_inputs(seed))
    for name, value in second_inputs(seed + 1).items():
        if name != "x":
            out[name + "_2"] = value
    return out


def reference(
    x, c, norm_mix_g, norm_ffn_g, final_norm_g, w_ada, b_ada, w_in, conv_w, conv_b, ssd_dt_bias,
    ssd_a_log, ssd_d, ssd_norm_g, hgrn_lower_bounds, hgrn_norm_g, w_out, w_grp, b_grp, w_exp,
    b_exp, w_gate, w_up, w_down, c_2, ada_w_2, ada_b_2, norm_g_2, ffn_w_up_2, ffn_conv_w_2,
    ffn_conv_b_2, ffn_w_down_2, rg_w_in_2, rg_conv_w_2, rg_conv_b_2, rg_wa_2, rg_ba_2, rg_wx_2,
    rg_bx_2, rg_lambda_2, rg_w_out_2, gla_w_in_2, gla_w_alpha_2, gla_b_alpha_2, gla_norm_g_2,
    gla_w_out_2,
):
    x = first_block(
        x, c, norm_mix_g, norm_ffn_g, final_norm_g, w_ada, b_ada, w_in, conv_w, conv_b,
        ssd_dt_bias, ssd_a_log, ssd_d, ssd_norm_g, hgrn_lower_bounds, hgrn_norm_g, w_out, w_grp,
        b_grp, w_exp, b_exp, w_gate, w_up, w_down,
    )
    return second_block(
        x, c_2, ada_w_2, ada_b_2, norm_g_2, ffn_w_up_2, ffn_conv_w_2, ffn_conv_b_2,
        ffn_w_down_2, rg_w_in_2, rg_conv_w_2, rg_conv_b_2, rg_wa_2, rg_ba_2, rg_wx_2, rg_bx_2,
        rg_lambda_2, rg_w_out_2, gla_w_in_2, gla_w_alpha_2, gla_b_alpha_2, gla_norm_g_2,
        gla_w_out_2,
    )


_drawn_inputs = setup_inputs


def setup_inputs(seed=0):
    import zlib

    import numpy as np

    out = dict(_drawn_inputs(seed))
    spreads = {}
    factors = {'norm_ffn_g': 2.729,
     'conv_b': 3.522,
     'ssd_norm_g': 4.012,
     'hgrn_lower_bounds': 6.0,
     'hgrn_norm_g': 6.261,
     'b_grp': 5.473,
     'b_exp': 3.978,
     'ffn_conv_b_2': 6.947,
     'rg_conv_b_2': 4.184,
     'rg_ba_2': 51.11,
     'rg_bx_2': 21.554,
     'gla_b_alpha_2': 8.0}
    for name, (base, spread) in spreads.items():
        noise = np.random.default_rng([zlib.crc32(name.encode()), seed]).standard_normal(out[name].shape)
        drawn = base * np.exp(spread * noise) if base else spread * noise
        out[name] = jnp.asarray(drawn.astype(out[name].dtype))
    for name, factor in factors.items():
        out[name] = (out[name] * factor).astype(out[name].dtype)
    return out
```

```python
from contextlib import ExitStack

import numpy as np
import concourse.bass as bass
from concourse import mybir

F32 = mybir.dt.float32
U32 = mybir.dt.uint32
ALU = mybir.AluOpType
ACT = mybir.ActivationFunctionType
AX = mybir.AxisListType

P = 128
D = 1024
T = 256
KT = D // P
DEPTH = 2
EPS = 1e-6

SSD_HEADS, SSD_GROUPS, SSD_CONV = 8, 2, 4
HEAD = 64
HG_HEADS = RET_HEADS = 4
N_GROUPS, PER_GROUP = 4, 8
N_EXPERTS = N_GROUPS * PER_GROUP
FE = D // 4
GATE_FLOOR = 1e-30
LN_SHIFT = 2.0 ** 40

RG_BLOCKS, RG_CONV, RG_C = 4, 4, 8.0
GLA_HEADS, GLA_DK, GLA_DV, GLA_RANK, GLA_TAU = 4, 128, 256, 16, 16.0
D_FF = ((8 * D // 3 + 127) // 128) * 128
FT = D_FF // P
FFN_CONV = 3
TRI = T + P
LEVELS = [1, 2, 4, 8, 16, 32, 64]
BIG = 1e30
GROUP_SLOTS = 128
N_SLOTS = N_GROUPS * GROUP_SLOTS

COLS = {
    "c": 8, "c_2": 8, "final_g": 8, "zero": 1, "one": 1, "eps": 1,
    "norm_mix_g": 8 * DEPTH, "norm_ffn_g": 8 * DEPTH, "b_ada": 48 * DEPTH, "b_ada_2": 48 * DEPTH,
    "norm_g_2": 8 * 4 * DEPTH,
    "conv_w": 6 * SSD_CONV * DEPTH, "conv_b": 6 * DEPTH, "ssd_d": 4 * DEPTH, "ssd_norm_g": 4 * DEPTH,
    "dt_bias": DEPTH, "a_log": DEPTH, "hgrn_lb": 2 * DEPTH, "hgrn_norm_g": 2 * DEPTH,
    "b_route": 36 * DEPTH, "w_route": KT * 36 * DEPTH,
    "ffn_conv_w": 2 * FT * FFN_CONV * DEPTH, "ffn_conv_b": 2 * FT * DEPTH,
    "rg_conv_w": KT * RG_CONV, "rg_conv_b": KT, "rg_ba": KT, "rg_bx": KT, "rg_lambda": KT,
    "gla_b_alpha": 4, "gla_norm_g": 2, "gla_w_z": KT * GLA_RANK, "gla_w_alpha": 512,
    "ident": P, "ones": P, "ones_head": P, "neg_mask": TRI, "level_mask": (len(LEVELS)) * P,
    "cos": T, "sin": T, "ret_decay": RET_HEADS * TRI, "rank4": 4, "rank8": 8,
    "before": P, "slot_no": N_SLOTS, "group_base": 4,
}
OFFSET, _at = {}, 0
for _name, _width in COLS.items():
    OFFSET[_name] = _at
    _at += _width
N_COLS = _at

UNIT = 2048


def weight_chunks():
    out = []
    for l in range(DEPTH):
        out += [("ada", l, i, 4096) for i in range(12)]
        out += [("in", l, i, KT * n) for i, n in enumerate(IN_WIDTHS)]
        out += [("out", l, i, 4096) for i in range(2)]
        for e in range(N_EXPERTS + 1):
            if e < N_EXPERTS:
                out.append(("gate_up", l, e, 4096))
            if e > 0:
                out.append(("down", l, e - 1, 2048))
    for l in range(DEPTH):
        out += [("ada_2", l, i, 4096) for i in range(12)]
        if l == 0:
            out += [("rg_in", 0, i, 4096) for i in (2, 3)] + [("rg_gates", 0, 0, 4096)]
            out += [("rg_in", 0, i, 4096) for i in (0, 1)]
            out += [("rg_out", 0, i, 4096) for i in range(2)]
        else:
            out += [("gla_in", 0, i, 4096) for i in (1, 0, 2, 3, 4, 5)]
            out += [("gla_out", 0, i, 4096) for i in range(2)]
        out += [("ffn_up", l, i, 4096) for i in range(FT // 2)]
        out += [("ffn_down", l, i, FT * P) for i in range(KT)]
    return out


IN_WIDTHS = [512, 264, 512, 512, 512, 512, 512]


class Engine:

    def __init__(self, sem, in_order):
        self.sem, self.in_order = sem, in_order
        self.count, self.steps, self.held = 0, [], []

    def last(self):
        return (self.sem, self.count)

    def do(self, emit, *after):
        waits = [a for a in after if a is not None] + self.held
        self.held = []
        if self.in_order:
            waits.append(self.last())
        self.count += 1
        self.steps.append(([w for w in waits if w[1] > 0], emit))
        return (self.sem, self.count)

    def pad_to(self, count):
        assert count >= self.count, (count, self.count)
        if count > self.count:
            sem, now = self.sem, self.count
            self.steps.append(([(sem, now)], ("pad", count - now)))
            self.count = count

    def play(self, eng):
        self.play_steps(eng, self.steps, [])

    def play_steps(self, eng, steps, passed):
        for waits, emit in steps:
            if isinstance(emit, tuple) and emit[0] == "branch":
                _, flag, when_set, otherwise = emit
                self.wait(eng, waits, passed)
                value = eng.value_load(flag)
                with eng.If(value > 0):
                    self.play_steps(eng, when_set, list(passed))
                with eng.Else():
                    self.play_steps(eng, otherwise, list(passed))
                continue
            self.wait(eng, waits, passed)
            if isinstance(emit, tuple):
                eng.sem_inc(self.sem, emit[1])
                continue
            emit(eng).then_inc(self.sem, 1)

    def wait(self, eng, waits, passed):
        for sem, value in waits:
            known = [i for i, (s, _) in enumerate(passed) if s is sem]
            if known and passed[known[0]][1] >= value:
                continue
            eng.wait_ge(sem, value)
            if known:
                passed[known[0]] = (sem, value)
            else:
                passed.append((sem, value))


def two_stacks_kernel(nc, weights, table, x_in, out):
    with ExitStack() as ctx:
        def sb(name, cols):
            return ctx.enter_context(nc.sbuf_tensor(name, [P, cols], F32))

        def sem(name):
            return ctx.enter_context(nc.semaphore(name))

        RING_UNITS = 10
        ring = sb("weight_ring", RING_UNITS * UNIT)
        tab = sb("parameter_table", N_COLS)
        x = sb("residual", KT * T)[:, :].rearrange("p (k t) -> p k t", t=T)
        h = sb("normed", KT * T)[:, :].rearrange("p (k t) -> p k t", t=T)
        arena = sb("arena", 17408)
        mod = sb("modulation", 48 + 16 + 16)
        rstd = sb("rstd", T)
        rstd_tmp = sb("rstd_tmp", T)
        c_act = sb("c_act", 16)
        lower = sb("lower_bound", 4 * DEPTH + 8)
        overflow = ctx.enter_context(nc.sbuf_tensor("overflow", [P, 1], mybir.dt.int32))
        banks = [ctx.enter_context(nc.psum_tensor(f"bank{i}", [P, 512], F32)) for i in range(8)]

        s_table, s_x, s_out = sem("s_table"), sem("s_x"), sem("s_out")
        s_ring = [sem(f"s_ring{i}") for i in range(RING_UNITS)]
        PE = Engine(sem("s_tensor"), False)
        V = Engine(sem("s_vector"), True)
        S = Engine(sem("s_scalar"), True)
        G = Engine(sem("s_gpsimd"), True)
        TABLE, X_IN = (s_table, 16), (s_x, 16)

        def col(name, i=0, n=1, parts=P):
            o = OFFSET[name] + i
            return tab[0:parts, o:o + n]

        def join():
            ends = [e.last() for e in (PE, V, S, G)]
            for e in (PE, V, S, G):
                e.held = e.held + ends

        class Arena:
            def __init__(self):
                self.at = 0

            def take(self, *shape):
                n = int(np.prod(shape))
                ap = arena[:, self.at:self.at + n]
                self.at += n
                assert self.at <= 17408, self.at
                if len(shape) == 2:
                    return ap.rearrange("p (a b) -> p a b", b=shape[1])
                if len(shape) == 3:
                    return ap.rearrange("p (a b c) -> p a b c", b=shape[1], c=shape[2])
                return ap

        def tt(e, o, a, b, op, *after):
            return e.do(lambda g: g.tensor_tensor(o, a, b, op), *after)

        def ts(e, o, a, s1, s2, op0, op1, *after):
            if s2 is None:
                return e.do(lambda g: g.tensor_scalar(o, a, s1, None, op0), *after)
            return e.do(lambda g: g.tensor_scalar(o, a, s1, s2, op0, op1), *after)

        def stt(o, a, s, b, op0, op1, *after):
            return V.do(lambda g: g.scalar_tensor_tensor(out=o, in0=a, scalar=s, in1=b, op0=op0, op1=op1), *after)

        def recip(o, a, *after):
            return V.do(lambda g: g.reciprocal(o, a), *after)

        def act(o, a, func, *after, scale=1.0, bias=None):
            b = bias if bias is not None else 0.0
            if bias is None and func != ACT.Copy:
                b = col("zero", parts=a.shape[0])
                if a.shape[0] != P:
                    pass
            return S.do(lambda g: g.activation(o, a, func, bias=b, scale=scale), *after)

        def copy(e, o, a, *after):
            if e is S:
                return S.do(lambda g: g.activation(o, a, ACT.Copy, bias=0.0, scale=1.0), *after)
            return e.do(lambda g: g.tensor_copy(o, a), *after)

        order = weight_chunks()
        where, at, owner, reuse = [], 0, [None] * RING_UNITS, []
        offset = 0
        for i, (_, _, _, n) in enumerate(order):
            units = -(-n // UNIT)
            if at % RING_UNITS + units > RING_UNITS:
                at += RING_UNITS - at % RING_UNITS
            u = at % RING_UNITS
            reuse.append([owner[j] for j in range(u, u + units) if owner[j] is not None])
            for j in range(u, u + units):
                owner[j] = i
            where.append((u * UNIT, n, offset))
            offset += n * P
            at += units
        consumed = [None] * len(order)
        taken = [0]

        def consumed_step(chunk, token):
            assert consumed[chunk] in (None, token), (chunk, consumed[chunk], token)
            consumed[chunk] = token
            return token

        def weight(name, l, i):
            k = taken[0]
            assert order[k][:3] == (name, l, i), (order[k], name, l, i)
            taken[0] += 1
            start, n, _ = where[k]
            return ring[:, start:start + n], (s_ring[k % RING_UNITS], 16 * (k // RING_UNITS + 1)), k

        class Banks:
            def __init__(self, ids):
                self.ids, self.n, self.free = ids, 0, {i: None for i in ids}

            def take(self):
                i = self.ids[self.n % len(self.ids)]
                self.n += 1
                return i, banks[i], self.free[i]

        def features(rot, w, landed, chunk, ncols, rhs, nk, evacuate, ready=None):
            wv = w.rearrange("p (k n) -> p k n", k=nk)
            tiles = -(-ncols // P)
            done = None
            for m0 in range(0, tiles, 2):
                i, bank, free = rot.take()
                ms = [m for m in (m0, m0 + 1) if m < tiles]

                def emit(g, ms=ms, bank=bank):
                    for m in ms:
                        width = min(P, ncols - m * P)
                        for k in range(nk):
                            ins = g.matmul(bank[0:width, (m - ms[0]) * T:(m - ms[0] + 1) * T],
                                           wv[:, k, m * P:m * P + width], rhs[:, k, :],
                                           start=(k == 0), stop=(k == nk - 1))
                    return ins
                done = PE.do(emit, landed, free, ready)
                rot.free[i] = evacuate(m0, bank[:, 0:len(ms) * T].rearrange("p (a t) -> p a t", t=T), done)
            consumed[chunk] = done
            return done

        def tokens(rot, w, landed, chunk, rhs, evacuate, ready=None):
            wv = w.rearrange("p (k n) -> p k n", k=KT)
            for b in range(2):
                i, bank, free = rot.take()

                def emit(g, b=b, bank=bank):
                    for k in range(KT):
                        ins = g.matmul(bank[:, :], rhs[:, k, b * P:(b + 1) * P], wv[:, k, :],
                                       start=(k == 0), stop=(k == KT - 1))
                    return ins
                done = PE.do(emit, landed, free, ready)
                rot.free[i] = evacuate(b, bank[:, :], done)
            consumed[chunk] = done

        def inverse_rms(src, tiles, ones, sq, bank, width, *after):
            for k in tiles:
                if k % 2:
                    q = act(sq[:, k, :], src[:, k, :], ACT.Square, *after)
                else:
                    q = tt(V, sq[:, k, :], src[:, k, :], src[:, k, :], ALU.mult, *after)
                done = PE.do(lambda g, k=k: g.matmul(bank[:, 0:T], ones, sq[:, k, :], start=(k == tiles[0]),
                                                     stop=(k == tiles[-1])), q, *after)
            root = act(rstd_tmp[:, :], bank[:, 0:T], ACT.Sqrt, done, V.last(), scale=1.0 / width, bias=col("eps"))
            return recip(rstd[:, :], rstd_tmp[:, :], root)

        ones = col("ones", 0, P)
        ones_head = col("ones_head", 0, P)
        ident = col("ident", 0, P)

        def modulated_norm(gain, shift_at, scale_at):
            join()
            a = Arena()
            sq = a.take(KT, T)
            gain1 = mod[:, 48:56]
            g1 = stt(gain1, mod[:, scale_at:scale_at + 8], col("one"), gain, ALU.add, ALU.mult)
            r = inverse_rms(x, list(range(KT)), ones, sq, banks[0], D)
            for k in range(KT):
                m = stt(h[:, k, :], x[:, k, :], gain1[:, k:k + 1], rstd[:, :], ALU.mult, ALU.mult, r)
                last = act(h[:, k, :], h[:, k, :], ACT.Identity, m, bias=mod[:, shift_at + k:shift_at + k + 1])
            return last

        def modulation(name, l, which, bias):
            join()
            for i in range(12):
                w, landed, chunk = weight(name, l, i)
                wv = w.rearrange("p (k n) -> p k n", k=KT)

                def emit(g, i=i, wv=wv):
                    for m in range(4):
                        for k in range(KT):
                            ins = g.matmul(banks[0][:, i * 4 + m:i * 4 + m + 1], wv[:, k, m * P:(m + 1) * P],
                                           c_act[:, 8 * which + k:8 * which + k + 1],
                                           start=(k == 0), stop=(k == KT - 1))
                    return ins
                consumed[chunk] = PE.do(emit, landed, TABLE)
            tt(V, mod[:, 0:48], banks[0][:, 0:48], bias, ALU.add, PE.last())

        def weighted_values(bank, rows, cols, v, g384, *after):
            def emit(g):
                g.matmul(bank[rows, cols:cols + T], v[0], g384[:, 0:T], start=True, stop=False)
                return g.matmul(bank[rows, cols + P:cols + T], v[1], g384[:, T:TRI], start=False, stop=True)
            return PE.do(emit, *after)

        def leveled_scores(q, k, cum, heads, nt, a, *after):
            scores = a.take(4, TRI)
            expo, both = a.take(nt * T), a.take(nt * T)
            both_v = both.rearrange("p (n t) -> p n t", t=T)
            zero = G.do(lambda g: g.memset(scores[:, :, :], 0.0), *after)
            rot = Banks([4, 5, 6, 7])
            level_mask = tab[:, OFFSET["level_mask"]:OFFSET["level_mask"] + 7 * P].bitcast(U32)

            kinds = [[n for n in range(4) if heads[n][1] == row] for row in sorted({hd[1] for hd in heads})]

            def block(members, lhs, rhs, s0, t0, *wait):
                i, bank, free = rot.take()

                def emit(g):
                    for at_, n in enumerate(members):
                        tile, row, rows = heads[n]
                        ins = g.matmul(bank[:, at_ * P:(at_ + 1) * P], lhs[row:row + rows, tile, s0:s0 + P],
                                       rhs[row:row + rows, tile, t0:t0 + P], start=True, stop=True)
                    return ins
                return i, bank, PE.do(emit, free, *wait)

            def place(members, i, bank, done, mask, cols):
                m0, step, count = members[0], (members[1] - members[0]), len(members)
                dst = scores[:, m0:m0 + step * (count - 1) + 1:step, cols:cols + P]
                data = bank[:, 0:count * P].rearrange("p (n t) -> p n t", t=P)
                if mask is None:
                    rot.free[i] = copy(V, dst, data, done)
                    return
                m = mask.unsqueeze(1).broadcast_to([P, count, P])
                rot.free[i] = V.do(lambda g: g.copy_predicated(dst, m, data), done, zero)

            diagonal = tab[:, OFFSET["ident"]:OFFSET["ident"] + P].bitcast(U32)
            for b in range(2):
                for members in kinds:
                    i, bank, done = block(members, k, q, b * P, b * P, *after)
                    place(members, i, bank, done, diagonal, b * T)
            read = None
            for n, half in enumerate(LEVELS + [P]):
                seg = dict(n=nt * T // (2 * half), t=2 * half)
                cv = cum.rearrange("p n t -> p (n t)").rearrange("p (n t) -> p n t", **seg)
                qv = q.rearrange("p n t -> p (n t)").rearrange("p (n t) -> p n t", **seg)
                kv = k.rearrange("p n t -> p (n t)").rearrange("p (n t) -> p n t", **seg)
                ev = expo.rearrange("p (n t) -> p n t", **seg)
                bv = both.rearrange("p (n t) -> p n t", **seg)
                mid = cv[:, :, half - 1:half].broadcast_to([P, seg["n"], half])
                tt(V, ev[:, :, 0:half], mid, cv[:, :, 0:half], ALU.subtract, S.last(), *after)
                d = tt(V, ev[:, :, half:], cv[:, :, half:], mid, ALU.subtract)
                e = act(expo, expo, ACT.Exp, d)
                tt(V, bv[:, :, 0:half], kv[:, :, 0:half], ev[:, :, 0:half], ALU.mult, e, read)
                w = tt(V, bv[:, :, half:], qv[:, :, half:], ev[:, :, half:], ALU.mult)
                for members in kinds:
                    for b in range(2 if half < P else 1):
                        if half < P:
                            i, bank, read = block(members, both_v, both_v, b * P, b * P, w)
                            place(members, i, bank, read, level_mask[:, n * P:(n + 1) * P], b * T)
                        else:
                            i, bank, read = block(members, both_v, both_v, 0, P, w)
                            place(members, i, bank, read, None, P)
            return scores, V.last()

        def head_norm_gate(src_bank, dst, gain, ones_m, width, gate, sq, o, sum_bank, tiles, *after):
            for n in tiles:
                s = copy(S, o[:, n, :], src_bank[:, n, :], *after)
            for n in tiles:
                tt(V, sq[:, n, :], o[:, n, :], o[:, n, :], ALU.mult, s)
                done = PE.do(lambda g, n=n: g.matmul(sum_bank[:, 0:T], ones_m, sq[:, n, :], start=True, stop=True),
                             V.last(), S.last())
                root = act(rstd_tmp[:, :], sum_bank[:, 0:T], ACT.Sqrt, done, V.last(), scale=1.0 / width,
                           bias=col("eps"))
                r = recip(rstd[:, :], rstd_tmp[:, :], root)
                stt(o[:, n, :], o[:, n, :], gain(n), rstd[:, :], ALU.mult, ALU.mult)
                tt(V, dst(n), o[:, n, :], gate[:, n, :], ALU.mult)

        def token_mixer(l, h_ready):
            join()
            a = Arena()
            conv = a.take(6, T)
            silu_z, sig_hg, silu_rg = a.take(4, T), a.take(2, T), a.take(2, T)
            v_tok, xs_tok = a.take(2, 512), a.take(2, 512)
            hq, hk, cum_f = a.take(2, T), a.take(2, T), a.take(2, T)
            rq, rk = a.take(2, T), a.take(2, T)
            mixed = h
            rot = Banks([0, 1, 2, 3])

            def convolve(base):
                def evacuate(m0, bank, done):
                    for j in range(2):
                        m = base + m0 + j
                        w = lambda tap: col("conv_w", (l * SSD_CONV + tap) * 6 + m)
                        f = act(conv[:, m, :], bank[:, j, :], ACT.Identity, done, V.last(), scale=w(3),
                                bias=col("conv_b", l * 6 + m))
                        for tap in (2, 1, 0):
                            d = 3 - tap
                            f = stt(conv[:, m, d:], bank[:, j, 0:T - d], w(tap), conv[:, m, d:],
                                    ALU.mult, ALU.add, f)
                    act(conv[:, base + m0:base + m0 + 2, :], conv[:, base + m0:base + m0 + 2, :], ACT.Silu, f)
                    return f
                return evacuate

            w, landed, chunk = weight("in", l, 0)
            features(rot, w, landed, chunk, 512, h, KT, convolve(0), h_ready)
            w, landed, chunk = weight("in", l, 1)
            dt_u, dt_e, dt, cum = a.take(T), a.take(T), a.take(T), a.take(T)
            neg_a = lower[0:8, 4 * DEPTH:4 * DEPTH + 1]
            conv_bc = convolve(4)

            def bc_dt(m0, bank, done):
                if m0 == 0:
                    return conv_bc(0, bank, done)
                act(neg_a, col("a_log", l, parts=8), ACT.Exp)
                u = ts(V, dt_u[0:8, :], bank[0:8, 0, :], col("dt_bias", l, parts=8), None, ALU.add, None, done)
                z = stt(dt_e[0:8, :], dt_u[0:8, :], -1.0, dt_u[0:8, :], ALU.mult, ALU.max, S.last())
                act(dt_e[0:8, :], dt_e[0:8, :], ACT.Exp, z, scale=-1.0)
                z = act(dt_e[0:8, :], dt_e[0:8, :], ACT.Ln, bias=col("one", parts=8))
                stt(dt[0:8, :], dt_u[0:8, :], 0.0, dt_e[0:8, :], ALU.max, ALU.add, z)
                ts(V, dt_e[0:8, :], dt[0:8, :], neg_a, -1.0, ALU.mult, ALU.mult)
                V.do(lambda g: g.tensor_tensor_scan(cum[0:8, :], ones_row[0:8, :], dt_e[0:8, :], 0.0,
                                                    ALU.mult, ALU.add))
                return u
            ones_row = a.take(T)
            V.do(lambda g: g.memset(ones_row, 1.0))
            features(rot, w, landed, chunk, 264, h, KT, bc_dt)

            log_f = a.take(2, T)

            def hf_hq(m0, bank, done):
                if m0 == 2:
                    return copy(S, hq[:, :, :], bank, done)
                f = act(hk[:, :, :], bank, ACT.Sigmoid, done)
                for j in range(2):
                    ts(V, hk[:, j, :], hk[:, j, :], lower[:, 4 + 2 * l + j:5 + 2 * l + j],
                       lower[:, 2 * l + j:2 * l + j + 1], ALU.mult, ALU.add, f)
                g_ = ts(V, log_f[:, :, :], hk[:, :, :], GATE_FLOOR, None, ALU.max, None)
                ts(V, hk[:, :, :], hk[:, :, :], -1.0, 1.0, ALU.mult, ALU.add)
                g_ = act(log_f[:, :, :], log_f[:, :, :], ACT.Ln, g_, scale=LN_SHIFT)
                ts(V, log_f[:, :, :], log_f[:, :, :], -float(np.log(LN_SHIFT)), None, ALU.add, None, g_)
                for j in range(2):
                    V.do(lambda g, j=j: g.tensor_tensor_scan(cum_f[:, j, :], ones_row, log_f[:, j, :], 0.0,
                                                             ALU.mult, ALU.add))
                return f
            w, landed, chunk = weight("in", l, 2)
            features(rot, w, landed, chunk, 512, h, KT, hf_hq)
            w, landed, chunk = weight("in", l, 3)
            tokens(rot, w, landed, chunk, h, lambda b, bank, done: copy(S, v_tok[:, b, :], bank, done))
            w, landed, chunk = weight("in", l, 4)
            features(rot, w, landed, chunk, 512, h, KT,
                     lambda m0, bank, done: copy(S, (rq, rk)[m0 // 2][:, :, :], bank, done))
            w, landed, chunk = weight("in", l, 5)
            features(rot, w, landed, chunk, 512, h, KT,
                     lambda m0, bank, done: act(silu_z[:, m0:m0 + 2, :], bank, ACT.Silu, done))
            w, landed, chunk = weight("in", l, 6)
            features(rot, w, landed, chunk, 512, h, KT,
                     lambda m0, bank, done: act((sig_hg, silu_rg)[m0 // 2][:, :, :], bank,
                                                (ACT.Sigmoid, ACT.Silu)[m0 // 2], done))
            join()

            mark = a.at
            score = a.take(2, TRI)
            dec, gmat = a.take(2, TRI), a.take(2, TRI)
            cols8 = a.take(4, 8)
            sq, o = a.take(4, T), a.take(4, T)

            def xs_turn(g):
                for b in range(2):
                    for m in range(4):
                        ins = g.transpose(banks[b][:, m * P:(m + 1) * P], conv[:, m, b * P:(b + 1) * P], ident)
                return ins
            turned = PE.do(xs_turn)
            for b in range(2):
                copy(S, xs_tok[:, b, :], banks[b][:, :], turned)
            def turn_cols(g):
                for n, (src, b) in enumerate(((cum, 0), (cum, 1), (dt, 0), (dt, 1))):
                    ins = g.matmul(banks[2][:, n * 8:(n + 1) * 8], src[0:8, b * P:(b + 1) * P], ident[0:8, 0:8],
                                   start=True, stop=True)
                return ins
            turned = PE.do(turn_cols)
            copy(V, cols8[:, :, :].rearrange("p a b -> p (a b)"), banks[2][:, 0:32], turned)
            for grp in range(2):
                r = slice(64 * grp, 64 * grp + 64)

                def emit(g, r=r, grp=grp):
                    g.matmul(banks[4 + grp][:, 0:T], conv[r, 4, 0:P], conv[r, 5, :], start=True, stop=True)
                    return g.matmul(banks[4 + grp][:, T:TRI], conv[r, 4, P:T], conv[r, 5, P:T],
                                    start=True, stop=True)
                done = PE.do(emit)
                sc = copy(S, score[:, grp, :], banks[4 + grp][:, 0:TRI], done)
            neg_mask = col("neg_mask", 0, TRI)
            bc_free = {6: None, 7: None, 3: None}
            g_free = [None, None]
            for n in range(SSD_HEADS):
                bi, grp, s2 = (6, 7, 3)[n % 3], n // 4, n % 2
                done = PE.do(lambda g, n=n, bi=bi: g.matmul(
                    banks[bi][:, 0:T], ident[0:8, n:n + 1].broadcast_to([8, P]), cum[0:8, :],
                    start=True, stop=True), bc_free[bi])
                stt(dec[:, s2, 0:T], banks[bi][:, 0:T], cols8[:, 0, n:n + 1], neg_mask[:, 0:T],
                    ALU.subtract, ALU.add, done)
                bc_free[bi] = stt(dec[:, s2, T:TRI], banks[bi][:, P:T], cols8[:, 1, n:n + 1], neg_mask[:, T:TRI],
                                  ALU.subtract, ALU.add)
                e = act(dec[:, s2, :], dec[:, s2, :], ACT.Exp, bc_free[bi])
                stt(gmat[:, s2, 0:T], score[:, grp, 0:T], cols8[:, 2, n:n + 1], dec[:, s2, 0:T],
                    ALU.mult, ALU.mult, e, g_free[s2], sc)
                d = stt(gmat[:, s2, T:TRI], score[:, grp, T:TRI], cols8[:, 3, n:n + 1], dec[:, s2, T:TRI],
                        ALU.mult, ALU.mult)
                rows = slice(64 * (n % 2), 64 * (n % 2) + 64)
                g_free[s2] = weighted_values(banks[n // 4], rows, (n // 2 % 2) * T,
                                             [xs_tok[:, b, n * HEAD:(n + 1) * HEAD] for b in range(2)],
                                             gmat[:, s2, :], d, sc)
            done = PE.last()
            for m in range(4):
                stt(o[:, m, :], conv[:, m, :], col("ssd_d", 4 * l + m), banks[m // 2][:, (m % 2) * T:(m % 2 + 1) * T],
                    ALU.mult, ALU.add, done)
                tt(V, o[:, m, :], o[:, m, :], silu_z[:, m, :], ALU.mult)
            for grp in range(2):
                r = inverse_rms(o, [2 * grp, 2 * grp + 1], ones, sq, banks[2], 256, V.last(), S.last())
                for m in (2 * grp, 2 * grp + 1):
                    stt(mixed[:, m, :], o[:, m, :], col("ssd_norm_g", 4 * l + m), rstd[:, :],
                        ALU.mult, ALU.mult, r)
            join()

            a.at = mark
            scores, done = leveled_scores(hq, hk, cum_f, [(n // 2, 64 * (n % 2), 64) for n in range(4)], 2, a)
            for n in range(HG_HEADS):
                rows = slice(64 * (n % 2), 64 * (n % 2) + 64)
                last = weighted_values(banks[0], rows, (n // 2) * T,
                                       [v_tok[:, b, n * HEAD:(n + 1) * HEAD] for b in range(2)],
                                       scores[:, n, :], done)
            sq, o = a.take(2, T), a.take(2, T)
            head_norm_gate(banks[0][:, :].rearrange("p (a t) -> p a t", t=T), lambda n: mixed[:, 4 + n, :],
                           lambda n: col("hgrn_norm_g", 2 * l + n), ones_head, HEAD, sig_hg, sq, o, banks[2],
                           (0, 1), last)
            join()

            a.at = mark
            ra, rb = a.take(2, T), a.take(2, T)
            cos = col("cos", 0, T).unsqueeze(1).broadcast_to([P, 2, T])
            sin = col("sin", 0, T).unsqueeze(1).broadcast_to([P, 2, T])
            for r_ in (rq, rk):
                tt(V, ra[:, :, :], r_[:, :, :], cos, ALU.mult)
                tt(V, rb[:, :, :], r_[:, :, :], sin, ALU.mult)
                tt(V, r_[:, 0, :], ra[:, 0, :], rb[:, 1, :], ALU.subtract)
                ready = tt(V, r_[:, 1, :], rb[:, 0, :], ra[:, 1, :], ALU.add)
            rs = a.take(4, TRI)
            for n in range(RET_HEADS):
                r = slice(32 * n, 32 * n + 32)

                def emit(g, r=r, n=n):
                    for j in range(2):
                        g.matmul(banks[4 + n][:, 0:T], rk[r, j, 0:P], rq[r, j, :], start=(j == 0), stop=(j == 1), tile_position=(32 * n, 0))
                    for j in range(2):
                        ins = g.matmul(banks[4 + n][:, T:TRI], rk[r, j, P:T], rq[r, j, P:T],
                                       start=(j == 0), stop=(j == 1), tile_position=(32 * n, 0))
                    return ins
                done = PE.do(emit, ready)
                d = tt(V, rs[:, n, :], banks[4 + n][:, 0:TRI], col("ret_decay", n * TRI, TRI), ALU.mult, done)
                rows = slice(64 * (n % 2), 64 * (n % 2) + 64)
                last = weighted_values(banks[0], rows, (n // 2) * T,
                                       [v_tok[:, b, 256 + n * HEAD:256 + (n + 1) * HEAD] for b in range(2)],
                                       rs[:, n, :], d)
            sq, o = a.take(2, T), a.take(2, T)
            head_norm_gate(banks[0][:, :].rearrange("p (a t) -> p a t", t=T), lambda n: mixed[:, 6 + n, :],
                           lambda n: col("one"), ones_head, HEAD, silu_rg, sq, o, banks[2], (0, 1), last)
            join()
            rot = Banks([0, 1, 2, 3])
            for c in range(2):
                w, landed, chunk = weight("out", l, c)

                def add(m0, bank, done, c=c):
                    for j in range(2):
                        m = 4 * c + m0 + j
                        r = stt(x[:, m, :], bank[:, j, :], mod[:, 16 + m:17 + m], x[:, m, :],
                                ALU.mult, ALU.add, done)
                    return r
                features(rot, w, landed, chunk, 512, mixed, KT, add)

        def moe(l):
            join()
            a = Arena()
            lg, ex = a.take(2, 36), a.take(2, 36)
            gmx, top, w1 = a.take(2, 1), a.take(2, 4), a.take(2, 4)
            eq4, eq8, ing, tmp8 = a.take(2, 4), a.take(2, 8), a.take(2, 8), a.take(2, 8)
            oh1, cmb, sel = a.take(2, 8), a.take(2, 32), a.take(2, 32)
            X = AX.X

            def route(g):
                for b in range(2):
                    for k in range(KT):
                        ins = g.matmul(banks[0][:, b * 36:(b + 1) * 36], h[:, k, b * P:(b + 1) * P],
                                       col("w_route", (l * KT + k) * 36, 36), start=(k == 0), stop=(k == KT - 1))
                return ins
            done = PE.do(route)
            bias = col("b_route", l * 36, 36).unsqueeze(1).broadcast_to([P, 2, 36])
            tt(V, lg[:, :, :], banks[0][:, 0:72].rearrange("p (b n) -> p b n", b=2), bias, ALU.add, done)

            def reduce(o, i, op):
                return V.do(lambda g: g.tensor_reduce(o, i, X, op))

            def first_max(dst, src, mx, n, eq, rank):
                reduce(mx, src, ALU.max)
                tt(V, eq, src, mx.broadcast_to([P, 2, n]), ALU.is_equal)
                tt(V, eq, eq, rank.unsqueeze(1).broadcast_to([P, 2, n]), ALU.mult)
                reduce(top[:, :, 3:4], eq, ALU.max)
                return tt(V, dst, eq, top[:, :, 3:4].broadcast_to([P, 2, n]), ALU.is_equal)
            first_max(eq4[:, :, :], lg[:, :, 0:4], gmx[:, :, :], 4, eq4[:, :, :], col("rank4", 0, 4))
            d = tt(V, ex[:, :, 0:4], lg[:, :, 0:4], gmx[:, :, :].broadcast_to([P, 2, 4]), ALU.subtract)
            d = act(ex[:, :, 0:4], ex[:, :, 0:4], ACT.Exp, d)
            V.do(lambda g: g.tensor_reduce(w1[:, :, 0:1], ex[:, :, 0:4], X, ALU.add), d)
            recip(w1[:, :, 0:1], w1[:, :, 0:1])
            for g_ in range(N_GROUPS):
                sel_g = eq4[:, :, g_:g_ + 1].broadcast_to([P, 2, 8])
                dst = ing if g_ == 0 else tmp8
                tt(V, dst[:, :, :], lg[:, :, 4 + 8 * g_:12 + 8 * g_], sel_g, ALU.mult)
                if g_:
                    tt(V, ing[:, :, :], ing[:, :, :], tmp8[:, :, :], ALU.add)
            first_max(oh1[:, :, :], ing[:, :, :], top[:, :, 0:1], 8, eq8[:, :, :], col("rank8", 0, 8))
            stt(tmp8[:, :, :], oh1[:, :, :], -BIG, ing[:, :, :], ALU.mult, ALU.add)
            first_max(eq8[:, :, :], tmp8[:, :, :], top[:, :, 1:2], 8, eq8[:, :, :], col("rank8", 0, 8))
            d = tt(V, top[:, :, 2:3], top[:, :, 1:2], top[:, :, 0:1], ALU.subtract)
            d = act(top[:, :, 2:3], top[:, :, 2:3], ACT.Exp, d)
            ts(V, w1[:, :, 1:2], top[:, :, 2:3], 1.0, None, ALU.add, None, d)
            recip(w1[:, :, 1:2], w1[:, :, 1:2])
            tt(V, w1[:, :, 2:3], w1[:, :, 1:2], w1[:, :, 0:1], ALU.mult)
            tt(V, w1[:, :, 3:4], w1[:, :, 2:3], top[:, :, 2:3], ALU.mult)
            tt(V, oh1[:, :, :], oh1[:, :, :], w1[:, :, 2:3].broadcast_to([P, 2, 8]), ALU.mult)
            tt(V, eq8[:, :, :], eq8[:, :, :], w1[:, :, 3:4].broadcast_to([P, 2, 8]), ALU.mult)
            tt(V, oh1[:, :, :], oh1[:, :, :], eq8[:, :, :], ALU.add)
            for g_ in range(N_GROUPS):
                d = tt(V, cmb[:, :, 8 * g_:8 * g_ + 8], oh1[:, :, :],
                       eq4[:, :, g_:g_ + 1].broadcast_to([P, 2, 8]), ALU.mult)

            onehot = eq4[:, :, :]
            rank, slot, count = a.take(2, 4), a.take(2, 1), a.take(4)
            before = col("before", 0, P)

            def ranks(g):
                g.matmul(banks[1][:, 0:4], before, onehot[:, 0, :], start=True, stop=True)
                g.matmul(banks[1][:, 4:8], ones, onehot[:, 0, :], start=True, stop=False)
                g.matmul(banks[1][:, 4:8], before, onehot[:, 1, :], start=False, stop=True)
                g.matmul(banks[1][:, 8:12], ones, onehot[:, 0, :], start=True, stop=False)
                return g.matmul(banks[1][:, 8:12], ones, onehot[:, 1, :], start=False, stop=True)
            done = PE.do(ranks, d)
            V.do(lambda g: g.tensor_reduce(count[:, 0:1], banks[1][:, 8:12], X, ALU.max), done)
            flagged = ts(V, overflow[:, :], count[:, 0:1], float(GROUP_SLOTS), None, ALU.is_gt, None)
            tt(V, rank[:, :, :], banks[1][:, 0:8].rearrange("p (b n) -> p b n", b=2),
               col("group_base", 0, 4).unsqueeze(1).broadcast_to([P, 2, 4]), ALU.add)
            tt(V, rank[:, :, :], rank[:, :, :], onehot, ALU.mult)
            reduce(slot[:, :, :], rank[:, :, :], ALU.add)
            join()
            base = a.at

            def gathered_experts():
                a.at = base
                pick, h_tok = a.take(2, N_SLOTS), a.take(2, D)
                gath = a.take(KT, N_SLOTS)
                pick_t, w_slot = a.take(N_GROUPS, T), a.take(N_GROUPS, PER_GROUP)
                silu, hid, hid_t = a.take(2, FE), a.take(2, FE), a.take(2, 2, P)
                y_slot = a.take(N_GROUPS, D)
                for b in range(2):
                    d = ts(V, pick[:, b, :], col("slot_no", 0, N_SLOTS), slot[:, b, :], None, ALU.is_equal, None)
                rot = Banks([0, 1, 2, 3, 4, 5, 6, 7])
                for b in range(2):
                    for c in range(2):
                        i, bank, free = rot.take()

                        def turn_h(g, b=b, c=c, bank=bank):
                            for k in range(4):
                                ins = g.transpose(bank[:, k * P:(k + 1) * P],
                                                  h[:, 4 * c + k, b * P:(b + 1) * P], ident)
                            return ins
                        done = PE.do(turn_h, free)
                        rot.free[i] = h_ready = copy(S, h_tok[:, b, 512 * c:512 * c + 512], bank[:, :], done)
                for k in range(KT):
                    i, bank, free = rot.take()

                    def gather(g, k=k, bank=bank):
                        g.matmul(bank[:, :], h_tok[:, 0, k * P:(k + 1) * P], pick[:, 0, :], start=True, stop=False)
                        return g.matmul(bank[:, :], h_tok[:, 1, k * P:(k + 1) * P], pick[:, 1, :],
                                        start=False, stop=True)
                    done = PE.do(gather, free, h_ready, d)
                    rot.free[i] = copy((S, V)[k % 2], gath[:, k, :], bank[:, :], done)
                gath_ready = [S.last(), V.last()]
                for j in range(2):
                    i, bank, free = rot.take()

                    def turn_pick(g, j=j, bank=bank):
                        for n in range(2):
                            for b in range(2):
                                ins = g.transpose(bank[:, n * T + b * P:n * T + (b + 1) * P],
                                                  pick[:, b, (2 * j + n) * P:(2 * j + n + 1) * P], ident)
                        return ins
                    done = PE.do(turn_pick, free, d)
                    rot.free[i] = copy(V, pick_t[:, 2 * j:2 * j + 2, :],
                                       bank[:, :].rearrange("p (n t) -> p n t", t=T), done)
                i, bank, free = rot.take()

                def slot_weights(g, bank=bank):
                    for n in range(N_GROUPS):
                        for b in range(2):
                            ins = g.matmul(bank[:, n * 8:(n + 1) * 8], pick[:, b, n * P:(n + 1) * P], oh1[:, b, :],
                                           start=(b == 0), stop=(b == 1))
                    return ins
                done = PE.do(slot_weights, free)
                copy(V, w_slot[:, :, :], bank[:, 0:32].rearrange("p (n e) -> p n e", e=8), done)
                PE.held = PE.held + [S.last(), V.last()]
                PE.pad_to(pe_start + PRELUDE)

                gu_free, turn_free, y_free = [None, None], [None, None], [None, None]
                hid_ready, hid_t_ready, hid_t_free, hid_free = [None] * 2, [None] * 2, [None] * 2, [None] * 2
                for e in range(N_EXPERTS + 1):
                    if e < N_EXPERTS:
                        p, grp = e % 2, e // PER_GROUP
                        w, landed, chunk = weight("gate_up", l, e)
                        wv = w.rearrange("p (k n) -> p k n", k=KT)

                        def gate_up(g, lo, hi, wv=wv, p=p, grp=grp):
                            for k in range(lo, hi):
                                ins = g.matmul(banks[4 + p][:, :], gath[:, k, grp * P:(grp + 1) * P], wv[:, k, :],
                                               start=(k == 0), stop=(k == KT - 1))
                            return ins
                        PE.do(lambda g, f=gate_up: f(g, 0, 4), landed, gu_free[p], *gath_ready)
                    if e > 0:
                        q = (e - 1) % 2

                        def turn_hid(g, q=q):
                            for f in range(2):
                                ins = g.transpose(banks[6 + q][:, f * P:(f + 1) * P], hid[:, q, f * P:(f + 1) * P],
                                                  ident)
                            return ins
                        hid_free[q] = PE.do(turn_hid, hid_ready[q], turn_free[q])
                        turn_free[q] = hid_t_ready[q] = copy(
                            S, hid_t[:, q, :, :], banks[6 + q][:, 0:FE].rearrange("p (f t) -> p f t", t=P),
                            hid_free[q], hid_t_free[q])
                    if e < N_EXPERTS:
                        done = consumed_step(chunk, PE.do(lambda g, f=gate_up: f(g, 4, KT)))
                        s = act(silu[:, p, :], banks[4 + p][:, 0:FE], ACT.Silu, done, hid_ready[p])
                        gu_free[p] = hid_ready[p] = stt(hid[:, p, :], silu[:, p, :],
                                                        w_slot[:, grp, e % PER_GROUP:e % PER_GROUP + 1],
                                                        banks[4 + p][:, FE:2 * FE], ALU.mult, ALU.mult, s, hid_free[p])
                    if e > 0:
                        j = e - 1
                        q, grp, yb = j % 2, j // PER_GROUP, 2 * (j // PER_GROUP % 2)
                        w, landed, chunk = weight("down", l, j)
                        wv = w.rearrange("p (k n) -> p k n", k=2)

                        def down(g, q=q, j=j, yb=yb, wv=wv):
                            for f in range(2):
                                for c in range(2):
                                    ins = g.matmul(banks[yb + c][:, :], hid_t[:, q, f, :],
                                                   wv[:, f, 512 * c:512 * (c + 1)],
                                                   start=(j % PER_GROUP == 0 and f == 0),
                                                   stop=(j % PER_GROUP == PER_GROUP - 1 and f == 1))
                            return ins
                        hid_t_free[q] = consumed_step(chunk, PE.do(down, landed, hid_t_ready[q], y_free[yb // 2]))
                        if j % PER_GROUP == PER_GROUP - 1:
                            for c in range(2):
                                y_free[yb // 2] = copy(V, y_slot[:, grp, 512 * c:512 * (c + 1)], banks[yb + c][:, :],
                                                       hid_t_free[q])
                def scatter(g):
                    for m in range(KT):
                        for n in range(N_GROUPS):
                            ins = g.matmul(banks[m // 2][:, (m % 2) * T:(m % 2 + 1) * T],
                                           y_slot[:, n, m * P:(m + 1) * P], pick_t[:, n, :],
                                           start=(n == 0), stop=(n == N_GROUPS - 1))
                    return ins
                PE.do(scatter, V.last())

            def dense_experts():
                a.at = base
                comb = a.take(N_EXPERTS, T)
                comb_t = a.take(T)
                def turn(g):
                    for b in range(2):
                        ins = g.transpose(banks[1][0:32, b * P:(b + 1) * P], cmb[:, b, :], ident)
                    return ins
                done = PE.do(turn)
                d = copy(V, comb_t[0:32, :], banks[1][0:32, 0:T], done)
                rot = Banks([2, 3])
                for e in range(0, N_EXPERTS, 2):
                    i, bank, free = rot.take()

                    def spread(g, e=e, bank=bank):
                        for j in range(2):
                            ins = g.matmul(bank[:, j * T:(j + 1) * T],
                                           ident[0:32, e + j:e + j + 1].broadcast_to([32, P]), comb_t[0:32, :],
                                           start=True, stop=True)
                        return ins
                    done = PE.do(spread, free, d)
                    rot.free[i] = copy(S, comb[:, e:e + 2, :], bank[:, :].rearrange("p (a t) -> p a t", t=T), done)
                join()
                PE.pad_to(pe_start + PRELUDE)

                silu, hid = a.take(2, 2, T), a.take(2, 2, T)
                hid_free, pair_free = [None, None], [None, None]
                hid_ready = [None, None]
                for e in range(N_EXPERTS + 1):
                    if e < N_EXPERTS:
                        p = e % 2
                        gate, up = banks[4 + 2 * p], banks[5 + 2 * p]
                        w, landed, chunk = weight("gate_up", l, e)
                        wv = w.rearrange("p (k n) -> p k n", k=KT)

                        def half(g, bank, base, wv=wv):
                            for m in range(2):
                                for k in range(KT):
                                    ins = g.matmul(bank[:, m * T:(m + 1) * T], wv[:, k, base + m * P:base + (m + 1) * P],
                                                   h[:, k, :], start=(k == 0), stop=(k == KT - 1))
                            return ins
                        done_g = PE.do(lambda g, gate=gate, half=half: half(g, gate, 0), landed, pair_free[p])
                        s = act(silu[:, p, :, :], gate[:, :].rearrange("p (a t) -> p a t", t=T), ACT.Silu, done_g,
                                hid_ready[p])
                        if e > 0:
                            PE.pad_to(PE.count + 1)
                        done_u = PE.do(lambda g, up=up, half=half: half(g, up, FE))
                        consumed_step(chunk, done_u)
                        upv = up[:, :].rearrange("p (a t) -> p a t", t=T)
                        pair_free[p] = tt(V, silu[:, p, :, :], silu[:, p, :, :], upv, ALU.mult, done_u, s)
                        hid_ready[p] = tt(V, hid[:, p, :, :], silu[:, p, :, :],
                                          comb[:, e, :].unsqueeze(1).broadcast_to([P, 2, T]), ALU.mult, hid_free[p])
                    else:
                        PE.pad_to(PE.count + 1)
                    if e > 0:
                        q = (e - 1) % 2
                        w, landed, chunk = weight("down", l, e - 1)
                        wv = w.rearrange("p (k n) -> p k n", k=2)

                        def down(g, e=e - 1, q=q, wv=wv):
                            for f in range(2):
                                for m in range(KT):
                                    ins = g.matmul(banks[m // 2][:, (m % 2) * T:(m % 2 + 1) * T],
                                                   wv[:, f, m * P:(m + 1) * P], hid[:, q, f, :],
                                                   start=(e == 0 and f == 0 and m % 2 == 0),
                                                   stop=(e == N_EXPERTS - 1 and f == 1), skip_group_check=True)
                            return ins
                        hid_free[q] = consumed_step(chunk, PE.do(down, landed, hid_ready[q]))

            pe_start = PE.count
            PRELUDE = 24
            first_chunk, starts = taken[0], [(e, e.count, e.steps, e.held) for e in (PE, V, S)]
            paths = []
            for path in (gathered_experts, dense_experts):
                taken[0] = first_chunk
                for e, n, _, held in starts:
                    e.count, e.steps, e.held = n, [], list(held)
                path()
                paths.append([(e.count, e.steps) for e, _, _, _ in starts])
            for n, (e, _, before_branch, held) in enumerate(starts):
                top_count = max(paths[0][n][0], paths[1][n][0])
                for count_, steps in (paths[0][n], paths[1][n]):
                    e.count, e.steps = count_, steps
                    e.pad_to(top_count)
                e.steps, e.held = before_branch, []
                e.steps.append(([flagged] + held, ("branch", overflow[0:1, 0:1], paths[1][n][1], paths[0][n][1])))
            join()
            for m in range(KT):
                stt(x[:, m, :], banks[m // 2][:, (m % 2) * T:(m % 2 + 1) * T], mod[:, 40 + m:41 + m], x[:, m, :],
                    ALU.mult, ALU.add, PE.last())

        def gated_residual(y, gain, gate_at, sq):
            col2 = mod[:, 56:64]
            tt(V, col2, mod[:, gate_at:gate_at + 8], gain, ALU.mult)
            r = inverse_rms(y, list(range(KT)), ones, sq, banks[7], D, V.last(), S.last())
            for k in range(KT):
                stt(y[:, k, :], y[:, k, :], col2[:, k:k + 1], rstd[:, :], ALU.mult, ALU.mult, r)
                tt(V, x[:, k, :], x[:, k, :], y[:, k, :], ALU.add)

        def project_out(name, src, y):
            rot = Banks([0, 1, 2, 3])
            for c in range(2):
                w, landed, chunk = weight(name, 0, c)
                features(rot, w, landed, chunk, 512, src, KT,
                         lambda m0, bank, done, c=c: copy(S, y[:, 4 * c + m0:4 * c + m0 + 2, :], bank, done))

        def rglru(l, h_ready):
            join()
            a = Arena()
            xc, gate = a.take(KT, T), a.take(KT, T)
            r_, i_, decay, mult = a.take(KT, T), a.take(KT, T), a.take(KT, T), a.take(KT, T)
            sp = mod[:, 64:80]
            rot = Banks([0, 1, 2, 3])
            lam = col("rg_lambda", 0, KT)
            d = stt(sp[:, 0:8], lam, -1.0, lam, ALU.mult, ALU.max)
            act(sp[:, 0:8], sp[:, 0:8], ACT.Exp, d, scale=-1.0)
            d = act(sp[:, 0:8], sp[:, 0:8], ACT.Ln, bias=col("one"))
            ts(V, sp[:, 8:16], lam, -1.0, 0.0, ALU.mult, ALU.max, d)
            tt(V, sp[:, 8:16], sp[:, 8:16], sp[:, 0:8], ALU.add)
            ts(V, sp[:, 0:8], sp[:, 8:16], -RG_C, None, ALU.mult, None)
            ts(V, sp[:, 8:16], sp[:, 8:16], RG_C, None, ALU.mult, None)

            def convolve(m0, bank, done, c):
                for j in range(2):
                    m = 4 * c + m0 + j
                    w = lambda tap: col("rg_conv_w", tap * KT + m)
                    f = act(xc[:, m, :], bank[:, j, :], ACT.Identity, done, V.last(), scale=w(3),
                            bias=col("rg_conv_b", m))
                    for tap in (2, 1, 0):
                        s = 3 - tap
                        f = stt(xc[:, m, s:], bank[:, j, 0:T - s], w(tap), xc[:, m, s:], ALU.mult, ALU.add, f)
                return f
            for c in range(2):
                w, landed, chunk = weight("rg_in", 0, 2 + c)
                features(rot, w, landed, chunk, 512, h, KT,
                         lambda m0, bank, done, c=c: convolve(m0, bank, done, c), h_ready)
            conv_done = V.last()
            gw, g_landed, g_chunk = weight("rg_gates", 0, 0)
            for c in range(2):
                w, landed, chunk = weight("rg_in", 0, c)
                features(rot, w, landed, chunk, 512, h, KT,
                         lambda m0, bank, done, c=c: act(gate[:, 4 * c + m0:4 * c + m0 + 2, :], bank,
                                                         ACT.Gelu_apprx_tanh, done))
            gv = gw.rearrange("p (w b k n) -> p w b k n", w=2, b=RG_BLOCKS, k=2)
            for which, (dst, bias) in enumerate(((r_, "rg_ba"), (i_, "rg_bx"))):
                for b in range(RG_BLOCKS):
                    i, bank, free = rot.take()

                    def emit(g, which=which, b=b, bank=bank):
                        for m in range(2):
                            for k in range(2):
                                ins = g.matmul(bank[:, m * T:(m + 1) * T], gv[:, which, b, k, m * P:(m + 1) * P],
                                               xc[:, 2 * b + k, :], start=(k == 0), stop=(k == 1))
                        return ins
                    done = PE.do(emit, g_landed, conv_done, free)
                    for m in range(2):
                        rot.free[i] = act(dst[:, 2 * b + m, :], bank[:, m * T:(m + 1) * T], ACT.Sigmoid, done,
                                          bias=col(bias, 2 * b + m))
            consumed[g_chunk] = PE.last()
            for m in range(KT):
                act(decay[:, m, :], r_[:, m, :], ACT.Exp, scale=sp[:, m:m + 1])
                e = act(mult[:, m, :], r_[:, m, :], ACT.Tanh, scale=sp[:, 8 + m:9 + m])
            ts(V, r_[:, :, :], mult[:, :, :], 1.0, None, ALU.add, None, e)
            recip(r_[:, :, :], r_[:, :, :])
            stt(mult[:, :, :], mult[:, :, :], 2.0, r_[:, :, :], ALU.mult, ALU.mult)
            d = ts(V, mult[:, :, :], mult[:, :, :], GATE_FLOOR, None, ALU.max, None)
            e = act(mult[:, :, :], mult[:, :, :], ACT.Sqrt, d)
            tt(V, i_[:, :, :], i_[:, :, :], xc[:, :, :], ALU.mult)
            tt(V, i_[:, :, :], i_[:, :, :], mult[:, :, :], ALU.mult, e)
            for m in range(KT):
                V.do(lambda g, m=m: g.tensor_tensor_scan(r_[:, m, :], decay[:, m, :], i_[:, m, :], 0.0,
                                                         ALU.mult, ALU.add))
            tt(V, xc[:, :, :], gate[:, :, :], r_[:, :, :], ALU.mult)
            join()
            project_out("rg_out", xc, decay)
            return decay, mult

        def gla(l, h_ready):
            join()
            a = Arena()
            q, k, cum = a.take(4, T), a.take(4, T), a.take(4, T)
            v_tok, silu_r = a.take(2, D), a.take(KT, T)
            z = a.take(T)
            lgt = a.take(4, T)
            ones_row = a.take(T)
            rot = Banks([0, 1, 2, 3])
            V.do(lambda g: g.memset(ones_row, 1.0))
            w_z = col("gla_w_z", 0, KT * GLA_RANK).rearrange("p (k n) -> p k n", k=KT)

            def z_product(g):
                for kk in range(KT):
                    ins = g.matmul(banks[4][0:GLA_RANK, 0:T], w_z[:, kk, :], h[:, kk, :],
                                   start=(kk == 0), stop=(kk == KT - 1))
                return ins
            done = PE.do(z_product, h_ready)
            d = copy(V, z[0:GLA_RANK, :], banks[4][0:GLA_RANK, 0:T], done)

            def alpha(g):
                for m in range(4):
                    ins = g.matmul(banks[5 + m // 2][:, (m % 2) * T:(m % 2 + 1) * T],
                                   tab[0:GLA_RANK, OFFSET["gla_w_alpha"] + m * P:OFFSET["gla_w_alpha"] + (m + 1) * P],
                                   z[0:GLA_RANK, :], start=True, stop=True)
                return ins
            done = PE.do(alpha, d)
            for m in range(4):
                d = ts(V, lgt[:, m, :], banks[5 + m // 2][:, (m % 2) * T:(m % 2 + 1) * T],
                       col("gla_b_alpha", m), None, ALU.add, None, done)
            ab = a.take(4, T)
            d = stt(ab[:, :, :], lgt[:, :, :], -1.0, lgt[:, :, :], ALU.mult, ALU.max)
            act(ab[:, :, :], ab[:, :, :], ACT.Exp, d, scale=-1.0)
            d = act(ab[:, :, :], ab[:, :, :], ACT.Ln, bias=col("one"))
            stt(lgt[:, :, :], lgt[:, :, :], 0.0, ab[:, :, :], ALU.min, ALU.subtract, d)
            ts(V, lgt[:, :, :], lgt[:, :, :], 1.0 / GLA_TAU, None, ALU.mult, None)
            for m in range(4):
                V.do(lambda g, m=m: g.tensor_tensor_scan(cum[:, m, :], ones_row, lgt[:, m, :], 0.0,
                                                         ALU.mult, ALU.add))
            w, landed, chunk = weight("gla_in", 0, 1)
            features(rot, w, landed, chunk, 512, h, KT,
                     lambda m0, bank, done: copy(S, k[:, m0:m0 + 2, :], bank, done))
            w, landed, chunk = weight("gla_in", 0, 0)
            features(rot, w, landed, chunk, 512, h, KT,
                     lambda m0, bank, done: S.do(lambda g: g.activation(
                         q[:, m0:m0 + 2, :], bank, ACT.Copy, bias=0.0, scale=GLA_DK ** -0.5), done))
            for c in range(2):
                w, landed, chunk = weight("gla_in", 0, 2 + c)
                tokens(rot, w, landed, chunk, h,
                       lambda b, bank, done, c=c: copy(S, v_tok[:, b, 512 * c:512 * (c + 1)], bank, done))
            for c in range(2):
                w, landed, chunk = weight("gla_in", 0, 4 + c)
                features(rot, w, landed, chunk, 512, h, KT,
                         lambda m0, bank, done, c=c: act(silu_r[:, 4 * c + m0:4 * c + m0 + 2, :], bank,
                                                         ACT.Silu, done))
            join()
            a.at = a.at - 1024 - T - 1024 - T
            scores, done = leveled_scores(q, k, cum, [(n, 0, P) for n in range(4)], 4, a)
            o = h
            for n in range(GLA_HEADS):
                for j in range(2):
                    m = 2 * n + j
                    last = weighted_values(banks[m // 2], slice(0, P), j * T,
                                           [v_tok[:, b, m * P:(m + 1) * P] for b in range(2)],
                                           scores[:, n, :], done)
                copy(S, o[:, 2 * n:2 * n + 2, :], banks[n][:, :].rearrange("p (a t) -> p a t", t=T), last)
            join()
            sq = v_tok.rearrange("p a b -> p (a b)").rearrange("p (a b) -> p a b", b=T)
            for n in range(GLA_HEADS):
                r = inverse_rms(o, [2 * n, 2 * n + 1], ones, sq, banks[4], GLA_DV, V.last(), S.last())
                for j in range(2):
                    m = 2 * n + j
                    stt(o[:, m, :], o[:, m, :], col("gla_norm_g", j), rstd[:, :], ALU.mult, ALU.mult, r)
                    tt(V, o[:, m, :], o[:, m, :], silu_r[:, m, :], ALU.mult)
            join()
            y = arena[:, 0:2048].rearrange("p (a b) -> p a b", b=T)
            project_out("gla_out", o, y)
            return y, sq

        def conv_ffn(l, h_ready):
            join()
            a = Arena()
            y, sq = a.take(KT, T), a.take(KT, T)
            act_t = a.take(FT, T)
            tmp = a.take(2, 4, T)
            rot = Banks([0, 1, 2, 3])
            rot2 = [0, None, None]
            for c in range(FT // 2):
                w, landed, chunk = weight("ffn_up", l, c)
                buf = tmp[:, c % 2, :, :]

                def convolve(m0, bank, done, c=c, buf=buf):
                    for j in range(2):
                        m = (0 if m0 == 0 else FT) + 2 * c + j
                        w = lambda tap: col("ffn_conv_w", (l * FFN_CONV + tap) * 2 * FT + m)
                        d = buf[:, m0 + j, :]
                        f = act(d, bank[:, j, :], ACT.Identity, done, V.last(), scale=w(2),
                                bias=col("ffn_conv_b", l * 2 * FT + m))
                        for tap in (1, 0):
                            s = 2 - tap
                            f = stt(d[:, s:], bank[:, j, 0:T - s], w(tap), d[:, s:], ALU.mult, ALU.add, f)
                    if m0 == 0:
                        act(buf[:, 0:2, :], buf[:, 0:2, :], ACT.Gelu_apprx_tanh, f)
                    else:
                        tt(V, act_t[:, 2 * c:2 * c + 2, :], buf[:, 0:2, :], buf[:, 2:4, :], ALU.mult, S.last())
                    return f
                features(rot, w, landed, chunk, 512, h, KT, convolve, h_ready)
            ready = V.last()
            for m in range(KT):
                w, landed, chunk = weight("ffn_down", l, m)
                features(rot, w, landed, chunk, P, act_t, FT,
                         lambda m0, bank, done, m=m: copy(S, y[:, m:m + 1, :], bank, done), ready)
            return y, sq

        for which, name in ((0, "c"), (1, "c_2")):
            act(c_act[:, 8 * which:8 * which + 8], col(name, 0, 8), ACT.Silu, TABLE)
        lb, tmp4 = col("hgrn_lb", 0, 4), lower[:, 8:16]
        tt(V, tmp4[:, 0:2], lb[:, 0:2], lb[:, 2:4], ALU.max, TABLE)
        tt(V, lower[:, 0:2], lb[:, 0:2], tmp4[:, 0:2], ALU.subtract)
        d = tt(V, lower[:, 2:4], lb[:, 2:4], tmp4[:, 0:2], ALU.subtract)
        d = act(lower[:, 0:4], lower[:, 0:4], ACT.Exp, d)
        tt(V, tmp4[:, 0:2], lower[:, 0:2], lower[:, 2:4], ALU.add, d)
        recip(tmp4[:, 2:4], tmp4[:, 0:2])
        tt(V, lower[:, 0:2], lower[:, 0:2], tmp4[:, 2:4], ALU.mult)
        tt(V, lower[:, 2:4], lower[:, 2:4], tmp4[:, 2:4], ALU.mult)
        tt(V, lower[:, 2:4], lower[:, 0:2], lower[:, 2:4], ALU.add)
        tt(V, lower[:, 2:4], lower[:, 2:4], lower[:, 0:2], ALU.subtract)
        tt(V, lower[:, 0:2], lower[:, 0:2], lower[:, 0:2], ALU.subtract)
        ts(V, lower[:, 4:8], lower[:, 0:4], -1.0, 1.0, ALU.mult, ALU.add)
        for e in (PE, V, S):
            e.held = e.held + [X_IN]

        for l in range(DEPTH):
            modulation("ada", l, 0, col("b_ada", 48 * l, 48))
            ready = modulated_norm(col("norm_mix_g", 8 * l, 8), 0, 8)
            token_mixer(l, ready)
            modulated_norm(col("norm_ffn_g", 8 * l, 8), 24, 32)
            moe(l)
        join()
        sq = Arena().take(KT, T)
        r = inverse_rms(x, list(range(KT)), ones, sq, banks[0], D)
        for k in range(KT):
            stt(x[:, k, :], x[:, k, :], col("final_g", k), rstd[:, :], ALU.mult, ALU.mult, r)

        for l in range(DEPTH):
            modulation("ada_2", l, 1, col("b_ada_2", 48 * l, 48))
            ready = modulated_norm(col("norm_g_2", (4 * l) * 8, 8), 0, 8)
            y, sq = (rglru if l == 0 else gla)(l, ready)
            join()
            gated_residual(y, col("norm_g_2", (4 * l + 1) * 8, 8), 16, sq)
            ready = modulated_norm(col("norm_g_2", (4 * l + 2) * 8, 8), 24, 32)
            y, sq = conv_ffn(l, ready)
            join()
            gated_residual(y, col("norm_g_2", (4 * l + 3) * 8, 8), 40, sq)
        finished = V.last()
        assert taken[0] == len(order)

        block = ctx.enter_context(nc.Block())

        @block.sync
        def _(sp):
            sp.dma_start(tab[:, :], table).then_inc(s_table, 16)
            sp.dma_start(x.rearrange("p k t -> p (k t)"), x_in).then_inc(s_x, 16)
            for k, (start, n, off) in enumerate(where):
                for j in reuse[k]:
                    sp.wait_ge(*consumed[j])
                sp.dma_start(ring[:, start:start + n],
                             weights[off:off + n * P].rearrange("(p n) -> p n", p=P)
                             ).then_inc(s_ring[k % RING_UNITS], 16)
            sp.wait_ge(*finished)
            sp.dma_start(out, x.rearrange("p k t -> p (k t)")).then_inc(s_out, 16)
            sp.wait_ge(s_out, 16)

        @block.tensor
        def _(eng):
            PE.play(eng)

        @block.vector
        def _(eng):
            V.play(eng)

        @block.scalar
        def _(eng):
            S.play(eng)

        @block.gpsimd
        def _(eng):
            G.play(eng)


def kernel(**inputs):
    import concourse.bacc as bacc
    from concourse.bass_utils import run_bass_kernel_spmd as run

    i = {name: np.asarray(a) for name, a in inputs.items()}

    def columns(a):
        return a.reshape(-1, P).T

    def chunk(w):
        return w.reshape(-1, P, w.shape[1]).transpose(1, 0, 2).reshape(P, -1)

    def wide(a):
        return np.pad(a, ((0, P - a.shape[0]), (0, 0)))

    s_, t_ = np.arange(P)[:, None], np.arange(T)[None, :]
    causal = np.concatenate([s_ <= t_, s_ + P <= t_[:, P:]], axis=1)
    lag = np.concatenate([t_ - s_, t_[:, P:] - s_ - P], axis=1)
    gamma = np.log1p(-np.exp2(-5.0 - np.arange(RET_HEADS)))
    decay = np.where(causal, np.exp(gamma[:, None, None] * lag * causal), 0.0) * HEAD ** -0.5
    half = HEAD // 2
    freq = (10000.0 ** (-np.arange(half, dtype=np.float32) / half)).astype(np.float32)
    angle = (np.arange(T, dtype=np.float32)[None, :] * np.tile(freq, 4)[:, None]).astype(np.float64)
    t1 = np.arange(P)[None, :]
    levels = [((s_ // (2 * n) == t1 // (2 * n)) & (s_ % (2 * n) < n) & (t1 % (2 * n) >= n)) for n in LEVELS]
    heads64 = (s_ // HEAD == t1 // HEAD)
    one = np.ones((P, 1))
    route = np.concatenate([i["w_grp"], i["w_exp"]], axis=2)
    b_route = np.concatenate([i["b_grp"], i["b_exp"]], axis=1)
    parts = {
        "c": columns(i["c"]), "c_2": columns(i["c_2"]), "final_g": columns(i["final_norm_g"]),
        "zero": np.zeros((P, 1)), "one": one, "eps": np.full((P, 1), EPS),
        "norm_mix_g": columns(i["norm_mix_g"]), "norm_ffn_g": columns(i["norm_ffn_g"]),
        "b_ada": columns(i["b_ada"]), "b_ada_2": columns(i["ada_b_2"]), "norm_g_2": columns(i["norm_g_2"]),
        "conv_w": columns(i["conv_w"]), "conv_b": columns(i["conv_b"]),
        "ssd_d": np.concatenate([columns(np.repeat(i["ssd_d"][l], HEAD)) for l in range(DEPTH)], axis=1),
        "ssd_norm_g": columns(i["ssd_norm_g"]),
        "dt_bias": wide(i["ssd_dt_bias"].T), "a_log": wide(i["ssd_a_log"].T),
        "hgrn_lb": columns(i["hgrn_lower_bounds"]), "hgrn_norm_g": columns(i["hgrn_norm_g"]),
        "b_route": np.broadcast_to(b_route.reshape(1, -1), (P, 36 * DEPTH)),
        "w_route": np.concatenate([chunk(route[l]) for l in range(DEPTH)], axis=1),
        "ffn_conv_w": columns(i["ffn_conv_w_2"]), "ffn_conv_b": columns(i["ffn_conv_b_2"]),
        "rg_conv_w": columns(i["rg_conv_w_2"]), "rg_conv_b": columns(i["rg_conv_b_2"]),
        "rg_ba": columns(i["rg_ba_2"]), "rg_bx": columns(i["rg_bx_2"]), "rg_lambda": columns(i["rg_lambda_2"]),
        "gla_b_alpha": columns(i["gla_b_alpha_2"]), "gla_norm_g": columns(i["gla_norm_g_2"]),
        "gla_w_z": chunk(i["gla_w_in_2"][0][:, 2 * 512 + 2 * D:]), "gla_w_alpha": wide(i["gla_w_alpha_2"][0]),
        "ident": np.eye(P), "ones": np.ones((P, P)), "ones_head": heads64,
        "neg_mask": np.where(causal, 0.0, -BIG), "level_mask": np.concatenate(levels, axis=1),
        "cos": np.cos(angle), "sin": np.sin(angle),
        "ret_decay": np.concatenate(list(decay), axis=1),
        "rank4": np.broadcast_to(np.arange(4, 0, -1), (P, 4)), "rank8": np.broadcast_to(np.arange(8, 0, -1), (P, 8)),
        "before": s_ < t1, "slot_no": np.broadcast_to(np.arange(N_SLOTS), (P, N_SLOTS)),
        "group_base": np.broadcast_to(GROUP_SLOTS * np.arange(N_GROUPS), (P, N_GROUPS)),
    }
    for name, width in COLS.items():
        assert parts[name].shape == (P, width), (name, parts[name].shape, width)
    table = np.concatenate([np.asarray(parts[name], np.float32) for name in COLS], axis=1)

    off = np.cumsum([0, 512, 768, 8] + [256] * 8)
    z, xbc, dt, hq, hf, hi, hg, rq, rk, rv, rg = [np.arange(off[n], off[n + 1]) for n in range(11)]

    def by_halves(cols):
        return cols.reshape(RET_HEADS, 2, half).transpose(1, 0, 2).reshape(-1)
    in_cols = [xbc[:512], np.concatenate([xbc[512:], dt]), np.concatenate([hf, hq]), np.concatenate([hi, rv]),
               np.concatenate([by_halves(rq), by_halves(rk)]), z, np.concatenate([hg, rg])]

    def piece(name, l, n):
        span = slice(512 * n, 512 * n + 512)
        if name == "ada":
            return chunk(i["w_ada"][l][:, span])
        if name == "ada_2":
            return chunk(i["ada_w_2"][l][:, span])
        if name == "in":
            return chunk(i["w_in"][l][:, in_cols[n]])
        if name == "out":
            return chunk(i["w_out"][l][:, span])
        if name == "gate_up":
            return chunk(np.concatenate([i["w_gate"][l, n], i["w_up"][l, n]], axis=1))
        if name == "down":
            return chunk(i["w_down"][l, n])
        if name == "rg_in":
            return chunk(i["rg_w_in_2"][0][:, span])
        if name == "rg_gates":
            return np.concatenate([chunk(w[0, b]) for w in (i["rg_wa_2"], i["rg_wx_2"]) for b in range(RG_BLOCKS)],
                                  axis=1)
        if name == "rg_out":
            return chunk(i["rg_w_out_2"][0][:, span])
        if name == "gla_in":
            return chunk(i["gla_w_in_2"][0][:, span])
        if name == "gla_out":
            return chunk(i["gla_w_out_2"][0][:, span])
        if name == "ffn_up":
            w = i["ffn_w_up_2"][l]
            return chunk(np.concatenate([w[:, 256 * n:256 * n + 256], w[:, D_FF + 256 * n:D_FF + 256 * n + 256]],
                                        axis=1))
        return chunk(i["ffn_w_down_2"][l][:, P * n:P * n + P])

    stream = []
    for name, l, n, width in weight_chunks():
        p = piece(name, l, n)
        assert p.shape == (P, width), (name, p.shape, width)
        stream.append(p.reshape(-1))
    stream = np.concatenate(stream)
    x_t = np.ascontiguousarray(chunk(i["x"].reshape(T, D).T))

    nc = bacc.Bacc("TRN2", target_bir_lowering=False, num_devices=1)
    w_ap = nc.dram_tensor("weights", stream.shape, F32, kind="ExternalInput").ap()
    t_ap = nc.dram_tensor("table", table.shape, F32, kind="ExternalInput").ap()
    x_ap = nc.dram_tensor("x_t", x_t.shape, F32, kind="ExternalInput").ap()
    o_ap = nc.dram_tensor("y_t", (P, KT * T), F32, kind="ExternalOutput").ap()
    two_stacks_kernel(nc, w_ap, t_ap, x_ap, o_ap)
    got = run(nc, [{"weights": stream, "table": table, "x_t": x_t}], core_ids=[0])
    y = got.results[0]["y_t"].reshape(P, KT, T)
    return np.ascontiguousarray(y.transpose(2, 1, 0)).reshape(1, T, D)
```

```python
from contextlib import ExitStack

import numpy as np
import concourse.bass as bass
from concourse import mybir

F32 = mybir.dt.float32
U32 = mybir.dt.uint32
ALU = mybir.AluOpType
ACT = mybir.ActivationFunctionType
AX = mybir.AxisListType

P = 128
D = 1024
T = 256
KT = D // P
DEPTH = 2
EPS = 1e-6

SSD_HEADS, SSD_GROUPS, SSD_CONV = 8, 2, 4
HEAD = 64
HG_HEADS = RET_HEADS = 4
N_GROUPS, PER_GROUP = 4, 8
N_EXPERTS = N_GROUPS * PER_GROUP
FE = D // 4
GATE_FLOOR = 1e-30
LN_SHIFT = 2.0 ** 40

RG_BLOCKS, RG_CONV, RG_C = 4, 4, 8.0
GLA_HEADS, GLA_DK, GLA_DV, GLA_RANK, GLA_TAU = 4, 128, 256, 16, 16.0
D_FF = ((8 * D // 3 + 127) // 128) * 128
FT = D_FF // P
FFN_CONV = 3
TRI = T + P
LEVELS = [1, 2, 4, 8, 16, 32, 64]
BIG = 1e30
GROUP_SLOTS = 128
N_SLOTS = N_GROUPS * GROUP_SLOTS

COLS = {
    "c": 8, "c_2": 8, "final_g": 8, "zero": 1, "one": 1, "eps": 1,
    "norm_mix_g": 8 * DEPTH, "norm_ffn_g": 8 * DEPTH, "b_ada": 48 * DEPTH, "b_ada_2": 48 * DEPTH,
    "norm_g_2": 8 * 4 * DEPTH,
    "conv_w": 6 * SSD_CONV * DEPTH, "conv_b": 6 * DEPTH, "ssd_d": 4 * DEPTH, "ssd_norm_g": 4 * DEPTH,
    "dt_bias": DEPTH, "a_log": DEPTH, "hgrn_lb": 2 * DEPTH, "hgrn_norm_g": 2 * DEPTH,
    "b_route": 36 * DEPTH, "w_route": KT * 36 * DEPTH,
    "ffn_conv_w": 2 * FT * FFN_CONV * DEPTH, "ffn_conv_b": 2 * FT * DEPTH,
    "rg_conv_w": KT * RG_CONV, "rg_conv_b": KT, "rg_ba": KT, "rg_bx": KT, "rg_lambda": KT,
    "gla_b_alpha": 4, "gla_norm_g": 2, "gla_w_z": KT * GLA_RANK, "gla_w_alpha": 512,
    "ident": P, "ones": P, "ones_head": P, "neg_mask": TRI, "level_mask": (len(LEVELS)) * P,
    "cos": T, "sin": T, "ret_decay": RET_HEADS * TRI, "rank4": 4, "rank8": 8,
    "before": P, "slot_no": N_SLOTS, "group_base": 4,
}
OFFSET, _at = {}, 0
for _name, _width in COLS.items():
    OFFSET[_name] = _at
    _at += _width
N_COLS = _at

UNIT = 2048


IN_WIDTHS = [512, 264, 512, 512, 512, 512, 512]


def chunk_sizes():
    out = {}
    for l in range(DEPTH):
        for name in ("ada", "ada_2"):
            out.update({(name, l, i): 4096 for i in range(12)})
        out.update({("in", l, i): KT * n for i, n in enumerate(IN_WIDTHS)})
        out.update({("out", l, i): 4096 for i in range(2)})
        out.update({("gate_up", l, e): 4096 for e in range(N_EXPERTS)})
        out.update({("down", l, e): 2048 for e in range(N_EXPERTS)})
        out.update({("ffn_up", l, i): 4096 for i in range(FT // 2)})
        out.update({("ffn_down", l, i): FT * P for i in range(KT)})
    out.update({("rg_in", 0, i): 4096 for i in range(4)})
    out.update({("rg_gates", 0, 0): 4096})
    out.update({("rg_out", 0, i): 4096 for i in range(2)})
    out.update({("gla_in", 0, i): 4096 for i in range(6)})
    out.update({("gla_out", 0, i): 4096 for i in range(2)})
    return out


class Engine:

    def __init__(self, sem, in_order):
        self.sem, self.in_order = sem, in_order
        self.count, self.steps, self.held = 0, [], []

    def last(self):
        return (self.sem, self.count)

    def do(self, emit, *after):
        waits = [a for a in after if a is not None] + self.held
        self.held = []
        if self.in_order:
            waits.append(self.last())
        self.count += 1
        self.steps.append(([w for w in waits if w[1] > 0], emit))
        return (self.sem, self.count)

    def pad_to(self, count):
        assert count >= self.count, (count, self.count)
        if count > self.count:
            sem, now = self.sem, self.count
            self.steps.append(([(sem, now)], ("pad", count - now)))
            self.count = count

    def play(self, eng):
        self.play_steps(eng, self.steps, [])

    def play_steps(self, eng, steps, passed):
        for waits, emit in steps:
            if isinstance(emit, tuple) and emit[0] == "branch":
                _, flag, when_set, otherwise = emit
                self.wait(eng, waits, passed)
                value = eng.value_load(flag)
                with eng.If(value > 0):
                    self.play_steps(eng, when_set, list(passed))
                with eng.Else():
                    self.play_steps(eng, otherwise, list(passed))
                continue
            self.wait(eng, waits, passed)
            if isinstance(emit, tuple):
                eng.sem_inc(self.sem, emit[1])
                continue
            emit(eng).then_inc(self.sem, 1)

    def wait(self, eng, waits, passed):
        for sem, value in waits:
            known = [i for i, (s, _) in enumerate(passed) if s is sem]
            if known and passed[known[0]][1] >= value:
                continue
            eng.wait_ge(sem, value)
            if known:
                passed[known[0]] = (sem, value)
            else:
                passed.append((sem, value))


def two_stacks_kernel(nc, weights, table, x_in, out):
    with ExitStack() as ctx:
        def sb(name, cols):
            return ctx.enter_context(nc.sbuf_tensor(name, [P, cols], F32))

        def sem(name):
            return ctx.enter_context(nc.semaphore(name))

        RING_UNITS = 10
        ring = sb("weight_ring", RING_UNITS * UNIT)
        tab = sb("parameter_table", N_COLS)
        x = sb("residual", KT * T)[:, :].rearrange("p (k t) -> p k t", t=T)
        h = sb("normed", KT * T)[:, :].rearrange("p (k t) -> p k t", t=T)
        arena = sb("arena", 17408)
        mods = sb("modulations", 4 * 48)
        ada_acc = sb("ada_acc", 2 * 512)
        small = sb("gains", 8 + 8 + 16)
        rstd = sb("rstd", T)
        rstd_tmp = sb("rstd_tmp", T)
        c_act = sb("c_act", 16)
        lower = sb("lower_bound", 4 * DEPTH + 8)
        overflow = ctx.enter_context(nc.sbuf_tensor("overflow", [P, 1], mybir.dt.int32))
        banks = [ctx.enter_context(nc.psum_tensor(f"bank{i}", [P, 512], F32)) for i in range(8)]

        s_table, s_x, s_out = sem("s_table"), sem("s_x"), sem("s_out")
        s_ring = [sem(f"s_ring{i}") for i in range(RING_UNITS)]
        ADA_BANK = 2
        PE = Engine(sem("s_tensor"), False)
        V = Engine(sem("s_vector"), True)
        S = Engine(sem("s_scalar"), True)
        G = Engine(sem("s_gpsimd"), True)
        TABLE, X_IN = (s_table, 16), (s_x, 16)

        def col(name, i=0, n=1, parts=P):
            o = OFFSET[name] + i
            return tab[0:parts, o:o + n]

        def join():
            ends = [e.last() for e in (PE, V, S, G)]
            for e in (PE, V, S, G):
                e.held = e.held + ends

        class Arena:
            def __init__(self):
                self.at = 0

            def take(self, *shape):
                n = int(np.prod(shape))
                ap = arena[:, self.at:self.at + n]
                self.at += n
                assert self.at <= 17408, self.at
                if len(shape) == 2:
                    return ap.rearrange("p (a b) -> p a b", b=shape[1])
                if len(shape) == 3:
                    return ap.rearrange("p (a b c) -> p a b c", b=shape[1], c=shape[2])
                return ap

        def tt(e, o, a, b, op, *after):
            return e.do(lambda g: g.tensor_tensor(o, a, b, op), *after)

        def ts(e, o, a, s1, s2, op0, op1, *after):
            if s2 is None:
                return e.do(lambda g: g.tensor_scalar(o, a, s1, None, op0), *after)
            return e.do(lambda g: g.tensor_scalar(o, a, s1, s2, op0, op1), *after)

        def stt(o, a, s, b, op0, op1, *after):
            return V.do(lambda g: g.scalar_tensor_tensor(out=o, in0=a, scalar=s, in1=b, op0=op0, op1=op1), *after)

        def recip(o, a, *after):
            return V.do(lambda g: g.reciprocal(o, a), *after)

        def act(o, a, func, *after, scale=1.0, bias=None):
            b = bias if bias is not None else 0.0
            if bias is None and func != ACT.Copy:
                b = col("zero", parts=a.shape[0])
                if a.shape[0] != P:
                    pass
            return S.do(lambda g: g.activation(o, a, func, bias=b, scale=scale), *after)

        def copy(e, o, a, *after):
            if e is S:
                return S.do(lambda g: g.activation(o, a, ACT.Copy, bias=0.0, scale=1.0), *after)
            return e.do(lambda g: g.tensor_copy(o, a), *after)

        sizes = chunk_sizes()
        order, where, owner, reuse = [], [], [None] * RING_UNITS, []
        ring_at = [0, 0]

        def place_chunk(key):
            n = sizes[key]
            units = -(-n // UNIT)
            if ring_at[0] % RING_UNITS + units > RING_UNITS:
                ring_at[0] += RING_UNITS - ring_at[0] % RING_UNITS
            u = ring_at[0] % RING_UNITS
            reuse.append([owner[j] for j in range(u, u + units) if owner[j] is not None])
            for j in range(u, u + units):
                owner[j] = len(order)
            order.append(key)
            where.append((u * UNIT, n, ring_at[1]))
            ring_at[0] += units
            ring_at[1] += n * P
        consumed = [None] * len(sizes)
        taken = [0]

        def consumed_step(chunk, token):
            assert consumed[chunk] in (None, token), (chunk, consumed[chunk], token)
            consumed[chunk] = token
            return token

        def weight(name, l, i):
            k = taken[0]
            if k == len(order):
                place_chunk((name, l, i))
            assert order[k] == (name, l, i), (order[k], name, l, i)
            taken[0] += 1
            start, n, _ = where[k]
            return ring[:, start:start + n], (s_ring[k % RING_UNITS], 16 * (k // RING_UNITS + 1)), k

        class Banks:
            def __init__(self, ids):
                self.ids, self.n, self.free = ids, 0, {i: None for i in ids}

            def take(self):
                i = self.ids[self.n % len(self.ids)]
                self.n += 1
                return i, banks[i], self.free[i]

        def run(steps):
            for _ in steps:
                pass

        def features(*args, **kw):
            run(feature_steps(*args, **kw))

        def tokens(*args, **kw):
            run(token_steps(*args, **kw))

        def chunk_features(name, l, i, *args, **kw):
            yield from feature_steps(*(args[0:1] + weight(name, l, i) + args[1:]), **kw)

        def chunk_tokens(name, l, i, *args, **kw):
            yield from token_steps(*(args[0:1] + weight(name, l, i) + args[1:]), **kw)

        def feature_steps(rot, w, landed, chunk, ncols, rhs, nk, evacuate, ready=None):
            wv = w.rearrange("p (k n) -> p k n", k=nk)
            tiles = -(-ncols // P)
            done = None
            for m0 in range(0, tiles, 2):
                i, bank, free = rot.take()
                ms = [m for m in (m0, m0 + 1) if m < tiles]

                def emit(g, ms=ms, bank=bank):
                    for m in ms:
                        width = min(P, ncols - m * P)
                        for k in range(nk):
                            ins = g.matmul(bank[0:width, (m - ms[0]) * T:(m - ms[0] + 1) * T],
                                           wv[:, k, m * P:m * P + width], rhs[:, k, :],
                                           start=(k == 0), stop=(k == nk - 1))
                    return ins
                done = PE.do(emit, landed, free, ready)
                if m0 + 2 >= tiles:
                    consumed_step(chunk, done)
                rot.free[i] = evacuate(m0, bank[:, 0:len(ms) * T].rearrange("p (a t) -> p a t", t=T), done)
                yield

        def token_steps(rot, w, landed, chunk, rhs, evacuate, ready=None):
            wv = w.rearrange("p (k n) -> p k n", k=KT)
            for b in range(2):
                i, bank, free = rot.take()

                def emit(g, b=b, bank=bank):
                    for k in range(KT):
                        ins = g.matmul(bank[:, :], rhs[:, k, b * P:(b + 1) * P], wv[:, k, :],
                                       start=(k == 0), stop=(k == KT - 1))
                    return ins
                done = PE.do(emit, landed, free, ready)
                if b == 1:
                    consumed_step(chunk, done)
                rot.free[i] = evacuate(b, bank[:, :], done)
                yield

        def inverse_rms(src, tiles, ones, sq, bank, width, *after):
            for k in tiles:
                if k % 2:
                    q = act(sq[:, k, :], src[:, k, :], ACT.Square, *after)
                else:
                    q = tt(V, sq[:, k, :], src[:, k, :], src[:, k, :], ALU.mult, *after)
                done = PE.do(lambda g, k=k: g.matmul(bank[:, 0:T], ones, sq[:, k, :], start=(k == tiles[0]),
                                                     stop=(k == tiles[-1])), q, *after)
            root = act(rstd_tmp[:, :], bank[:, 0:T], ACT.Sqrt, done, V.last(), scale=1.0 / width, bias=col("eps"))
            return recip(rstd[:, :], rstd_tmp[:, :], root)

        ones = col("ones", 0, P)
        ones_head = col("ones_head", 0, P)
        ident = col("ident", 0, P)

        def modulated_norm(mod, gain, shift_at, scale_at):
            join()
            a = Arena()
            sq = a.take(KT, T)
            gain1 = small[:, 0:8]
            g1 = stt(gain1, mod[:, scale_at:scale_at + 8], col("one"), gain, ALU.add, ALU.mult)
            r = inverse_rms(x, list(range(KT)), ones, sq, banks[0], D)
            for k in range(KT):
                m = stt(h[:, k, :], x[:, k, :], gain1[:, k:k + 1], rstd[:, :], ALU.mult, ALU.mult, r)
                last = act(h[:, k, :], h[:, k, :], ACT.Identity, m, bias=mod[:, shift_at + k:shift_at + k + 1])
            return last

        class Modulations:
            def __init__(self, chunks):
                self.chunks, self.bank = chunks, None
                self.begun = 0
                self.scaled = self.summed = None
                self.acc_free, self.bank_free = [None, None], None

            def step(self):
                if self.begun == len(self.chunks):
                    return
                name, l, i, c_at, bias = self.chunks[self.begun]
                self.add_bias()
                w, landed, chunk = weight(name, l, i)
                wv = w.rearrange("p (k n) -> p k n", k=KT)
                p = self.begun % 2
                acc = ada_acc[:, 512 * p:512 * p + 512]
                for k in range(KT):
                    c_k = c_act[:, c_at + k:c_at + k + 1]
                    if k == 0:
                        done = ts(V, acc, wv[:, k, :], c_k, None, ALU.mult, None, landed, self.acc_free[p])
                    else:
                        done = stt(acc, wv[:, k, :], c_k, acc, ALU.mult, ALU.add)
                consumed_step(chunk, done)
                self.sum_rows()
                self.scaled = (acc, p, 4 * self.begun, bias, done)
                self.begun += 1

            def sum_rows(self):
                if self.scaled is not None:
                    acc, p, dst, bias, done = self.scaled
                    bank = self.bank

                    def emit(g):
                        for m in range(4):
                            ins = g.matmul(bank[:, m:m + 1], acc[:, m * P:(m + 1) * P], col("one"),
                                           start=True, stop=True)
                        return ins
                    self.acc_free[p] = PE.do(emit, done, self.bank_free)
                    self.summed = (bank, dst, bias, self.acc_free[p])
                    self.scaled = None

            def add_bias(self):
                if self.summed is not None:
                    bank, dst, bias, done = self.summed
                    self.bank_free = tt(V, mods[:, dst:dst + 4], bank[:, 0:4], bias, ALU.add, done)
                    self.summed = None

            def through(self, layer, chunks):
                while self.begun < 12 * layer + chunks:
                    self.step()
                self.settle()

            def settle(self):
                self.add_bias()
                self.sum_rows()
                self.add_bias()

            def state(self):
                return (self.begun, self.scaled, self.summed, list(self.acc_free), self.bank_free)

            def restore(self, state):
                self.begun, self.scaled, self.summed, acc_free, self.bank_free = state
                self.acc_free = list(acc_free)

        class Background:

            def __init__(self, *steps):
                self.steps = list(steps)

            def step(self, n=1):
                while n and self.steps:
                    try:
                        next(self.steps[0])
                        n -= 1
                    except StopIteration:
                        self.steps.pop(0)

            def finish(self):
                while self.steps:
                    self.step()

        def weighted_values(bank, rows, cols, v, g384, *after):
            def emit(g):
                g.matmul(bank[rows, cols:cols + T], v[0], g384[:, 0:T], start=True, stop=False)
                return g.matmul(bank[rows, cols + P:cols + T], v[1], g384[:, T:TRI], start=False, stop=True)
            return PE.do(emit, *after)

        def leveled_scores(q, k, cum, heads, nt, a, rot, beside, *after):
            scores = a.take(4, TRI)
            expo2, both2 = a.take(2, nt * T), a.take(2, nt * T)
            zero = G.do(lambda g: g.memset(scores[:, :, :], 0.0), V.last(), S.last(), PE.last(), *after)
            level_mask = tab[:, OFFSET["level_mask"]:OFFSET["level_mask"] + 7 * P].bitcast(U32)
            diagonal = tab[:, OFFSET["ident"]:OFFSET["ident"] + P].bitcast(U32)
            kinds = [[n for n in range(4) if heads[n][1] == row] for row in sorted({hd[1] for hd in heads})]
            if len(kinds) == 2:
                groups = [(members, (0, 1)) for members in kinds]
            else:
                groups = [(kinds[0], (0,)), (kinds[0], (1,))]

            def products(lhs, rhs, off_diagonal, *wait):
                out = []
                for members, blocks in groups:
                    if off_diagonal:
                        blocks = blocks[:1]
                        if blocks[0] == 1:
                            continue
                    i, bank, free = rot.take()

                    def emit(g, members=members, blocks=blocks, bank=bank):
                        at_ = 0
                        for b in blocks:
                            t0 = P if off_diagonal else b * P
                            for n in members:
                                tile, row, rows = heads[n]
                                ins = g.matmul(bank[:, at_:at_ + P], lhs[row:row + rows, tile, b * P:b * P + P],
                                               rhs[row:row + rows, tile, t0:t0 + P], start=True, stop=True)
                                at_ += P
                        return ins
                    done = PE.do(emit, free, *wait)
                    for at_, b in enumerate(blocks):
                        width = len(members) * P
                        out.append((members, b, i, bank[:, at_ * width:(at_ + 1) * width], done))
                return out

            def place(blocks, mask):
                for members, b, i, data, done in blocks:
                    m0, step, count = members[0], (members[1] - members[0]), len(members)
                    cols = P if mask is None else b * T
                    dst = scores[:, m0:m0 + step * (count - 1) + 1:step, cols:cols + P]
                    data = data.rearrange("p (n t) -> p n t", t=P)
                    if mask is None:
                        rot.free[i] = copy(V, dst, data, done)
                    else:
                        m = mask.unsqueeze(1).broadcast_to([P, count, P])
                        rot.free[i] = V.do(lambda g, dst=dst, m=m, data=data: g.copy_predicated(dst, m, data),
                                           done, zero)

            halves = LEVELS + [P]

            def views(n):
                seg = dict(n=nt * T // (2 * halves[n]), t=2 * halves[n])
                flat = [v.rearrange("p n t -> p (n t)").rearrange("p (n t) -> p n t", **seg) for v in (cum, q, k)]
                return flat + [expo2[:, n % 2, :].rearrange("p (n t) -> p n t", **seg),
                               both2[:, n % 2, :].rearrange("p (n t) -> p n t", **seg)]

            def exponents(n):
                half = halves[n]
                cv, _, _, ev, _ = views(n)
                mid = cv[:, :, half - 1:half].broadcast_to([P, nt * T // (2 * half), half])
                tt(V, ev[:, :, 0:half], mid, cv[:, :, 0:half], ALU.subtract, *after)
                d = tt(V, ev[:, :, half:], cv[:, :, half:], mid, ALU.subtract)
                return act(expo2[:, n % 2, :], expo2[:, n % 2, :], ACT.Exp, d)

            def factors(n, e, read):
                half = halves[n]
                _, qv, kv, ev, bv = views(n)
                tt(V, bv[:, :, 0:half], kv[:, :, 0:half], ev[:, :, 0:half], ALU.mult, e, read)
                return tt(V, bv[:, :, half:], qv[:, :, half:], ev[:, :, half:], ALU.mult)

            e = exponents(0)
            waiting, mask = products(k, q, False, *after), diagonal
            read = [None, None]
            for n in range(len(halves)):
                e_next = exponents(n + 1) if n + 1 < len(halves) else None
                w = factors(n, e, read[n % 2])
                place(waiting, mask)
                both_v = both2[:, n % 2, :].rearrange("p (n t) -> p n t", t=T)
                waiting = products(both_v, both_v, halves[n] == P, w)
                mask = level_mask[:, n * P:(n + 1) * P] if halves[n] < P else None
                read[n % 2] = PE.last()
                e = e_next
                beside()
            place(waiting, mask)
            return scores, V.last()

        def head_norm_gate(src_bank, dst, gain, ones_m, width, gate, sq, o, sum_bank, tiles, *after):
            for n in tiles:
                s = copy(S, o[:, n, :], src_bank[:, n, :], *after)
            for n in tiles:
                tt(V, sq[:, n, :], o[:, n, :], o[:, n, :], ALU.mult, s)
                done = PE.do(lambda g, n=n: g.matmul(sum_bank[:, 0:T], ones_m, sq[:, n, :], start=True, stop=True),
                             V.last(), S.last())
                root = act(rstd_tmp[:, :], sum_bank[:, 0:T], ACT.Sqrt, done, V.last(), scale=1.0 / width,
                           bias=col("eps"))
                r = recip(rstd[:, :], rstd_tmp[:, :], root)
                stt(o[:, n, :], o[:, n, :], gain(n), rstd[:, :], ALU.mult, ALU.mult)
                tt(V, dst(n), o[:, n, :], gate[:, n, :], ALU.mult)

        ada = Modulations([(name, l, i, 8 * which, col(("b_ada", "b_ada_2")[which], 48 * l + 4 * i, 4))
                           for name, l, which in (("ada", 0, 0), ("ada", 1, 0), ("ada_2", 0, 1), ("ada_2", 1, 1))
                           for i in range(12)])
        ada.bank = banks[2]

        def ada_until(layer):
            if ada.begun < 12 * layer:
                ada.step()

        def token_mixer(l, mod, h_ready):
            join()
            a = Arena()
            mixed = a.take(KT, T)
            conv = a.take(6, T)
            silu_z, sig_hg, silu_rg = a.take(4, T), a.take(2, T), a.take(2, T)
            v_tok, xs_tok = a.take(2, 512), a.take(2, 512)
            hq, hk, cum_f = a.take(2, T), a.take(2, T), a.take(2, T)
            rq, rk = a.take(2, T), a.take(2, T)
            dt_u, dt_e, dt, cum = a.take(T), a.take(T), a.take(T), a.take(T)
            log_f, ones_row = a.take(2, T), a.take(T)
            V.do(lambda g: g.memset(ones_row, 1.0))
            rot, pair = Banks([0, 1]), Banks([6, 7])

            def convolve(base):
                def evacuate(m0, bank, done):
                    for j in range(2):
                        m = base + m0 + j
                        w = lambda tap: col("conv_w", (l * SSD_CONV + tap) * 6 + m)
                        f = act(conv[:, m, :], bank[:, j, :], ACT.Identity, done, V.last(), scale=w(3),
                                bias=col("conv_b", l * 6 + m))
                        for tap in (2, 1, 0):
                            d = 3 - tap
                            f = stt(conv[:, m, d:], bank[:, j, 0:T - d], w(tap), conv[:, m, d:],
                                    ALU.mult, ALU.add, f)
                    act(conv[:, base + m0:base + m0 + 2, :], conv[:, base + m0:base + m0 + 2, :], ACT.Silu, f)
                    return f
                return evacuate

            neg_a = lower[0:8, 4 * DEPTH:4 * DEPTH + 1]
            conv_bc = convolve(4)

            def bc_dt(m0, bank, done):
                if m0 == 0:
                    return conv_bc(0, bank, done)
                act(neg_a, col("a_log", l, parts=8), ACT.Exp)
                u = ts(V, dt_u[0:8, :], bank[0:8, 0, :], col("dt_bias", l, parts=8), None, ALU.add, None, done)
                z = stt(dt_e[0:8, :], dt_u[0:8, :], -1.0, dt_u[0:8, :], ALU.mult, ALU.max, S.last())
                act(dt_e[0:8, :], dt_e[0:8, :], ACT.Exp, z, scale=-1.0)
                z = act(dt_e[0:8, :], dt_e[0:8, :], ACT.Ln, bias=col("one", parts=8))
                stt(dt[0:8, :], dt_u[0:8, :], 0.0, dt_e[0:8, :], ALU.max, ALU.add, z)
                ts(V, dt_e[0:8, :], dt[0:8, :], neg_a, -1.0, ALU.mult, ALU.mult)
                V.do(lambda g: g.tensor_tensor_scan(cum[0:8, :], ones_row[0:8, :], dt_e[0:8, :], 0.0,
                                                    ALU.mult, ALU.add))
                return u

            def hf_hq(m0, bank, done):
                if m0 == 2:
                    return copy(S, hq[:, :, :], bank, done)
                f = act(hk[:, :, :], bank, ACT.Sigmoid, done)
                for j in range(2):
                    ts(V, hk[:, j, :], hk[:, j, :], lower[:, 4 + 2 * l + j:5 + 2 * l + j],
                       lower[:, 2 * l + j:2 * l + j + 1], ALU.mult, ALU.add, f)
                g_ = ts(V, log_f[:, :, :], hk[:, :, :], GATE_FLOOR, None, ALU.max, None)
                ts(V, hk[:, :, :], hk[:, :, :], -1.0, 1.0, ALU.mult, ALU.add)
                g_ = act(log_f[:, :, :], log_f[:, :, :], ACT.Ln, g_, scale=LN_SHIFT)
                ts(V, log_f[:, :, :], log_f[:, :, :], -float(np.log(LN_SHIFT)), None, ALU.add, None, g_)
                for j in range(2):
                    V.do(lambda g, j=j: g.tensor_tensor_scan(cum_f[:, j, :], ones_row, log_f[:, j, :], 0.0,
                                                             ALU.mult, ALU.add))
                return f

            run(chunk_features("in", l, 1, rot, 264, h, KT, bc_dt, h_ready))
            run(chunk_features("in", l, 0, rot, 512, h, KT, convolve(0)))
            beside = Background(
                chunk_features("in", l, 5, rot, 512, h, KT,
                               lambda m0, bank, done: act(silu_z[:, m0:m0 + 2, :], bank, ACT.Silu, done)),
                chunk_features("in", l, 2, rot, 512, h, KT, hf_hq),
                chunk_tokens("in", l, 3, rot, h, lambda b, bank, done: copy(S, v_tok[:, b, :], bank, done)),
                chunk_features("in", l, 4, rot, 512, h, KT,
                               lambda m0, bank, done: copy(S, (rq, rk)[m0 // 2][:, :, :], bank, done)),
                chunk_features("in", l, 6, rot, 512, h, KT,
                               lambda m0, bank, done: act((sig_hg, silu_rg)[m0 // 2][:, :, :], bank,
                                                          (ACT.Sigmoid, ACT.Silu)[m0 // 2], done)))

            mark = a.at
            score = a.take(2, TRI)
            dec, gmat = a.take(2, TRI), a.take(2, TRI)
            cols8 = a.take(4, 8)
            sq, o = a.take(4, T), a.take(4, T)
            conv_ready = [S.last(), V.last()]

            def turn_cols(g):
                for n, (src, b) in enumerate(((cum, 0), (cum, 1), (dt, 0), (dt, 1))):
                    ins = g.matmul(banks[3][:, n * 8:(n + 1) * 8], src[0:8, b * P:(b + 1) * P], ident[0:8, 0:8],
                                   start=True, stop=True)
                return ins
            turned = PE.do(turn_cols, *conv_ready)
            copy(V, cols8[:, :, :].rearrange("p a b -> p (a b)"), banks[3][:, 0:32], turned)
            beside.step()
            for grp in range(2):
                r = slice(64 * grp, 64 * grp + 64)
                i, bank, free = pair.take()

                def emit(g, r=r, bank=bank):
                    g.matmul(bank[:, 0:T], conv[r, 4, 0:P], conv[r, 5, :], start=True, stop=True)
                    return g.matmul(bank[:, T:TRI], conv[r, 4, P:T], conv[r, 5, P:T], start=True, stop=True)
                done = PE.do(emit, free, *conv_ready)
                pair.free[i] = copy(V, score[:, grp, :], bank[:, 0:TRI], done)

            def xs_turn(b):
                i, bank, free = pair.take()

                def emit(g):
                    for m in range(4):
                        ins = g.transpose(bank[:, m * P:(m + 1) * P], conv[:, m, b * P:(b + 1) * P], ident)
                    return ins
                turned = PE.do(emit, free)
                pair.free[i] = copy(S, xs_tok[:, b, :], bank[:, :], turned)
            xs_turn(0)
            xs_turn(1)
            xs_ready = S.last()
            beside.step()
            neg_mask = col("neg_mask", 0, TRI)
            g_free = [None, None]
            spread = {}

            def spread_cum(n):
                if n < SSD_HEADS:
                    i, bank, free = pair.take()
                    spread[n] = (i, bank, PE.do(lambda g: g.matmul(
                        bank[:, 0:T], ident[0:8, n:n + 1].broadcast_to([8, P]), cum[0:8, :],
                        start=True, stop=True), free))

            def decay(n):
                i, bank, done = spread.pop(n)
                s2 = n % 2
                stt(dec[:, s2, 0:T], bank[:, 0:T], cols8[:, 0, n:n + 1], neg_mask[:, 0:T],
                    ALU.subtract, ALU.add, done)
                pair.free[i] = stt(dec[:, s2, T:TRI], bank[:, P:T], cols8[:, 1, n:n + 1], neg_mask[:, T:TRI],
                                   ALU.subtract, ALU.add)
                return act(dec[:, s2, :], dec[:, s2, :], ACT.Exp, pair.free[i])
            spread_cum(0)
            spread_cum(1)
            e = decay(0)
            for n in range(SSD_HEADS):
                grp, s2 = n // 4, n % 2
                spread_cum(n + 2)
                e_next = decay(n + 1) if n + 1 < SSD_HEADS else None
                stt(gmat[:, s2, 0:T], score[:, grp, 0:T], cols8[:, 2, n:n + 1], dec[:, s2, 0:T],
                    ALU.mult, ALU.mult, e, g_free[s2])
                d = stt(gmat[:, s2, T:TRI], score[:, grp, T:TRI], cols8[:, 3, n:n + 1], dec[:, s2, T:TRI],
                        ALU.mult, ALU.mult)
                rows = slice(64 * (n % 2), 64 * (n % 2) + 64)
                beside.step()
                g_free[s2] = weighted_values(banks[4 + n // 4], rows, (n // 2 % 2) * T,
                                             [xs_tok[:, b, n * HEAD:(n + 1) * HEAD] for b in range(2)],
                                             gmat[:, s2, :], d, xs_ready)
                if n % 2:
                    ada_until(1)
                e = e_next
            done = PE.last()
            for m in range(4):
                stt(o[:, m, :], conv[:, m, :], col("ssd_d", 4 * l + m),
                    banks[4 + m // 2][:, (m % 2) * T:(m % 2 + 1) * T], ALU.mult, ALU.add, done)
                out_read = tt(V, o[:, m, :], o[:, m, :], silu_z[:, m, :], ALU.mult, S.last())
            beside.step()
            for grp in range(2):
                r = inverse_rms(o, [2 * grp, 2 * grp + 1], ones, sq, banks[3], 256, V.last(), S.last())
                for m in (2 * grp, 2 * grp + 1):
                    stt(mixed[:, m, :], o[:, m, :], col("ssd_norm_g", 4 * l + m), rstd[:, :],
                        ALU.mult, ALU.mult, r)
            beside.finish()

            join()
            a.at = mark
            scores, done = leveled_scores(hq, hk, cum_f, [(n // 2, 64 * (n % 2), 64) for n in range(4)], 2, a,
                                          pair, lambda: ada_until(1))
            for n in range(HG_HEADS):
                rows = slice(64 * (n % 2), 64 * (n % 2) + 64)
                last = weighted_values(banks[4], rows, (n // 2) * T,
                                       [v_tok[:, b, n * HEAD:(n + 1) * HEAD] for b in range(2)],
                                       scores[:, n, :], done, out_read)
            sq, o = a.take(2, T), a.take(2, T)
            head_norm_gate(banks[4][:, :].rearrange("p (a t) -> p a t", t=T), lambda n: mixed[:, 4 + n, :],
                           lambda n: col("hgrn_norm_g", 2 * l + n), ones_head, HEAD, sig_hg, sq, o, banks[3],
                           (0, 1), last)

            join()
            a.at = mark
            ra, rb = a.take(2, T), a.take(2, T)
            cos = col("cos", 0, T).unsqueeze(1).broadcast_to([P, 2, T])
            sin = col("sin", 0, T).unsqueeze(1).broadcast_to([P, 2, T])
            for r_ in (rq, rk):
                tt(V, ra[:, :, :], r_[:, :, :], cos, ALU.mult)
                tt(V, rb[:, :, :], r_[:, :, :], sin, ALU.mult)
                tt(V, r_[:, 0, :], ra[:, 0, :], rb[:, 1, :], ALU.subtract)
                ready = tt(V, r_[:, 1, :], rb[:, 0, :], ra[:, 1, :], ALU.add)
            rs = a.take(4, TRI)
            for n in range(RET_HEADS):
                r = slice(32 * n, 32 * n + 32)
                i, bank, free = pair.take()

                def emit(g, r=r, n=n, bank=bank):
                    for j in range(2):
                        g.matmul(bank[:, 0:T], rk[r, j, 0:P], rq[r, j, :], start=(j == 0), stop=(j == 1),
                                 tile_position=(32 * n, 0))
                    for j in range(2):
                        ins = g.matmul(bank[:, T:TRI], rk[r, j, P:T], rq[r, j, P:T],
                                       start=(j == 0), stop=(j == 1), tile_position=(32 * n, 0))
                    return ins
                done = PE.do(emit, ready, free)
                pair.free[i] = d = tt(V, rs[:, n, :], bank[:, 0:TRI], col("ret_decay", n * TRI, TRI), ALU.mult, done)
                rows = slice(64 * (n % 2), 64 * (n % 2) + 64)
                last = weighted_values(banks[5], rows, (n // 2) * T,
                                       [v_tok[:, b, 256 + n * HEAD:256 + (n + 1) * HEAD] for b in range(2)],
                                       rs[:, n, :], d, out_read)
            sq, o = a.take(2, T), a.take(2, T)
            head_norm_gate(banks[5][:, :].rearrange("p (a t) -> p a t", t=T), lambda n: mixed[:, 6 + n, :],
                           lambda n: col("one"), ones_head, HEAD, silu_rg, sq, o, banks[3], (0, 1), last)
            ada.through(l, 6)
            ready = V.last()
            for c in range(2):
                def add(m0, bank, done, c=c):
                    for j in range(2):
                        m = 4 * c + m0 + j
                        r = stt(x[:, m, :], bank[:, j, :], mod[:, 16 + m:17 + m], x[:, m, :],
                                ALU.mult, ALU.add, done)
                    return r
                run(chunk_features("out", l, c, rot, 512, mixed, KT, add, ready))

        def moe(l, mod):
            join()
            a = Arena()
            lg, ex = a.take(2, 36), a.take(2, 36)
            gmx, top, w1 = a.take(2, 1), a.take(2, 4), a.take(2, 4)
            eq4, eq8, ing, tmp8 = a.take(2, 4), a.take(2, 8), a.take(2, 8), a.take(2, 8)
            oh1, cmb, sel = a.take(2, 8), a.take(2, 32), a.take(2, 32)
            X = AX.X

            def route(g):
                for b in range(2):
                    for k in range(KT):
                        ins = g.matmul(banks[0][:, b * 36:(b + 1) * 36], h[:, k, b * P:(b + 1) * P],
                                       col("w_route", (l * KT + k) * 36, 36), start=(k == 0), stop=(k == KT - 1))
                return ins
            done = PE.do(route)
            bias = col("b_route", l * 36, 36).unsqueeze(1).broadcast_to([P, 2, 36])
            tt(V, lg[:, :, :], banks[0][:, 0:72].rearrange("p (b n) -> p b n", b=2), bias, ALU.add, done)

            def reduce(o, i, op):
                return V.do(lambda g: g.tensor_reduce(o, i, X, op))

            def first_max(dst, src, mx, n, eq, rank):
                reduce(mx, src, ALU.max)
                tt(V, eq, src, mx.broadcast_to([P, 2, n]), ALU.is_equal)
                tt(V, eq, eq, rank.unsqueeze(1).broadcast_to([P, 2, n]), ALU.mult)
                reduce(top[:, :, 3:4], eq, ALU.max)
                return tt(V, dst, eq, top[:, :, 3:4].broadcast_to([P, 2, n]), ALU.is_equal)
            first_max(eq4[:, :, :], lg[:, :, 0:4], gmx[:, :, :], 4, eq4[:, :, :], col("rank4", 0, 4))
            d = tt(V, ex[:, :, 0:4], lg[:, :, 0:4], gmx[:, :, :].broadcast_to([P, 2, 4]), ALU.subtract)
            d = act(ex[:, :, 0:4], ex[:, :, 0:4], ACT.Exp, d)
            V.do(lambda g: g.tensor_reduce(w1[:, :, 0:1], ex[:, :, 0:4], X, ALU.add), d)
            recip(w1[:, :, 0:1], w1[:, :, 0:1])
            for g_ in range(N_GROUPS):
                sel_g = eq4[:, :, g_:g_ + 1].broadcast_to([P, 2, 8])
                dst = ing if g_ == 0 else tmp8
                tt(V, dst[:, :, :], lg[:, :, 4 + 8 * g_:12 + 8 * g_], sel_g, ALU.mult)
                if g_:
                    tt(V, ing[:, :, :], ing[:, :, :], tmp8[:, :, :], ALU.add)
            first_max(oh1[:, :, :], ing[:, :, :], top[:, :, 0:1], 8, eq8[:, :, :], col("rank8", 0, 8))
            stt(tmp8[:, :, :], oh1[:, :, :], -BIG, ing[:, :, :], ALU.mult, ALU.add)
            first_max(eq8[:, :, :], tmp8[:, :, :], top[:, :, 1:2], 8, eq8[:, :, :], col("rank8", 0, 8))
            d = tt(V, top[:, :, 2:3], top[:, :, 1:2], top[:, :, 0:1], ALU.subtract)
            d = act(top[:, :, 2:3], top[:, :, 2:3], ACT.Exp, d)
            ts(V, w1[:, :, 1:2], top[:, :, 2:3], 1.0, None, ALU.add, None, d)
            recip(w1[:, :, 1:2], w1[:, :, 1:2])
            tt(V, w1[:, :, 2:3], w1[:, :, 1:2], w1[:, :, 0:1], ALU.mult)
            tt(V, w1[:, :, 3:4], w1[:, :, 2:3], top[:, :, 2:3], ALU.mult)
            tt(V, oh1[:, :, :], oh1[:, :, :], w1[:, :, 2:3].broadcast_to([P, 2, 8]), ALU.mult)
            tt(V, eq8[:, :, :], eq8[:, :, :], w1[:, :, 3:4].broadcast_to([P, 2, 8]), ALU.mult)
            tt(V, oh1[:, :, :], oh1[:, :, :], eq8[:, :, :], ALU.add)
            for g_ in range(N_GROUPS):
                d = tt(V, cmb[:, :, 8 * g_:8 * g_ + 8], oh1[:, :, :],
                       eq4[:, :, g_:g_ + 1].broadcast_to([P, 2, 8]), ALU.mult)

            onehot = eq4[:, :, :]
            rank, slot, count = a.take(2, 4), a.take(2, 1), a.take(4)
            before = col("before", 0, P)

            def ranks(g):
                g.matmul(banks[1][:, 0:4], before, onehot[:, 0, :], start=True, stop=True)
                g.matmul(banks[1][:, 4:8], ones, onehot[:, 0, :], start=True, stop=False)
                g.matmul(banks[1][:, 4:8], before, onehot[:, 1, :], start=False, stop=True)
                g.matmul(banks[1][:, 8:12], ones, onehot[:, 0, :], start=True, stop=False)
                return g.matmul(banks[1][:, 8:12], ones, onehot[:, 1, :], start=False, stop=True)
            done = PE.do(ranks, d)
            V.do(lambda g: g.tensor_reduce(count[:, 0:1], banks[1][:, 8:12], X, ALU.max), done)
            flagged = ts(V, overflow[:, :], count[:, 0:1], float(GROUP_SLOTS), None, ALU.is_gt, None)
            tt(V, rank[:, :, :], banks[1][:, 0:8].rearrange("p (b n) -> p b n", b=2),
               col("group_base", 0, 4).unsqueeze(1).broadcast_to([P, 2, 4]), ALU.add)
            tt(V, rank[:, :, :], rank[:, :, :], onehot, ALU.mult)
            reduce(slot[:, :, :], rank[:, :, :], ALU.add)
            join()
            base = a.at

            def gathered_experts():
                a.at = base
                pick, h_tok = a.take(2, N_SLOTS), a.take(2, D)
                gath = a.take(KT, N_SLOTS)
                pick_t, w_slot = a.take(N_GROUPS, T), a.take(N_GROUPS, PER_GROUP)
                silu, hid, hid_t = a.take(2, FE), a.take(2, FE), a.take(2, 2, P)
                y_slot = a.take(N_GROUPS, D)
                for b in range(2):
                    d = ts(V, pick[:, b, :], col("slot_no", 0, N_SLOTS), slot[:, b, :], None, ALU.is_equal, None)
                rot = Banks([0, 1, 2, 3, 4, 5, 6, 7])
                for b in range(2):
                    for c in range(2):
                        i, bank, free = rot.take()

                        def turn_h(g, b=b, c=c, bank=bank):
                            for k in range(4):
                                ins = g.transpose(bank[:, k * P:(k + 1) * P],
                                                  h[:, 4 * c + k, b * P:(b + 1) * P], ident)
                            return ins
                        done = PE.do(turn_h, free)
                        rot.free[i] = h_ready = copy(S, h_tok[:, b, 512 * c:512 * c + 512], bank[:, :], done)
                for k in range(KT):
                    i, bank, free = rot.take()

                    def gather(g, k=k, bank=bank):
                        g.matmul(bank[:, :], h_tok[:, 0, k * P:(k + 1) * P], pick[:, 0, :], start=True, stop=False)
                        return g.matmul(bank[:, :], h_tok[:, 1, k * P:(k + 1) * P], pick[:, 1, :],
                                        start=False, stop=True)
                    done = PE.do(gather, free, h_ready, d)
                    rot.free[i] = copy((S, V)[k % 2], gath[:, k, :], bank[:, :], done)
                gath_ready = [S.last(), V.last()]
                for j in range(2):
                    i, bank, free = rot.take()

                    def turn_pick(g, j=j, bank=bank):
                        for n in range(2):
                            for b in range(2):
                                ins = g.transpose(bank[:, n * T + b * P:n * T + (b + 1) * P],
                                                  pick[:, b, (2 * j + n) * P:(2 * j + n + 1) * P], ident)
                        return ins
                    done = PE.do(turn_pick, free, d)
                    rot.free[i] = copy(V, pick_t[:, 2 * j:2 * j + 2, :],
                                       bank[:, :].rearrange("p (n t) -> p n t", t=T), done)
                i, bank, free = rot.take()

                def slot_weights(g, bank=bank):
                    for n in range(N_GROUPS):
                        for b in range(2):
                            ins = g.matmul(bank[:, n * 8:(n + 1) * 8], pick[:, b, n * P:(n + 1) * P], oh1[:, b, :],
                                           start=(b == 0), stop=(b == 1))
                    return ins
                done = PE.do(slot_weights, free)
                copy(V, w_slot[:, :, :], bank[:, 0:32].rearrange("p (n e) -> p n e", e=8), done)
                PE.held = PE.held + [S.last(), V.last()]
                PE.pad_to(pe_start + PRELUDE)

                gu_free, turn_free, y_free = [None, None], [None, None], [None, None]
                hid_ready, hid_t_ready, hid_t_free, hid_free = [None] * 2, [None] * 2, [None] * 2, [None] * 2
                for e in range(N_EXPERTS + 1):
                    if e < N_EXPERTS:
                        p, grp = e % 2, e // PER_GROUP
                        w, landed, chunk = weight("gate_up", l, e)
                        wv = w.rearrange("p (k n) -> p k n", k=KT)

                        def gate_up(g, lo, hi, wv=wv, p=p, grp=grp):
                            for k in range(lo, hi):
                                ins = g.matmul(banks[4 + p][:, :], gath[:, k, grp * P:(grp + 1) * P], wv[:, k, :],
                                               start=(k == 0), stop=(k == KT - 1))
                            return ins
                        PE.do(lambda g, f=gate_up: f(g, 0, 4), landed, gu_free[p], *gath_ready)
                    if e > 0:
                        q = (e - 1) % 2

                        def turn_hid(g, q=q):
                            for f in range(2):
                                ins = g.transpose(banks[6 + q][:, f * P:(f + 1) * P], hid[:, q, f * P:(f + 1) * P],
                                                  ident)
                            return ins
                        hid_free[q] = PE.do(turn_hid, hid_ready[q], turn_free[q])
                        turn_free[q] = hid_t_ready[q] = copy(
                            S, hid_t[:, q, :, :], banks[6 + q][:, 0:FE].rearrange("p (f t) -> p f t", t=P),
                            hid_free[q], hid_t_free[q])
                    if e < N_EXPERTS:
                        done = consumed_step(chunk, PE.do(lambda g, f=gate_up: f(g, 4, KT)))
                        s = act(silu[:, p, :], banks[4 + p][:, 0:FE], ACT.Silu, done, hid_ready[p])
                        gu_free[p] = hid_ready[p] = stt(hid[:, p, :], silu[:, p, :],
                                                        w_slot[:, grp, e % PER_GROUP:e % PER_GROUP + 1],
                                                        banks[4 + p][:, FE:2 * FE], ALU.mult, ALU.mult, s, hid_free[p])
                    if e > 0:
                        j = e - 1
                        q, grp, yb = j % 2, j // PER_GROUP, 0
                        w, landed, chunk = weight("down", l, j)
                        wv = w.rearrange("p (k n) -> p k n", k=2)

                        def down(g, q=q, j=j, yb=yb, wv=wv):
                            for f in range(2):
                                for c in range(2):
                                    ins = g.matmul(banks[yb + c][:, :], hid_t[:, q, f, :],
                                                   wv[:, f, 512 * c:512 * (c + 1)],
                                                   start=(j % PER_GROUP == 0 and f == 0),
                                                   stop=(j % PER_GROUP == PER_GROUP - 1 and f == 1))
                            return ins
                        hid_t_free[q] = consumed_step(chunk, PE.do(down, landed, hid_t_ready[q], y_free[yb // 2]))
                        if j % PER_GROUP == PER_GROUP - 1:
                            for c in range(2):
                                y_free[yb // 2] = copy(V, y_slot[:, grp, 512 * c:512 * (c + 1)], banks[yb + c][:, :],
                                                       hid_t_free[q])
                    beside_expert(e)
                ada.settle()
                PE.held = PE.held + [V.last()]
                def scatter(g):
                    for m in range(KT):
                        for n in range(N_GROUPS):
                            ins = g.matmul(banks[m // 2][:, (m % 2) * T:(m % 2 + 1) * T],
                                           y_slot[:, n, m * P:(m + 1) * P], pick_t[:, n, :],
                                           start=(n == 0), stop=(n == N_GROUPS - 1))
                    return ins
                PE.do(scatter, V.last())

            def dense_experts():
                a.at = base
                comb = a.take(N_EXPERTS, T)
                comb_t = a.take(T)
                def turn(g):
                    for b in range(2):
                        ins = g.transpose(banks[1][0:32, b * P:(b + 1) * P], cmb[:, b, :], ident)
                    return ins
                done = PE.do(turn)
                d = copy(V, comb_t[0:32, :], banks[1][0:32, 0:T], done)
                rot = Banks([2, 3])
                for e in range(0, N_EXPERTS, 2):
                    i, bank, free = rot.take()

                    def spread(g, e=e, bank=bank):
                        for j in range(2):
                            ins = g.matmul(bank[:, j * T:(j + 1) * T],
                                           ident[0:32, e + j:e + j + 1].broadcast_to([32, P]), comb_t[0:32, :],
                                           start=True, stop=True)
                        return ins
                    done = PE.do(spread, free, d)
                    rot.free[i] = copy(S, comb[:, e:e + 2, :], bank[:, :].rearrange("p (a t) -> p a t", t=T), done)
                join()
                PE.pad_to(pe_start + PRELUDE)

                silu, hid = a.take(2, 2, T), a.take(2, 2, T)
                hid_free, pair_free = [None, None], [None, None]
                hid_ready = [None, None]
                for e in range(N_EXPERTS + 1):
                    if e < N_EXPERTS:
                        p = e % 2
                        gate, up = banks[4], banks[5]
                        w, landed, chunk = weight("gate_up", l, e)
                        wv = w.rearrange("p (k n) -> p k n", k=KT)

                        def half(g, bank, base, wv=wv):
                            for m in range(2):
                                for k in range(KT):
                                    ins = g.matmul(bank[:, m * T:(m + 1) * T], wv[:, k, base + m * P:base + (m + 1) * P],
                                                   h[:, k, :], start=(k == 0), stop=(k == KT - 1))
                            return ins
                        done_g = PE.do(lambda g, gate=gate, half=half: half(g, gate, 0), landed, pair_free[1 - p])
                        s = act(silu[:, p, :, :], gate[:, :].rearrange("p (a t) -> p a t", t=T), ACT.Silu, done_g,
                                hid_ready[p])
                        if e > 0:
                            PE.pad_to(PE.count + 1)
                        done_u = PE.do(lambda g, up=up, half=half: half(g, up, FE))
                        consumed_step(chunk, done_u)
                        upv = up[:, :].rearrange("p (a t) -> p a t", t=T)
                        pair_free[p] = tt(V, silu[:, p, :, :], silu[:, p, :, :], upv, ALU.mult, done_u, s)
                        hid_ready[p] = tt(V, hid[:, p, :, :], silu[:, p, :, :],
                                          comb[:, e, :].unsqueeze(1).broadcast_to([P, 2, T]), ALU.mult, hid_free[p])
                    else:
                        PE.pad_to(PE.count + 1)
                    if e > 0:
                        q = (e - 1) % 2
                        w, landed, chunk = weight("down", l, e - 1)
                        wv = w.rearrange("p (k n) -> p k n", k=2)

                        def down(g, e=e - 1, q=q, wv=wv):
                            for f in range(2):
                                for m in range(KT):
                                    ins = g.matmul(banks[m // 2][:, (m % 2) * T:(m % 2 + 1) * T],
                                                   wv[:, f, m * P:(m + 1) * P], hid[:, q, f, :],
                                                   start=(e == 0 and f == 0 and m % 2 == 0),
                                                   stop=(e == N_EXPERTS - 1 and f == 1), skip_group_check=True)
                            return ins
                        hid_free[q] = consumed_step(chunk, PE.do(down, landed, hid_ready[q]))
                    beside_expert(e)
                ada.settle()

            pe_start, v_start = PE.count, V.count
            PRELUDE, V_PRELUDE, V_STEPS = 24, 40, 16
            ada_end = 12 * (l + 2)
            ada.settle()
            ada_start = ada.state()

            def beside_expert(e):
                V.pad_to(v_start + V_PRELUDE + V_STEPS * e)
                if ada.begun < ada_end and e % 2 == 1:
                    ada.step()
            first_chunk, starts = taken[0], [(e, e.count, e.steps, e.held) for e in (PE, V, S)]
            paths = []
            for path in (gathered_experts, dense_experts):
                taken[0] = first_chunk
                for e, n, _, held in starts:
                    e.count, e.steps, e.held = n, [], list(held)
                ada.restore(ada_start)
                ada.bank = banks[2 if path is gathered_experts else 6]
                path()
                paths.append([(e.count, e.steps) for e, _, _, _ in starts])
            for n, (e, _, before_branch, held) in enumerate(starts):
                top_count = max(paths[0][n][0], paths[1][n][0])
                for count_, steps in (paths[0][n], paths[1][n]):
                    e.count, e.steps = count_, steps
                    e.pad_to(top_count)
                e.steps, e.held = before_branch, []
                e.steps.append(([flagged] + held, ("branch", overflow[0:1, 0:1], paths[1][n][1], paths[0][n][1])))
            ada.bank, ada.acc_free, ada.bank_free = banks[2], [None, None], None
            join()
            for m in range(KT):
                stt(x[:, m, :], banks[m // 2][:, (m % 2) * T:(m % 2 + 1) * T], mod[:, 40 + m:41 + m], x[:, m, :],
                    ALU.mult, ALU.add, PE.last())

        def gated_residual(mod, y, gain, gate_at, sq):
            col2 = small[:, 8:16]
            tt(V, col2, mod[:, gate_at:gate_at + 8], gain, ALU.mult)
            r = inverse_rms(y, list(range(KT)), ones, sq, banks[7], D, V.last(), S.last())
            for k in range(KT):
                stt(y[:, k, :], y[:, k, :], col2[:, k:k + 1], rstd[:, :], ALU.mult, ALU.mult, r)
                tt(V, x[:, k, :], x[:, k, :], y[:, k, :], ALU.add)

        def project_out(name, src, y):
            rot = Banks([0, 1, 2, 3])
            for c in range(2):
                w, landed, chunk = weight(name, 0, c)
                features(rot, w, landed, chunk, 512, src, KT,
                         lambda m0, bank, done, c=c: copy(S, y[:, 4 * c + m0:4 * c + m0 + 2, :], bank, done))

        def rglru(l, h_ready):
            join()
            a = Arena()
            xc, gate = a.take(KT, T), a.take(KT, T)
            r_, i_, decay, mult = a.take(KT, T), a.take(KT, T), a.take(KT, T), a.take(KT, T)
            sp = small[:, 16:32]
            rot = Banks([0, 1, 2, 3])
            lam = col("rg_lambda", 0, KT)
            d = stt(sp[:, 0:8], lam, -1.0, lam, ALU.mult, ALU.max)
            act(sp[:, 0:8], sp[:, 0:8], ACT.Exp, d, scale=-1.0)
            d = act(sp[:, 0:8], sp[:, 0:8], ACT.Ln, bias=col("one"))
            ts(V, sp[:, 8:16], lam, -1.0, 0.0, ALU.mult, ALU.max, d)
            tt(V, sp[:, 8:16], sp[:, 8:16], sp[:, 0:8], ALU.add)
            ts(V, sp[:, 0:8], sp[:, 8:16], -RG_C, None, ALU.mult, None)
            ts(V, sp[:, 8:16], sp[:, 8:16], RG_C, None, ALU.mult, None)

            def convolve(m0, bank, done, c):
                for j in range(2):
                    m = 4 * c + m0 + j
                    w = lambda tap: col("rg_conv_w", tap * KT + m)
                    f = act(xc[:, m, :], bank[:, j, :], ACT.Identity, done, V.last(), scale=w(3),
                            bias=col("rg_conv_b", m))
                    for tap in (2, 1, 0):
                        s = 3 - tap
                        f = stt(xc[:, m, s:], bank[:, j, 0:T - s], w(tap), xc[:, m, s:], ALU.mult, ALU.add, f)
                return f
            for c in range(2):
                w, landed, chunk = weight("rg_in", 0, 2 + c)
                features(rot, w, landed, chunk, 512, h, KT,
                         lambda m0, bank, done, c=c: convolve(m0, bank, done, c), h_ready)
            conv_done = V.last()
            gw, g_landed, g_chunk = weight("rg_gates", 0, 0)
            for c in range(2):
                w, landed, chunk = weight("rg_in", 0, c)
                features(rot, w, landed, chunk, 512, h, KT,
                         lambda m0, bank, done, c=c: act(gate[:, 4 * c + m0:4 * c + m0 + 2, :], bank,
                                                         ACT.Gelu_apprx_tanh, done))
            gv = gw.rearrange("p (w b k n) -> p w b k n", w=2, b=RG_BLOCKS, k=2)
            for which, (dst, bias) in enumerate(((r_, "rg_ba"), (i_, "rg_bx"))):
                for b in range(RG_BLOCKS):
                    i, bank, free = rot.take()

                    def emit(g, which=which, b=b, bank=bank):
                        for m in range(2):
                            for k in range(2):
                                ins = g.matmul(bank[:, m * T:(m + 1) * T], gv[:, which, b, k, m * P:(m + 1) * P],
                                               xc[:, 2 * b + k, :], start=(k == 0), stop=(k == 1))
                        return ins
                    done = PE.do(emit, g_landed, conv_done, free)
                    for m in range(2):
                        rot.free[i] = act(dst[:, 2 * b + m, :], bank[:, m * T:(m + 1) * T], ACT.Sigmoid, done,
                                          bias=col(bias, 2 * b + m))
            consumed[g_chunk] = PE.last()
            for m in range(KT):
                act(decay[:, m, :], r_[:, m, :], ACT.Exp, scale=sp[:, m:m + 1])
                e = act(mult[:, m, :], r_[:, m, :], ACT.Tanh, scale=sp[:, 8 + m:9 + m])
            ts(V, r_[:, :, :], mult[:, :, :], 1.0, None, ALU.add, None, e)
            recip(r_[:, :, :], r_[:, :, :])
            stt(mult[:, :, :], mult[:, :, :], 2.0, r_[:, :, :], ALU.mult, ALU.mult)
            d = ts(V, mult[:, :, :], mult[:, :, :], GATE_FLOOR, None, ALU.max, None)
            e = act(mult[:, :, :], mult[:, :, :], ACT.Sqrt, d)
            tt(V, i_[:, :, :], i_[:, :, :], xc[:, :, :], ALU.mult)
            tt(V, i_[:, :, :], i_[:, :, :], mult[:, :, :], ALU.mult, e)
            for m in range(KT):
                V.do(lambda g, m=m: g.tensor_tensor_scan(r_[:, m, :], decay[:, m, :], i_[:, m, :], 0.0,
                                                         ALU.mult, ALU.add))
            tt(V, xc[:, :, :], gate[:, :, :], r_[:, :, :], ALU.mult)
            join()
            project_out("rg_out", xc, decay)
            return decay, mult

        def gla(l, h_ready):
            join()
            a = Arena()
            q, k, cum = a.take(4, T), a.take(4, T), a.take(4, T)
            v_tok, silu_r = a.take(2, D), a.take(KT, T)
            z = a.take(T)
            lgt = a.take(4, T)
            ones_row = a.take(T)
            rot = Banks([0, 1, 2, 3])
            V.do(lambda g: g.memset(ones_row, 1.0))
            w_z = col("gla_w_z", 0, KT * GLA_RANK).rearrange("p (k n) -> p k n", k=KT)

            def z_product(g):
                for kk in range(KT):
                    ins = g.matmul(banks[4][0:GLA_RANK, 0:T], w_z[:, kk, :], h[:, kk, :],
                                   start=(kk == 0), stop=(kk == KT - 1))
                return ins
            done = PE.do(z_product, h_ready)
            d = copy(V, z[0:GLA_RANK, :], banks[4][0:GLA_RANK, 0:T], done)

            def alpha(g):
                for m in range(4):
                    ins = g.matmul(banks[5 + m // 2][:, (m % 2) * T:(m % 2 + 1) * T],
                                   tab[0:GLA_RANK, OFFSET["gla_w_alpha"] + m * P:OFFSET["gla_w_alpha"] + (m + 1) * P],
                                   z[0:GLA_RANK, :], start=True, stop=True)
                return ins
            done = PE.do(alpha, d)
            for m in range(4):
                d = ts(V, lgt[:, m, :], banks[5 + m // 2][:, (m % 2) * T:(m % 2 + 1) * T],
                       col("gla_b_alpha", m), None, ALU.add, None, done)
            ab = a.take(4, T)
            d = stt(ab[:, :, :], lgt[:, :, :], -1.0, lgt[:, :, :], ALU.mult, ALU.max)
            act(ab[:, :, :], ab[:, :, :], ACT.Exp, d, scale=-1.0)
            d = act(ab[:, :, :], ab[:, :, :], ACT.Ln, bias=col("one"))
            stt(lgt[:, :, :], lgt[:, :, :], 0.0, ab[:, :, :], ALU.min, ALU.subtract, d)
            ts(V, lgt[:, :, :], lgt[:, :, :], 1.0 / GLA_TAU, None, ALU.mult, None)
            for m in range(4):
                V.do(lambda g, m=m: g.tensor_tensor_scan(cum[:, m, :], ones_row, lgt[:, m, :], 0.0,
                                                         ALU.mult, ALU.add))
            w, landed, chunk = weight("gla_in", 0, 1)
            features(rot, w, landed, chunk, 512, h, KT,
                     lambda m0, bank, done: copy(S, k[:, m0:m0 + 2, :], bank, done))
            w, landed, chunk = weight("gla_in", 0, 0)
            features(rot, w, landed, chunk, 512, h, KT,
                     lambda m0, bank, done: S.do(lambda g: g.activation(
                         q[:, m0:m0 + 2, :], bank, ACT.Copy, bias=0.0, scale=GLA_DK ** -0.5), done))
            for c in range(2):
                w, landed, chunk = weight("gla_in", 0, 2 + c)
                tokens(rot, w, landed, chunk, h,
                       lambda b, bank, done, c=c: copy(S, v_tok[:, b, 512 * c:512 * (c + 1)], bank, done))
            for c in range(2):
                w, landed, chunk = weight("gla_in", 0, 4 + c)
                features(rot, w, landed, chunk, 512, h, KT,
                         lambda m0, bank, done, c=c: act(silu_r[:, 4 * c + m0:4 * c + m0 + 2, :], bank,
                                                         ACT.Silu, done))
            join()
            a.at = a.at - 1024 - T - 1024 - T
            scores, done = leveled_scores(q, k, cum, [(n, 0, P) for n in range(4)], 4, a, Banks([6, 7]),
                                          lambda: None)
            o = h
            for n in range(GLA_HEADS):
                for j in range(2):
                    m = 2 * n + j
                    last = weighted_values(banks[m // 2], slice(0, P), j * T,
                                           [v_tok[:, b, m * P:(m + 1) * P] for b in range(2)],
                                           scores[:, n, :], done)
                copy(S, o[:, 2 * n:2 * n + 2, :], banks[n][:, :].rearrange("p (a t) -> p a t", t=T), last)
            join()
            sq = v_tok.rearrange("p a b -> p (a b)").rearrange("p (a b) -> p a b", b=T)
            for n in range(GLA_HEADS):
                r = inverse_rms(o, [2 * n, 2 * n + 1], ones, sq, banks[4], GLA_DV, V.last(), S.last())
                for j in range(2):
                    m = 2 * n + j
                    stt(o[:, m, :], o[:, m, :], col("gla_norm_g", j), rstd[:, :], ALU.mult, ALU.mult, r)
                    tt(V, o[:, m, :], o[:, m, :], silu_r[:, m, :], ALU.mult)
            join()
            y = arena[:, 0:2048].rearrange("p (a b) -> p a b", b=T)
            project_out("gla_out", o, y)
            return y, sq

        def conv_ffn(l, h_ready):
            join()
            a = Arena()
            y, sq = a.take(KT, T), a.take(KT, T)
            act_t = a.take(FT, T)
            tmp = a.take(2, 4, T)
            rot = Banks([0, 1, 3, 4])
            rot2 = [0, None, None]
            for c in range(FT // 2):
                w, landed, chunk = weight("ffn_up", l, c)
                buf = tmp[:, c % 2, :, :]

                def convolve(m0, bank, done, c=c, buf=buf):
                    for j in range(2):
                        m = (0 if m0 == 0 else FT) + 2 * c + j
                        w = lambda tap: col("ffn_conv_w", (l * FFN_CONV + tap) * 2 * FT + m)
                        d = buf[:, m0 + j, :]
                        f = act(d, bank[:, j, :], ACT.Identity, done, V.last(), scale=w(2),
                                bias=col("ffn_conv_b", l * 2 * FT + m))
                        for tap in (1, 0):
                            s = 2 - tap
                            f = stt(d[:, s:], bank[:, j, 0:T - s], w(tap), d[:, s:], ALU.mult, ALU.add, f)
                    if m0 == 0:
                        act(buf[:, 0:2, :], buf[:, 0:2, :], ACT.Gelu_apprx_tanh, f)
                    else:
                        tt(V, act_t[:, 2 * c:2 * c + 2, :], buf[:, 0:2, :], buf[:, 2:4, :], ALU.mult, S.last())
                    return f
                features(rot, w, landed, chunk, 512, h, KT, convolve, h_ready)
                ada.step()
            ready = V.last()
            for m in range(KT):
                w, landed, chunk = weight("ffn_down", l, m)
                features(rot, w, landed, chunk, P, act_t, FT,
                         lambda m0, bank, done, m=m: copy(S, y[:, m:m + 1, :], bank, done), ready)
            return y, sq

        for which, name in ((0, "c"), (1, "c_2")):
            act(c_act[:, 8 * which:8 * which + 8], col(name, 0, 8), ACT.Silu, TABLE)
        lb, tmp4 = col("hgrn_lb", 0, 4), lower[:, 8:16]
        tt(V, tmp4[:, 0:2], lb[:, 0:2], lb[:, 2:4], ALU.max, TABLE)
        tt(V, lower[:, 0:2], lb[:, 0:2], tmp4[:, 0:2], ALU.subtract)
        d = tt(V, lower[:, 2:4], lb[:, 2:4], tmp4[:, 0:2], ALU.subtract)
        d = act(lower[:, 0:4], lower[:, 0:4], ACT.Exp, d)
        tt(V, tmp4[:, 0:2], lower[:, 0:2], lower[:, 2:4], ALU.add, d)
        recip(tmp4[:, 2:4], tmp4[:, 0:2])
        tt(V, lower[:, 0:2], lower[:, 0:2], tmp4[:, 2:4], ALU.mult)
        tt(V, lower[:, 2:4], lower[:, 2:4], tmp4[:, 2:4], ALU.mult)
        tt(V, lower[:, 2:4], lower[:, 0:2], lower[:, 2:4], ALU.add)
        tt(V, lower[:, 2:4], lower[:, 2:4], lower[:, 0:2], ALU.subtract)
        tt(V, lower[:, 0:2], lower[:, 0:2], lower[:, 0:2], ALU.subtract)
        ts(V, lower[:, 4:8], lower[:, 0:4], -1.0, 1.0, ALU.mult, ALU.add)
        for e in (PE, V, S):
            e.held = e.held + [X_IN]

        for l in range(DEPTH):
            mod = mods[:, 48 * l:48 * l + 48]
            ada.through(l, 4)
            ready = modulated_norm(mod, col("norm_mix_g", 8 * l, 8), 0, 8)
            token_mixer(l, mod, ready)
            ada.through(l, 12)
            modulated_norm(mod, col("norm_ffn_g", 8 * l, 8), 24, 32)
            moe(l, mod)
        join()
        sq = Arena().take(KT, T)
        r = inverse_rms(x, list(range(KT)), ones, sq, banks[0], D)
        for k in range(KT):
            stt(x[:, k, :], x[:, k, :], col("final_g", k), rstd[:, :], ALU.mult, ALU.mult, r)

        for l in range(DEPTH):
            mod = mods[:, 48 * (2 + l):48 * (2 + l) + 48]
            ada.through(2 + l, 12)
            ready = modulated_norm(mod, col("norm_g_2", (4 * l) * 8, 8), 0, 8)
            y, sq = (rglru if l == 0 else gla)(l, ready)
            join()
            gated_residual(mod, y, col("norm_g_2", (4 * l + 1) * 8, 8), 16, sq)
            ready = modulated_norm(mod, col("norm_g_2", (4 * l + 2) * 8, 8), 24, 32)
            y, sq = conv_ffn(l, ready)
            join()
            gated_residual(mod, y, col("norm_g_2", (4 * l + 3) * 8, 8), 40, sq)
        finished = V.last()
        assert taken[0] == len(order) == len(sizes)

        block = ctx.enter_context(nc.Block())

        @block.sync
        def _(sp):
            sp.dma_start(tab[:, :], table).then_inc(s_table, 16)
            sp.dma_start(x.rearrange("p k t -> p (k t)"), x_in).then_inc(s_x, 16)
            for k, (start, n, off) in enumerate(where):
                for j in reuse[k]:
                    sp.wait_ge(*consumed[j])
                sp.dma_start(ring[:, start:start + n],
                             weights[off:off + n * P].rearrange("(p n) -> p n", p=P)
                             ).then_inc(s_ring[k % RING_UNITS], 16)
            sp.wait_ge(*finished)
            sp.dma_start(out, x.rearrange("p k t -> p (k t)")).then_inc(s_out, 16)
            sp.wait_ge(s_out, 16)

        @block.tensor
        def _(eng):
            PE.play(eng)

        @block.vector
        def _(eng):
            V.play(eng)

        @block.scalar
        def _(eng):
            S.play(eng)

        @block.gpsimd
        def _(eng):
            G.play(eng)

    return order


def kernel(**inputs):
    import concourse.bacc as bacc
    from concourse.bass_utils import run_bass_kernel_spmd as run

    i = {name: np.asarray(a) for name, a in inputs.items()}

    def columns(a):
        return a.reshape(-1, P).T

    def chunk(w):
        return w.reshape(-1, P, w.shape[1]).transpose(1, 0, 2).reshape(P, -1)

    def wide(a):
        return np.pad(a, ((0, P - a.shape[0]), (0, 0)))

    s_, t_ = np.arange(P)[:, None], np.arange(T)[None, :]
    causal = np.concatenate([s_ <= t_, s_ + P <= t_[:, P:]], axis=1)
    lag = np.concatenate([t_ - s_, t_[:, P:] - s_ - P], axis=1)
    gamma = np.log1p(-np.exp2(-5.0 - np.arange(RET_HEADS)))
    decay = np.where(causal, np.exp(gamma[:, None, None] * lag * causal), 0.0) * HEAD ** -0.5
    half = HEAD // 2
    freq = (10000.0 ** (-np.arange(half, dtype=np.float32) / half)).astype(np.float32)
    angle = (np.arange(T, dtype=np.float32)[None, :] * np.tile(freq, 4)[:, None]).astype(np.float64)
    t1 = np.arange(P)[None, :]
    levels = [((s_ // (2 * n) == t1 // (2 * n)) & (s_ % (2 * n) < n) & (t1 % (2 * n) >= n)) for n in LEVELS]
    heads64 = (s_ // HEAD == t1 // HEAD)
    one = np.ones((P, 1))
    route = np.concatenate([i["w_grp"], i["w_exp"]], axis=2)
    b_route = np.concatenate([i["b_grp"], i["b_exp"]], axis=1)
    parts = {
        "c": columns(i["c"]), "c_2": columns(i["c_2"]), "final_g": columns(i["final_norm_g"]),
        "zero": np.zeros((P, 1)), "one": one, "eps": np.full((P, 1), EPS),
        "norm_mix_g": columns(i["norm_mix_g"]), "norm_ffn_g": columns(i["norm_ffn_g"]),
        "b_ada": columns(i["b_ada"]), "b_ada_2": columns(i["ada_b_2"]), "norm_g_2": columns(i["norm_g_2"]),
        "conv_w": columns(i["conv_w"]), "conv_b": columns(i["conv_b"]),
        "ssd_d": np.concatenate([columns(np.repeat(i["ssd_d"][l], HEAD)) for l in range(DEPTH)], axis=1),
        "ssd_norm_g": columns(i["ssd_norm_g"]),
        "dt_bias": wide(i["ssd_dt_bias"].T), "a_log": wide(i["ssd_a_log"].T),
        "hgrn_lb": columns(i["hgrn_lower_bounds"]), "hgrn_norm_g": columns(i["hgrn_norm_g"]),
        "b_route": np.broadcast_to(b_route.reshape(1, -1), (P, 36 * DEPTH)),
        "w_route": np.concatenate([chunk(route[l]) for l in range(DEPTH)], axis=1),
        "ffn_conv_w": columns(i["ffn_conv_w_2"]), "ffn_conv_b": columns(i["ffn_conv_b_2"]),
        "rg_conv_w": columns(i["rg_conv_w_2"]), "rg_conv_b": columns(i["rg_conv_b_2"]),
        "rg_ba": columns(i["rg_ba_2"]), "rg_bx": columns(i["rg_bx_2"]), "rg_lambda": columns(i["rg_lambda_2"]),
        "gla_b_alpha": columns(i["gla_b_alpha_2"]), "gla_norm_g": columns(i["gla_norm_g_2"]),
        "gla_w_z": chunk(i["gla_w_in_2"][0][:, 2 * 512 + 2 * D:]), "gla_w_alpha": wide(i["gla_w_alpha_2"][0]),
        "ident": np.eye(P), "ones": np.ones((P, P)), "ones_head": heads64,
        "neg_mask": np.where(causal, 0.0, -BIG), "level_mask": np.concatenate(levels, axis=1),
        "cos": np.cos(angle), "sin": np.sin(angle),
        "ret_decay": np.concatenate(list(decay), axis=1),
        "rank4": np.broadcast_to(np.arange(4, 0, -1), (P, 4)), "rank8": np.broadcast_to(np.arange(8, 0, -1), (P, 8)),
        "before": s_ < t1, "slot_no": np.broadcast_to(np.arange(N_SLOTS), (P, N_SLOTS)),
        "group_base": np.broadcast_to(GROUP_SLOTS * np.arange(N_GROUPS), (P, N_GROUPS)),
    }
    for name, width in COLS.items():
        assert parts[name].shape == (P, width), (name, parts[name].shape, width)
    table = np.concatenate([np.asarray(parts[name], np.float32) for name in COLS], axis=1)

    off = np.cumsum([0, 512, 768, 8] + [256] * 8)
    z, xbc, dt, hq, hf, hi, hg, rq, rk, rv, rg = [np.arange(off[n], off[n + 1]) for n in range(11)]

    def by_halves(cols):
        return cols.reshape(RET_HEADS, 2, half).transpose(1, 0, 2).reshape(-1)
    in_cols = [xbc[:512], np.concatenate([xbc[512:], dt]), np.concatenate([hf, hq]), np.concatenate([hi, rv]),
               np.concatenate([by_halves(rq), by_halves(rk)]), z, np.concatenate([hg, rg])]

    def piece(name, l, n):
        span = slice(512 * n, 512 * n + 512)
        if name == "ada":
            return chunk(i["w_ada"][l][:, span])
        if name == "ada_2":
            return chunk(i["ada_w_2"][l][:, span])
        if name == "in":
            return chunk(i["w_in"][l][:, in_cols[n]])
        if name == "out":
            return chunk(i["w_out"][l][:, span])
        if name == "gate_up":
            return chunk(np.concatenate([i["w_gate"][l, n], i["w_up"][l, n]], axis=1))
        if name == "down":
            return chunk(i["w_down"][l, n])
        if name == "rg_in":
            return chunk(i["rg_w_in_2"][0][:, span])
        if name == "rg_gates":
            return np.concatenate([chunk(w[0, b]) for w in (i["rg_wa_2"], i["rg_wx_2"]) for b in range(RG_BLOCKS)],
                                  axis=1)
        if name == "rg_out":
            return chunk(i["rg_w_out_2"][0][:, span])
        if name == "gla_in":
            return chunk(i["gla_w_in_2"][0][:, span])
        if name == "gla_out":
            return chunk(i["gla_w_out_2"][0][:, span])
        if name == "ffn_up":
            w = i["ffn_w_up_2"][l]
            return chunk(np.concatenate([w[:, 256 * n:256 * n + 256], w[:, D_FF + 256 * n:D_FF + 256 * n + 256]],
                                        axis=1))
        return chunk(i["ffn_w_down_2"][l][:, P * n:P * n + P])

    x_t = np.ascontiguousarray(chunk(i["x"].reshape(T, D).T))

    nc = bacc.Bacc("TRN2", target_bir_lowering=False, num_devices=1)
    sizes = chunk_sizes()
    w_ap = nc.dram_tensor("weights", (P * sum(sizes.values()),), F32, kind="ExternalInput").ap()
    t_ap = nc.dram_tensor("table", table.shape, F32, kind="ExternalInput").ap()
    x_ap = nc.dram_tensor("x_t", x_t.shape, F32, kind="ExternalInput").ap()
    o_ap = nc.dram_tensor("y_t", (P, KT * T), F32, kind="ExternalOutput").ap()
    order = two_stacks_kernel(nc, w_ap, t_ap, x_ap, o_ap)
    stream = []
    for key in order:
        p = piece(*key)
        assert p.shape == (P, sizes[key]), (key, p.shape)
        stream.append(p.reshape(-1))
    stream = np.concatenate(stream)
    got = run(nc, [{"weights": stream, "table": table, "x_t": x_t}], core_ids=[0])
    y = got.results[0]["y_t"].reshape(P, KT, T)
    return np.ascontiguousarray(y.transpose(2, 1, 0)).reshape(1, T, D)
```

```python
from contextlib import ExitStack

import numpy as np
import concourse.bass as bass
from concourse import mybir

F32 = mybir.dt.float32
U32 = mybir.dt.uint32
ALU = mybir.AluOpType
ACT = mybir.ActivationFunctionType
AX = mybir.AxisListType

P = 128
D = 1024
T = 256
KT = D // P
DEPTH = 2
EPS = 1e-6

SSD_HEADS, SSD_GROUPS, SSD_CONV = 8, 2, 4
HEAD = 64
HG_HEADS = RET_HEADS = 4
N_GROUPS, PER_GROUP = 4, 8
N_EXPERTS = N_GROUPS * PER_GROUP
FE = D // 4
GATE_FLOOR = 1e-30
TANH_FLOOR = 1e-19
LN_SHIFT = 2.0 ** 40

RG_BLOCKS, RG_CONV, RG_C = 4, 4, 8.0
GLA_HEADS, GLA_DK, GLA_DV, GLA_RANK, GLA_TAU = 4, 128, 256, 16, 16.0
D_FF = ((8 * D // 3 + 127) // 128) * 128
FT = D_FF // P
FFN_CONV = 3
TRI = T + P
LEVELS = [1, 2, 4, 8, 16, 32, 64]
BIG = 1e30
GROUP_SLOTS = 128
N_SLOTS = N_GROUPS * GROUP_SLOTS

FIRST_LATER = "conv_w"
COLS = {
    "c": 8, "c_2": 8, "final_g": 8, "zero": 1, "one": 1, "eps": 1,
    "norm_mix_g": 8 * DEPTH, "norm_ffn_g": 8 * DEPTH, "b_ada": 48 * DEPTH, "b_ada_2": 48 * DEPTH,
    "norm_g_2": 8 * 4 * DEPTH, "hgrn_lb": 2 * DEPTH, "mean_all": P,
    "conv_w": 6 * SSD_CONV * DEPTH, "conv_b": 6 * DEPTH, "ssd_d": 4 * DEPTH, "ssd_norm_g": 4 * DEPTH,
    "dt_bias": DEPTH, "a_log": DEPTH, "hgrn_norm_g": 2 * DEPTH,
    "b_route": 36 * DEPTH, "w_route": KT * 36 * DEPTH,
    "ffn_conv_w": 2 * FT * FFN_CONV * DEPTH, "ffn_conv_b": 2 * FT * DEPTH,
    "rg_conv_w": KT * RG_CONV, "rg_conv_b": KT, "rg_ba": KT, "rg_bx": KT, "rg_lambda": KT,
    "gla_b_alpha": 4, "gla_norm_g": 2, "gla_w_z": KT * GLA_RANK, "gla_w_alpha": 512,
    "ident": P, "ones": P, "mean_256": P, "mean_head": P, "neg_mask": TRI, "level_mask": len(LEVELS) * P,
    "cos": T, "sin": T, "ret_decay": RET_HEADS * TRI, "rank4": 4, "rank8": 8,
    "before": P, "slot_no": N_SLOTS, "group_base": 4,
}
OFFSET, _at = {}, 0
for _name, _width in COLS.items():
    OFFSET[_name] = _at
    _at += _width
N_COLS = _at

UNIT = 2048


IN_WIDTHS = [512, 264, 512, 512, 512, 512, 512]


def chunk_sizes():
    out = {}
    for l in range(DEPTH):
        for name in ("ada", "ada_2"):
            out.update({(name, l, i): 4096 for i in range(12)})
        out.update({("in", l, i): KT * n for i, n in enumerate(IN_WIDTHS)})
        out.update({("out", l, i): 4096 for i in range(2)})
        out.update({("gate_up", l, e): 4096 for e in range(N_EXPERTS)})
        out.update({("down", l, e): 2048 for e in range(N_EXPERTS)})
        out.update({("ffn_up", l, i): 4096 for i in range(FT // 2)})
        out.update({("ffn_down", l, i): FT * P for i in range(KT)})
    out.update({("rg_in", 0, i): 4096 for i in range(4)})
    out.update({("rg_gates", 0, 0): 4096})
    out.update({("rg_out", 0, i): 4096 for i in range(2)})
    out.update({("gla_in", 0, i): 4096 for i in range(6)})
    out.update({("gla_out", 0, i): 4096 for i in range(2)})
    return out


class Engine:

    def __init__(self, sem, in_order):
        self.sem, self.in_order = sem, in_order
        self.count, self.steps, self.held = 0, [], []

    def last(self):
        return (self.sem, self.count)

    def do(self, emit, *after):
        waits = [a for a in after if a is not None] + self.held
        self.held = []
        if self.in_order:
            waits.append(self.last())
        self.count += 1
        self.steps.append(([w for w in waits if w[1] > 0], emit))
        return (self.sem, self.count)

    def pad_to(self, count):
        assert count >= self.count, (count, self.count)
        if count > self.count:
            sem, now = self.sem, self.count
            self.steps.append(([(sem, now)], ("pad", count - now)))
            self.count = count

    def play(self, eng):
        self.play_steps(eng, self.steps, [])

    def play_steps(self, eng, steps, passed):
        for waits, emit in steps:
            if isinstance(emit, tuple) and emit[0] == "branch":
                _, flag, when_set, otherwise = emit
                self.wait(eng, waits, passed)
                value = eng.value_load(flag)
                with eng.If(value > 0):
                    self.play_steps(eng, when_set, list(passed))
                with eng.Else():
                    self.play_steps(eng, otherwise, list(passed))
                continue
            self.wait(eng, waits, passed)
            if isinstance(emit, tuple):
                eng.sem_inc(self.sem, emit[1])
                continue
            emit(eng).then_inc(self.sem, 1)

    def wait(self, eng, waits, passed):
        for sem, value in waits:
            known = [i for i, (s, _) in enumerate(passed) if s is sem]
            if known and passed[known[0]][1] >= value:
                continue
            eng.wait_ge(sem, value)
            if known:
                passed[known[0]] = (sem, value)
            else:
                passed.append((sem, value))


def two_stacks_kernel(nc, weights, table, x_in, out):
    with ExitStack() as ctx:
        def sb(name, cols):
            return ctx.enter_context(nc.sbuf_tensor(name, [P, cols], F32))

        def sem(name):
            return ctx.enter_context(nc.semaphore(name))

        RING_UNITS = 10
        ring = sb("weight_ring", RING_UNITS * UNIT)
        tab = sb("parameter_table", N_COLS)
        x = sb("residual", KT * T)[:, :].rearrange("p (k t) -> p k t", t=T)
        h = sb("normed", KT * T)[:, :].rearrange("p (k t) -> p k t", t=T)
        arena = sb("arena", 17408)
        mods = sb("modulations", 4 * 48)
        ada_acc = sb("ada_acc", 2 * 512)
        small = sb("gains", 8 + 8 + 16)
        rstd = sb("rstd", T)[:, :]
        squares = sb("squares", KT * T)[:, :].rearrange("p (k t) -> p k t", t=T)
        c_act = sb("c_act", 16)
        lower = sb("lower_bound", 4 * DEPTH + 8)
        overflow = ctx.enter_context(nc.sbuf_tensor("overflow", [P, 1], mybir.dt.int32))
        banks = [ctx.enter_context(nc.psum_tensor(f"bank{i}", [P, 512], F32)) for i in range(8)]

        s_table, s_later, s_x, s_out = sem("s_table"), sem("s_table_later"), sem("s_x"), sem("s_out")
        s_ring = [sem(f"s_ring{i}") for i in range(RING_UNITS)]
        PE = Engine(sem("s_tensor"), False)
        V = Engine(sem("s_vector"), True)
        S = Engine(sem("s_scalar"), True)
        G = Engine(sem("s_gpsimd"), True)
        TABLE, TABLE_LATER, X_IN = (s_table, 16), (s_later, 16), (s_x, 16)

        def col(name, i=0, n=1, parts=P):
            o = OFFSET[name] + i
            return tab[0:parts, o:o + n]

        def join():
            ends = [e.last() for e in (PE, V, S, G)]
            for e in (PE, V, S, G):
                e.held = e.held + ends

        class Arena:
            def __init__(self):
                self.at = 0

            def take(self, *shape):
                n = int(np.prod(shape))
                ap = arena[:, self.at:self.at + n]
                self.at += n
                assert self.at <= 17408, self.at
                if len(shape) == 2:
                    return ap.rearrange("p (a b) -> p a b", b=shape[1])
                if len(shape) == 3:
                    return ap.rearrange("p (a b c) -> p a b c", b=shape[1], c=shape[2])
                return ap

        def tt(e, o, a, b, op, *after):
            return e.do(lambda g: g.tensor_tensor(o, a, b, op), *after)

        def ts(e, o, a, s1, s2, op0, op1, *after):
            if s2 is None:
                return e.do(lambda g: g.tensor_scalar(o, a, s1, None, op0), *after)
            return e.do(lambda g: g.tensor_scalar(o, a, s1, s2, op0, op1), *after)

        def stt(o, a, s, b, op0, op1, *after):
            return V.do(lambda g: g.scalar_tensor_tensor(out=o, in0=a, scalar=s, in1=b, op0=op0, op1=op1), *after)

        def recip(o, a, *after):
            return V.do(lambda g: g.reciprocal(o, a), *after)

        def act(o, a, func, *after, scale=1.0, bias=None):
            b = bias if bias is not None else 0.0
            if bias is None and func != ACT.Copy:
                b = col("zero", parts=a.shape[0])
            return S.do(lambda g: g.activation(o, a, func, bias=b, scale=scale), *after)

        def copy(e, o, a, *after):
            if e is S:
                return S.do(lambda g: g.activation(o, a, ACT.Copy, bias=0.0, scale=1.0), *after)
            return e.do(lambda g: g.tensor_copy(o, a), *after)

        sizes = chunk_sizes()
        order, where, owner, reuse = [], [], [None] * RING_UNITS, []
        ring_at = [0, 0]

        def place_chunk(key):
            n = sizes[key]
            units = -(-n // UNIT)
            if ring_at[0] % RING_UNITS + units > RING_UNITS:
                ring_at[0] += RING_UNITS - ring_at[0] % RING_UNITS
            u = ring_at[0] % RING_UNITS
            reuse.append([owner[j] for j in range(u, u + units) if owner[j] is not None])
            for j in range(u, u + units):
                owner[j] = len(order)
            order.append(key)
            where.append((u * UNIT, n, ring_at[1]))
            ring_at[0] += units
            ring_at[1] += n * P
        consumed = [None] * len(sizes)
        taken = [0]

        def consumed_step(chunk, token):
            assert consumed[chunk] in (None, token), (chunk, consumed[chunk], token)
            consumed[chunk] = token
            return token

        def weight(name, l, i):
            k = taken[0]
            if k == len(order):
                place_chunk((name, l, i))
            assert order[k] == (name, l, i), (order[k], name, l, i)
            taken[0] += 1
            start, n, _ = where[k]
            return ring[:, start:start + n], (s_ring[k % RING_UNITS], 16 * (k // RING_UNITS + 1)), k

        class Banks:
            def __init__(self, ids):
                self.ids, self.n, self.free = ids, 0, {i: None for i in ids}

            def take(self):
                i = self.ids[self.n % len(self.ids)]
                self.n += 1
                return i, banks[i], self.free[i]

        def run(steps):
            for _ in steps:
                pass

        def features(*args, **kw):
            run(feature_steps(*args, **kw))

        def tokens(*args, **kw):
            run(token_steps(*args, **kw))

        def chunk_features(name, l, i, *args, **kw):
            yield from feature_steps(*(args[0:1] + weight(name, l, i) + args[1:]), **kw)

        def chunk_tokens(name, l, i, *args, **kw):
            yield from token_steps(*(args[0:1] + weight(name, l, i) + args[1:]), **kw)

        def feature_steps(rot, w, landed, chunk, ncols, rhs, nk, evacuate, ready=None):
            wv = w.rearrange("p (k n) -> p k n", k=nk)
            tiles = -(-ncols // P)
            done = None
            for m0 in range(0, tiles, 2):
                i, bank, free = rot.take()
                ms = [m for m in (m0, m0 + 1) if m < tiles]

                def emit(g, ms=ms, bank=bank):
                    for m in ms:
                        width = min(P, ncols - m * P)
                        for k in range(nk):
                            ins = g.matmul(bank[0:width, (m - ms[0]) * T:(m - ms[0] + 1) * T],
                                           wv[:, k, m * P:m * P + width], rhs[:, k, :],
                                           start=(k == 0), stop=(k == nk - 1))
                    return ins
                done = PE.do(emit, landed, free, ready)
                if m0 + 2 >= tiles:
                    consumed_step(chunk, done)
                rot.free[i] = evacuate(m0, bank[:, 0:len(ms) * T].rearrange("p (a t) -> p a t", t=T), done)
                yield

        def token_steps(rot, w, landed, chunk, rhs, evacuate, ready=None):
            wv = w.rearrange("p (k n) -> p k n", k=KT)
            for b in range(2):
                i, bank, free = rot.take()

                def emit(g, b=b, bank=bank):
                    for k in range(KT):
                        ins = g.matmul(bank[:, :], rhs[:, k, b * P:(b + 1) * P], wv[:, k, :],
                                       start=(k == 0), stop=(k == KT - 1))
                    return ins
                done = PE.do(emit, landed, free, ready)
                if b == 1:
                    consumed_step(chunk, done)
                rot.free[i] = evacuate(b, bank[:, :], done)
                yield

        def causal_conv(bank, out, done, weight_of, bias_of, taps, free=None):
            for j in range(2):
                first = act(out[j], bank[:, j, :], ACT.Identity, done, free, scale=weight_of(j, taps - 1),
                            bias=bias_of(j))
            for j in range(2):
                for tap in range(taps - 2, -1, -1):
                    d = taps - 1 - tap
                    last = stt(out[j][:, d:], bank[:, j, 0:T - d], weight_of(j, tap), out[j][:, d:],
                               ALU.mult, ALU.add, first)
            return last

        ones = col("ones", 0, P)
        mean_all, mean_256, mean_head = col("mean_all", 0, P), col("mean_256", 0, P), col("mean_head", 0, P)
        ident = col("ident", 0, P)

        def inverse_root(bank, done, o, *after):
            act(o, bank, ACT.Ln, done, *after, bias=col("eps"))
            return act(o, o, ACT.Exp, scale=-0.5)

        class MeanSquare:

            sq_read = None

            def __init__(self, bank):
                self.bank, self.waiting, self.begun = bank, [], 0

            def add(self, e, src, m, n, ready):
                self.flush()
                o, v = squares[:, m:m + n, :], src[:, m:m + n, :]
                if e is S:
                    q = act(o, v, ACT.Square, ready, MeanSquare.sq_read)
                else:
                    q = tt(V, o, v, v, ALU.mult, ready, MeanSquare.sq_read)
                self.waiting = [(m + j, q) for j in range(n)]

            def flush(self):
                for m, q in self.waiting:
                    k = self.begun
                    self.begun += 1
                    self.last = PE.do(lambda g, m=m, k=k: g.matmul(
                        self.bank[:, 0:T], mean_all, squares[:, m, :], start=(k == 0), stop=(k == KT - 1)), q)
                self.waiting = []

            def inverse(self):
                self.flush()
                assert self.begun == KT
                self.begun, MeanSquare.sq_read = 0, self.last
                return inverse_root(self.bank[:, 0:T], self.last, rstd, V.last())

        def modulated_norm(mod, gain, shift_at, scale_at):
            gain1 = small[:, 0:8]
            stt(gain1, mod[:, scale_at:scale_at + 8], col("one"), gain, ALU.add, ALU.mult)
            r = x_squares.inverse()
            for k in range(KT):
                m = stt(h[:, k, :], x[:, k, :], gain1[:, k:k + 1], rstd, ALU.mult, ALU.mult, r)
                last = act(h[:, k, :], h[:, k, :], ACT.Identity, m, bias=mod[:, shift_at + k:shift_at + k + 1])
            return last

        class Modulations:
            def __init__(self, chunks):
                self.chunks, self.bank = chunks, None
                self.begun = 0
                self.scaled = self.summed = None
                self.acc_free, self.bank_free = [None, None], None

            def step(self):
                if self.begun == len(self.chunks):
                    return
                self.sum_rows()
                name, l, i, c_at, bias = self.chunks[self.begun]
                w, landed, chunk = weight(name, l, i)
                wv = w.rearrange("p (k n) -> p k n", k=KT)
                p = self.begun % 2
                acc = ada_acc[:, 512 * p:512 * p + 512]
                for k in range(KT):
                    c_k = c_act[:, c_at + k:c_at + k + 1]
                    if k == 0:
                        done = ts(V, acc, wv[:, k, :], c_k, None, ALU.mult, None, landed, self.acc_free[p])
                    else:
                        done = stt(acc, wv[:, k, :], c_k, acc, ALU.mult, ALU.add)
                consumed_step(chunk, done)
                self.add_bias()
                self.scaled = (acc, p, 4 * self.begun, bias, done)
                self.begun += 1

            def sum_rows(self):
                if self.scaled is not None:
                    acc, p, dst, bias, done = self.scaled
                    bank = self.bank

                    def emit(g):
                        for m in range(4):
                            ins = g.matmul(bank[:, m:m + 1], acc[:, m * P:(m + 1) * P], col("one"),
                                           start=True, stop=True)
                        return ins
                    self.acc_free[p] = PE.do(emit, done, self.bank_free)
                    self.summed = (bank, dst, bias, self.acc_free[p])
                    self.scaled = None

            def add_bias(self):
                if self.summed is not None:
                    bank, dst, bias, done = self.summed
                    self.bank_free = tt(V, mods[:, dst:dst + 4], bank[:, 0:4], bias, ALU.add, done)
                    self.summed = None

            def through(self, layer, chunks):
                while self.begun < 12 * layer + chunks:
                    self.step()
                self.settle()

            def settle(self):
                self.add_bias()
                self.sum_rows()
                self.add_bias()

            def state(self):
                return (self.begun, self.scaled, self.summed, list(self.acc_free), self.bank_free)

            def restore(self, state):
                self.begun, self.scaled, self.summed, acc_free, self.bank_free = state
                self.acc_free = list(acc_free)

        class Background:

            def __init__(self, *steps):
                self.steps = list(steps)

            def step(self, n=1):
                while n and self.steps:
                    try:
                        next(self.steps[0])
                        n -= 1
                    except StopIteration:
                        self.steps.pop(0)

            def finish(self):
                while self.steps:
                    self.step()

        def weighted_values(bank, rows, cols, v, g384, *after):
            def emit(g):
                g.matmul(bank[rows, cols:cols + T], v[0], g384[:, 0:T], start=True, stop=False)
                return g.matmul(bank[rows, cols + P:cols + T], v[1], g384[:, T:TRI], start=False, stop=True)
            return PE.do(emit, *after)

        def leveled_scores(q, k, cum, heads, nt, a, rot, beside, *after):
            scores = a.take(4, TRI)
            expo2, both2 = a.take(2, nt * T), a.take(2, nt * T)
            zero = G.do(lambda g: g.memset(scores[:, :, :], 0.0), V.last(), S.last(), PE.last(), *after)
            level_mask = tab[:, OFFSET["level_mask"]:OFFSET["level_mask"] + 7 * P].bitcast(U32)
            diagonal = tab[:, OFFSET["ident"]:OFFSET["ident"] + P].bitcast(U32)
            kinds = [[n for n in range(4) if heads[n][1] == row] for row in sorted({hd[1] for hd in heads})]
            if len(kinds) == 2:
                groups = [(members, (0, 1)) for members in kinds]
            else:
                groups = [(kinds[0], (0,)), (kinds[0], (1,))]

            def products(lhs, rhs, off_diagonal, *wait):
                out = []
                for members, blocks in groups:
                    if off_diagonal:
                        blocks = blocks[:1]
                        if blocks[0] == 1:
                            continue
                    i, bank, free = rot.take()

                    def emit(g, members=members, blocks=blocks, bank=bank):
                        at_ = 0
                        for b in blocks:
                            t0 = P if off_diagonal else b * P
                            for n in members:
                                tile, row, rows = heads[n]
                                ins = g.matmul(bank[:, at_:at_ + P], lhs[row:row + rows, tile, b * P:b * P + P],
                                               rhs[row:row + rows, tile, t0:t0 + P], start=True, stop=True)
                                at_ += P
                        return ins
                    done = PE.do(emit, free, *wait)
                    for at_, b in enumerate(blocks):
                        width = len(members) * P
                        out.append((members, b, i, bank[:, at_ * width:(at_ + 1) * width], done))
                return out

            def place(blocks, mask):
                for members, b, i, data, done in blocks:
                    m0, step, count = members[0], (members[1] - members[0]), len(members)
                    cols = P if mask is None else b * T
                    dst = scores[:, m0:m0 + step * (count - 1) + 1:step, cols:cols + P]
                    data = data.rearrange("p (n t) -> p n t", t=P)
                    if mask is None:
                        rot.free[i] = copy(V, dst, data, done)
                    else:
                        m = mask.unsqueeze(1).broadcast_to([P, count, P])
                        rot.free[i] = V.do(lambda g, dst=dst, m=m, data=data: g.copy_predicated(dst, m, data),
                                           done, zero)

            halves = LEVELS + [P]

            def views(n):
                seg = dict(n=nt * T // (2 * halves[n]), t=2 * halves[n])
                flat = [v.rearrange("p n t -> p (n t)").rearrange("p (n t) -> p n t", **seg) for v in (cum, q, k)]
                return flat + [expo2[:, n % 2, :].rearrange("p (n t) -> p n t", **seg),
                               both2[:, n % 2, :].rearrange("p (n t) -> p n t", **seg)]

            def exponents(n):
                half = halves[n]
                cv, _, _, ev, _ = views(n)
                mid = cv[:, :, half - 1:half].broadcast_to([P, nt * T // (2 * half), half])
                tt(V, ev[:, :, 0:half], mid, cv[:, :, 0:half], ALU.subtract, *after)
                d = tt(V, ev[:, :, half:], cv[:, :, half:], mid, ALU.subtract)
                return act(expo2[:, n % 2, :], expo2[:, n % 2, :], ACT.Exp, d)

            def factors(n, e, read):
                half = halves[n]
                _, qv, kv, ev, bv = views(n)
                tt(V, bv[:, :, 0:half], kv[:, :, 0:half], ev[:, :, 0:half], ALU.mult, e, read)
                return tt(V, bv[:, :, half:], qv[:, :, half:], ev[:, :, half:], ALU.mult)

            e = exponents(0)
            waiting, mask = products(k, q, False, *after), diagonal
            read = [None, None]
            for n in range(len(halves)):
                e_next = exponents(n + 1) if n + 1 < len(halves) else None
                w = factors(n, e, read[n % 2])
                place(waiting, mask)
                both_v = both2[:, n % 2, :].rearrange("p (n t) -> p n t", t=T)
                waiting = products(both_v, both_v, halves[n] == P, w)
                mask = level_mask[:, n * P:(n + 1) * P] if halves[n] < P else None
                read[n % 2] = PE.last()
                e = e_next
                beside()
            place(waiting, mask)
            return scores, V.last()

        def group_rms(o, groups, sq, sum_banks):
            q = tt(V, sq[:, 0:2 * groups, :], o[:, 0:2 * groups, :], o[:, 0:2 * groups, :], ALU.mult,
                   S.last(), PE.last())
            done = []
            for n in range(0, groups, 2):
                def emit(g, n=n):
                    for m in (n, n + 1):
                        for j in range(2):
                            ins = g.matmul(sum_banks[n // 2][:, (m - n) * T:(m - n + 1) * T], mean_256,
                                           sq[:, 2 * m + j, :], start=(j == 0), stop=(j == 1))
                    return ins
                done.append(PE.do(emit, q))
            for n in range(0, groups, 2):
                act(sq[:, n:n + 2, :], sum_banks[n // 2][:, :].rearrange("p (a t) -> p a t", t=T), ACT.Ln, done[-1],
                    bias=col("eps"))
            r = act(sq[:, 0:groups, :], sq[:, 0:groups, :], ACT.Exp, scale=-0.5)
            return sq, r

        def head_norm_gates(parts, buffers):
            sums = []
            for (src, _, _, _, sum_bank, written), (sq, o) in zip(parts, buffers):
                c = copy(S, o[:, :, :], src[:, :].rearrange("p (a t) -> p a t", t=T), written)
                q = tt(V, sq[:, :, :], o[:, :, :], o[:, :, :], ALU.mult, c)
                sums.append(PE.do(lambda g, sum_bank=sum_bank, sq=sq: g.matmul(
                    sum_bank[:, :], mean_head, sq.rearrange("p a t -> p (a t)"), start=True, stop=True), q))
            for (_, _, gain, gate, _, _), (_, o) in zip(parts, buffers):
                tt(V, o[:, :, :], o[:, :, :], gate, ALU.mult)
                if gain is not None:
                    for n in range(2):
                        ts(V, o[:, n, :], o[:, n, :], gain(n), None, ALU.mult, None)
            for (_, _, _, _, sum_bank, _), (sq, _), done in zip(parts, buffers, sums):
                act(sq.rearrange("p a t -> p (a t)"), sum_bank[:, :], ACT.Ln, done, bias=col("eps"))
            for (_, dst, _, _, _, _), (sq, o) in zip(parts, buffers):
                r = act(sq[:, :, :], sq[:, :, :], ACT.Exp, scale=-0.5)
                tt(V, dst, o[:, :, :], sq[:, :, :], ALU.mult, r)

        ada = Modulations([(name, l, i, 8 * which, col(("b_ada", "b_ada_2")[which], 48 * l + 4 * i, 4))
                           for name, l, which in (("ada", 0, 0), ("ada", 1, 0), ("ada_2", 0, 1), ("ada_2", 1, 1))
                           for i in range(12)])
        ada.bank = banks[2]

        def ada_until(layer):
            if ada.begun < 12 * layer:
                ada.step()

        def token_mixer(l, mod, h_ready):
            join()
            a = Arena()
            mixed = a.take(KT, T)
            conv = a.take(6, T)
            silu_z, sig_hg, silu_rg = a.take(4, T), a.take(2, T), a.take(2, T)
            v_tok, xs_tok = a.take(2, 512), a.take(2, 512)
            hq, hk, cum_f = a.take(2, T), a.take(2, T), a.take(2, T)
            rq, rk = a.take(2, T), a.take(2, T)
            dts = a.take(4, T)
            dt_u, dt_e, dt, cum = [dts[:, n, :] for n in range(4)]
            log_f, ones_row = a.take(2, T), a.take(T)
            V.do(lambda g: g.memset(ones_row, 1.0))
            rot, pair = Banks([0, 1]), Banks([6, 7])

            def convolve(base):
                def evacuate(m0, bank, done):
                    m = base + m0
                    f = causal_conv(bank, [conv[:, m + j, :] for j in range(2)], done,
                                    lambda j, tap: col("conv_w", (l * SSD_CONV + tap) * 6 + m + j),
                                    lambda j: col("conv_b", l * 6 + m + j), SSD_CONV)
                    act(conv[:, base + m0:base + m0 + 2, :], conv[:, base + m0:base + m0 + 2, :], ACT.Silu, f)
                    return f
                return evacuate

            neg_a = lower[0:8, 4 * DEPTH:4 * DEPTH + 1]
            conv_bc = convolve(4)

            def bc_dt(m0, bank, done):
                if m0 == 0:
                    return conv_bc(0, bank, done)
                act(neg_a, col("a_log", l, parts=8), ACT.Exp)
                u = ts(V, dt_u[0:8, :], bank[0:8, 0, :], col("dt_bias", l, parts=8), None, ALU.add, None, done)
                z = stt(dt_e[0:8, :], dt_u[0:8, :], -1.0, dt_u[0:8, :], ALU.mult, ALU.max, S.last())
                act(dt_e[0:8, :], dt_e[0:8, :], ACT.Exp, z, scale=-1.0)
                z = act(dt_e[0:8, :], dt_e[0:8, :], ACT.Ln, bias=col("one", parts=8))
                stt(dt[0:8, :], dt_u[0:8, :], 0.0, dt_e[0:8, :], ALU.max, ALU.add, z)
                ts(V, dt_e[0:8, :], dt[0:8, :], neg_a, -1.0, ALU.mult, ALU.mult)
                V.do(lambda g: g.tensor_tensor_scan(cum[0:8, :], ones_row[0:8, :], dt_e[0:8, :], 0.0,
                                                    ALU.mult, ALU.add))
                return u

            def hf_hq(m0, bank, done):
                if m0 == 2:
                    return copy(S, hq[:, :, :], bank, done)
                f = act(hk[:, :, :], bank, ACT.Sigmoid, done)
                for j in range(2):
                    ts(V, hk[:, j, :], hk[:, j, :], lower[:, 4 + 2 * l + j:5 + 2 * l + j],
                       lower[:, 2 * l + j:2 * l + j + 1], ALU.mult, ALU.add, f)
                g_ = ts(V, log_f[:, :, :], hk[:, :, :], GATE_FLOOR, None, ALU.max, None)
                ts(V, hk[:, :, :], hk[:, :, :], -1.0, 1.0, ALU.mult, ALU.add)
                g_ = act(log_f[:, :, :], log_f[:, :, :], ACT.Ln, g_, scale=LN_SHIFT)
                ts(V, log_f[:, :, :], log_f[:, :, :], -float(np.log(LN_SHIFT)), None, ALU.add, None, g_)
                for j in range(2):
                    V.do(lambda g, j=j: g.tensor_tensor_scan(cum_f[:, j, :], ones_row, log_f[:, j, :], 0.0,
                                                             ALU.mult, ALU.add))
                return f

            run(chunk_features("in", l, 1, rot, 264, h, KT, bc_dt, h_ready))
            run(chunk_features("in", l, 0, rot, 512, h, KT, convolve(0)))
            beside = Background(
                chunk_features("in", l, 5, rot, 512, h, KT,
                               lambda m0, bank, done: act(silu_z[:, m0:m0 + 2, :], bank, ACT.Silu, done)),
                chunk_features("in", l, 2, rot, 512, h, KT, hf_hq),
                chunk_tokens("in", l, 3, rot, h, lambda b, bank, done: copy(S, v_tok[:, b, :], bank, done)),
                chunk_features("in", l, 4, rot, 512, h, KT,
                               lambda m0, bank, done: copy(S, (rq, rk)[m0 // 2][:, :, :], bank, done)),
                chunk_features("in", l, 6, rot, 512, h, KT,
                               lambda m0, bank, done: act((sig_hg, silu_rg)[m0 // 2][:, :, :], bank,
                                                          (ACT.Sigmoid, ACT.Silu)[m0 // 2], done)))

            mark = a.at
            score = a.take(2, TRI)
            dec, gmat = a.take(2, TRI), a.take(2, TRI)
            cols8 = a.take(4, 8)
            sq, o = a.take(4, T), a.take(4, T)
            conv_ready = [S.last(), V.last()]

            def turn_cols(g):
                for n, (src, b) in enumerate(((cum, 0), (cum, 1), (dt, 0), (dt, 1))):
                    ins = g.matmul(banks[3][:, n * 8:(n + 1) * 8], src[0:8, b * P:(b + 1) * P], ident[0:8, 0:8],
                                   start=True, stop=True)
                return ins
            turned = PE.do(turn_cols, *conv_ready)
            copy(V, cols8[:, :, :].rearrange("p a b -> p (a b)"), banks[3][:, 0:32], turned)
            beside.step()
            for grp in range(2):
                r = slice(64 * grp, 64 * grp + 64)
                i, bank, free = pair.take()

                def emit(g, r=r, bank=bank):
                    g.matmul(bank[:, 0:T], conv[r, 4, 0:P], conv[r, 5, :], start=True, stop=True)
                    return g.matmul(bank[:, T:TRI], conv[r, 4, P:T], conv[r, 5, P:T], start=True, stop=True)
                done = PE.do(emit, free, *conv_ready)
                pair.free[i] = copy(V, score[:, grp, :], bank[:, 0:TRI], done)

            def xs_turn(b):
                i, bank, free = pair.take()

                def emit(g):
                    for m in range(4):
                        ins = g.transpose(bank[:, m * P:(m + 1) * P], conv[:, m, b * P:(b + 1) * P], ident)
                    return ins
                turned = PE.do(emit, free)
                pair.free[i] = copy(S, xs_tok[:, b, :], bank[:, :], turned)
            xs_turn(0)
            xs_turn(1)
            xs_ready = S.last()
            beside.step()
            neg_mask = col("neg_mask", 0, TRI)
            g_free = [None, None]
            spread = {}

            def spread_cum(n):
                if n < SSD_HEADS:
                    i, bank, free = pair.take()
                    spread[n] = (i, bank, PE.do(lambda g: g.matmul(
                        bank[:, 0:T], ident[0:8, n:n + 1].broadcast_to([8, P]), cum[0:8, :],
                        start=True, stop=True), free))

            def decay(n):
                i, bank, done = spread.pop(n)
                s2 = n % 2
                stt(dec[:, s2, 0:T], bank[:, 0:T], cols8[:, 0, n:n + 1], neg_mask[:, 0:T],
                    ALU.subtract, ALU.add, done)
                pair.free[i] = stt(dec[:, s2, T:TRI], bank[:, P:T], cols8[:, 1, n:n + 1], neg_mask[:, T:TRI],
                                   ALU.subtract, ALU.add)
                return act(dec[:, s2, :], dec[:, s2, :], ACT.Exp, pair.free[i])
            spread_cum(0)
            spread_cum(1)
            e = decay(0)
            for n in range(SSD_HEADS):
                grp, s2 = n // 4, n % 2
                spread_cum(n + 2)
                e_next = decay(n + 1) if n + 1 < SSD_HEADS else None
                stt(gmat[:, s2, 0:T], score[:, grp, 0:T], cols8[:, 2, n:n + 1], dec[:, s2, 0:T],
                    ALU.mult, ALU.mult, e, g_free[s2])
                d = stt(gmat[:, s2, T:TRI], score[:, grp, T:TRI], cols8[:, 3, n:n + 1], dec[:, s2, T:TRI],
                        ALU.mult, ALU.mult)
                rows = slice(64 * (n % 2), 64 * (n % 2) + 64)
                beside.step()
                g_free[s2] = weighted_values(banks[4 + n // 4], rows, (n // 2 % 2) * T,
                                             [xs_tok[:, b, n * HEAD:(n + 1) * HEAD] for b in range(2)],
                                             gmat[:, s2, :], d, xs_ready)
                ada_until(1)
                e = e_next
            done = PE.last()
            for m in range(4):
                stt(o[:, m, :], conv[:, m, :], col("ssd_d", 4 * l + m),
                    banks[4 + m // 2][:, (m % 2) * T:(m % 2 + 1) * T], ALU.mult, ALU.add, done)
                out_read = tt(V, o[:, m, :], o[:, m, :], silu_z[:, m, :], ALU.mult, S.last())
            beside.step()
            group_rstd, r = group_rms(o, 2, sq, [banks[3]])
            for grp in range(2):
                for m in (2 * grp, 2 * grp + 1):
                    stt(mixed[:, m, :], o[:, m, :], col("ssd_norm_g", 4 * l + m), group_rstd[:, grp, :],
                        ALU.mult, ALU.mult, r)
            beside.finish()

            join()
            a.at = mark
            rs = conv.rearrange("p a b -> p (a b)").rearrange("p (a b) -> p a b", b=TRI)
            xs_old = xs_tok.rearrange("p a b -> p (a b)").rearrange("p (a b) -> p a b", b=T)
            ra, rb = xs_old[:, 0:2, :], xs_old[:, 2:4, :]
            norms = [(silu_z[:, 0:2, :], silu_z[:, 2:4, :]), (dts[:, 0:2, :], dts[:, 2:4, :])]
            hgrn_scores, scored = leveled_scores(hq, hk, cum_f, [(n // 2, 64 * (n % 2), 64) for n in range(4)],
                                                 2, a, pair, lambda: ada_until(1))
            cos = col("cos", 0, T).unsqueeze(1).broadcast_to([P, 2, T])
            sin = col("sin", 0, T).unsqueeze(1).broadcast_to([P, 2, T])
            for r_ in (rq, rk):
                tt(G, ra[:, :, :], r_[:, :, :], cos, ALU.mult)
                tt(G, rb[:, :, :], r_[:, :, :], sin, ALU.mult)
                tt(G, r_[:, 0, :], ra[:, 0, :], rb[:, 1, :], ALU.subtract)
                rotated = tt(G, r_[:, 1, :], rb[:, 0, :], ra[:, 1, :], ALU.add)
            waiting = {}

            def retention_scores(n):
                r = slice(32 * n, 32 * n + 32)
                i, bank, free = pair.take()

                def emit(g):
                    for j in range(2):
                        g.matmul(bank[:, 0:T], rk[r, j, 0:P], rq[r, j, :], start=(j == 0), stop=(j == 1),
                                 tile_position=(32 * n, 0))
                    for j in range(2):
                        ins = g.matmul(bank[:, T:TRI], rk[r, j, P:T], rq[r, j, P:T],
                                       start=(j == 0), stop=(j == 1), tile_position=(32 * n, 0))
                    return ins
                waiting[n] = (i, bank, PE.do(emit, rotated, free))

            def decayed(n):
                i, bank, done = waiting[n]
                pair.free[i] = waiting[n] = tt(V, rs[:, n, :], bank[:, 0:TRI], col("ret_decay", n * TRI, TRI),
                                               ALU.mult, done)

            def head_values(bank, n, v_at, scores, done):
                return weighted_values(bank, slice(64 * (n % 2), 64 * (n % 2) + 64), (n // 2) * T,
                                       [v_tok[:, b, v_at + n * HEAD:v_at + (n + 1) * HEAD] for b in range(2)],
                                       scores[:, n, :], done, out_read)
            retention_scores(0)
            retention_scores(1)
            for n in range(HG_HEADS):
                hgrn_out = head_values(banks[4], n, 0, hgrn_scores, scored)
            for n in (0, 1):
                decayed(n)
            for n in (2, 3):
                retention_scores(n)
            for n in (0, 1):
                head_values(banks[5], n, 256, rs, waiting[n])
            for n in (2, 3):
                decayed(n)
                ret_out = head_values(banks[5], n, 256, rs, waiting[n])
            head_norm_gates([
                (banks[4], mixed[:, 4:6, :], lambda n: col("hgrn_norm_g", 2 * l + n), sig_hg, banks[3], hgrn_out),
                (banks[5], mixed[:, 6:8, :], None, silu_rg, banks[6], ret_out)], norms)
            ada.through(l, 6)
            ready = V.last()
            for c in range(2):
                def add(m0, bank, done, c=c):
                    for j in range(2):
                        m = 4 * c + m0 + j
                        r = stt(x[:, m, :], bank[:, j, :], mod[:, 16 + m:17 + m], x[:, m, :],
                                ALU.mult, ALU.add, done)
                    x_squares.add(S, x, 4 * c + m0, 2, r)
                    return r
                run(chunk_features("out", l, c, rot, 512, mixed, KT, add, ready))

        def moe(l, mod):
            join()
            a = Arena()
            lg, ex = a.take(2, 36), a.take(2, 36)
            gmx, top, w1 = a.take(2, 1), a.take(2, 4), a.take(2, 4)
            eq4, eq8, ing, tmp8 = a.take(2, 4), a.take(2, 8), a.take(2, 8), a.take(2, 8)
            oh1, cmb = a.take(2, 8), a.take(2, 32)
            h_tok = a.take(2, D)
            X = AX.X

            def route(g):
                for b in range(2):
                    for k in range(KT):
                        ins = g.matmul(banks[0][:, b * 36:(b + 1) * 36], h[:, k, b * P:(b + 1) * P],
                                       col("w_route", (l * KT + k) * 36, 36), start=(k == 0), stop=(k == KT - 1))
                return ins
            done = PE.do(route)
            bias = col("b_route", l * 36, 36).unsqueeze(1).broadcast_to([P, 2, 36])
            tt(V, lg[:, :, :], banks[0][:, 0:72].rearrange("p (b n) -> p b n", b=2), bias, ALU.add, done)

            def reduce(o, i, op):
                return V.do(lambda g: g.tensor_reduce(o, i, X, op))

            def first_max(dst, src, mx, n, eq, rank):
                reduce(mx, src, ALU.max)
                tt(V, eq, src, mx.broadcast_to([P, 2, n]), ALU.is_equal)
                tt(V, eq, eq, rank.unsqueeze(1).broadcast_to([P, 2, n]), ALU.mult)
                reduce(top[:, :, 3:4], eq, ALU.max)
                return tt(V, dst, eq, top[:, :, 3:4].broadcast_to([P, 2, n]), ALU.is_equal)
            first_max(eq4[:, :, :], lg[:, :, 0:4], gmx[:, :, :], 4, eq4[:, :, :], col("rank4", 0, 4))
            d = tt(V, ex[:, :, 0:4], lg[:, :, 0:4], gmx[:, :, :].broadcast_to([P, 2, 4]), ALU.subtract)
            d = act(ex[:, :, 0:4], ex[:, :, 0:4], ACT.Exp, d)
            for b in range(2):
                for c in range(2):
                    bank = banks[2 + 2 * b + c]

                    def turn_h(g, b=b, c=c, bank=bank):
                        for k in range(4):
                            ins = g.transpose(bank[:, k * P:(k + 1) * P], h[:, 4 * c + k, b * P:(b + 1) * P], ident)
                        return ins
                    copy(S, h_tok[:, b, 512 * c:512 * c + 512], bank[:, :], PE.do(turn_h))
            V.do(lambda g: g.tensor_reduce(w1[:, :, 0:1], ex[:, :, 0:4], X, ALU.add), d)
            recip(w1[:, :, 0:1], w1[:, :, 0:1])
            for g_ in range(N_GROUPS):
                sel_g = eq4[:, :, g_:g_ + 1].broadcast_to([P, 2, 8])
                dst = ing if g_ == 0 else tmp8
                tt(V, dst[:, :, :], lg[:, :, 4 + 8 * g_:12 + 8 * g_], sel_g, ALU.mult)
                if g_:
                    tt(V, ing[:, :, :], ing[:, :, :], tmp8[:, :, :], ALU.add)
            first_max(oh1[:, :, :], ing[:, :, :], top[:, :, 0:1], 8, eq8[:, :, :], col("rank8", 0, 8))
            stt(tmp8[:, :, :], oh1[:, :, :], -BIG, ing[:, :, :], ALU.mult, ALU.add)
            first_max(eq8[:, :, :], tmp8[:, :, :], top[:, :, 1:2], 8, eq8[:, :, :], col("rank8", 0, 8))
            d = tt(V, top[:, :, 2:3], top[:, :, 1:2], top[:, :, 0:1], ALU.subtract)
            d = act(top[:, :, 2:3], top[:, :, 2:3], ACT.Exp, d)
            ts(V, w1[:, :, 1:2], top[:, :, 2:3], 1.0, None, ALU.add, None, d)
            recip(w1[:, :, 1:2], w1[:, :, 1:2])
            tt(V, w1[:, :, 2:3], w1[:, :, 1:2], w1[:, :, 0:1], ALU.mult)
            tt(V, w1[:, :, 3:4], w1[:, :, 2:3], top[:, :, 2:3], ALU.mult)
            tt(V, oh1[:, :, :], oh1[:, :, :], w1[:, :, 2:3].broadcast_to([P, 2, 8]), ALU.mult)
            tt(V, eq8[:, :, :], eq8[:, :, :], w1[:, :, 3:4].broadcast_to([P, 2, 8]), ALU.mult)
            tt(V, oh1[:, :, :], oh1[:, :, :], eq8[:, :, :], ALU.add)
            for g_ in range(N_GROUPS):
                d = tt(V, cmb[:, :, 8 * g_:8 * g_ + 8], oh1[:, :, :],
                       eq4[:, :, g_:g_ + 1].broadcast_to([P, 2, 8]), ALU.mult)

            onehot = eq4[:, :, :]
            rank, slot, count = a.take(2, 4), a.take(2, 1), a.take(4)
            before = col("before", 0, P)

            def ranks(g):
                g.matmul(banks[1][:, 0:4], before, onehot[:, 0, :], start=True, stop=True)
                g.matmul(banks[1][:, 4:8], ones, onehot[:, 0, :], start=True, stop=False)
                g.matmul(banks[1][:, 4:8], before, onehot[:, 1, :], start=False, stop=True)
                g.matmul(banks[1][:, 8:12], ones, onehot[:, 0, :], start=True, stop=False)
                return g.matmul(banks[1][:, 8:12], ones, onehot[:, 1, :], start=False, stop=True)
            done = PE.do(ranks, d)
            V.do(lambda g: g.tensor_reduce(count[:, 0:1], banks[1][:, 8:12], X, ALU.max), done)
            flagged = ts(V, overflow[:, :], count[:, 0:1], float(GROUP_SLOTS), None, ALU.is_gt, None)
            tt(V, rank[:, :, :], banks[1][:, 0:8].rearrange("p (b n) -> p b n", b=2),
               col("group_base", 0, 4).unsqueeze(1).broadcast_to([P, 2, 4]), ALU.add)
            tt(V, rank[:, :, :], rank[:, :, :], onehot, ALU.mult)
            reduce(slot[:, :, :], rank[:, :, :], ALU.add)
            join()
            base = a.at

            def gathered_experts():
                a.at = base
                pick = a.take(2, N_SLOTS)
                gath = a.take(KT, N_SLOTS)
                pick_t, w_slot = a.take(N_GROUPS, T), a.take(N_GROUPS, PER_GROUP)
                silu, hid, hid_t = a.take(2, FE), a.take(2, FE), a.take(2, 2, P)
                y_slot = a.take(N_GROUPS, D)
                for b in range(2):
                    d = ts(V, pick[:, b, :], col("slot_no", 0, N_SLOTS), slot[:, b, :], None, ALU.is_equal, None)
                rot = Banks([2, 3, 4, 5, 6, 7, 0, 1])
                h_ready = None
                for k in range(KT):
                    i, bank, free = rot.take()

                    def gather(g, k=k, bank=bank):
                        g.matmul(bank[:, :], h_tok[:, 0, k * P:(k + 1) * P], pick[:, 0, :], start=True, stop=False)
                        return g.matmul(bank[:, :], h_tok[:, 1, k * P:(k + 1) * P], pick[:, 1, :],
                                        start=False, stop=True)
                    done = PE.do(gather, free, h_ready, d)
                    rot.free[i] = copy((S, V)[k % 2], gath[:, k, :], bank[:, :], done)
                gath_ready = [S.last(), V.last()]
                for j in range(2):
                    i, bank, free = rot.take()

                    def turn_pick(g, j=j, bank=bank):
                        for n in range(2):
                            for b in range(2):
                                ins = g.transpose(bank[:, n * T + b * P:n * T + (b + 1) * P],
                                                  pick[:, b, (2 * j + n) * P:(2 * j + n + 1) * P], ident)
                        return ins
                    done = PE.do(turn_pick, free, d)
                    rot.free[i] = copy(V, pick_t[:, 2 * j:2 * j + 2, :],
                                       bank[:, :].rearrange("p (n t) -> p n t", t=T), done)
                i, bank, free = rot.take()

                def slot_weights(g, bank=bank):
                    for n in range(N_GROUPS):
                        for b in range(2):
                            ins = g.matmul(bank[:, n * 8:(n + 1) * 8], pick[:, b, n * P:(n + 1) * P], oh1[:, b, :],
                                           start=(b == 0), stop=(b == 1))
                    return ins
                done = PE.do(slot_weights, free)
                copy(V, w_slot[:, :, :], bank[:, 0:32].rearrange("p (n e) -> p n e", e=8), done)
                PE.held = PE.held + [S.last(), V.last()]
                PE.pad_to(pe_start + PRELUDE)

                gu_free, turn_free, y_free = [None, None], [None, None], None
                hid_ready, hid_t_ready, hid_t_free, hid_free = [None] * 2, [None] * 2, [None] * 2, [None] * 2
                for e in range(N_EXPERTS + 1):
                    if e < N_EXPERTS:
                        p, grp = e % 2, e // PER_GROUP
                        w, landed, chunk = weight("gate_up", l, e)
                        wv = w.rearrange("p (k n) -> p k n", k=KT)

                        def gate_up(g, lo, hi, wv=wv, p=p, grp=grp):
                            for k in range(lo, hi):
                                ins = g.matmul(banks[4 + p][:, :], gath[:, k, grp * P:(grp + 1) * P], wv[:, k, :],
                                               start=(k == 0), stop=(k == KT - 1))
                            return ins
                        PE.do(lambda g, f=gate_up: f(g, 0, 4), landed, gu_free[p], *gath_ready)
                    if e > 0:
                        q = (e - 1) % 2

                        def turn_hid(g, q=q):
                            for f in range(2):
                                ins = g.transpose(banks[6 + q][:, f * P:(f + 1) * P], hid[:, q, f * P:(f + 1) * P],
                                                  ident)
                            return ins
                        hid_free[q] = PE.do(turn_hid, hid_ready[q], turn_free[q])
                        turn_free[q] = hid_t_ready[q] = copy(
                            S, hid_t[:, q, :, :], banks[6 + q][:, 0:FE].rearrange("p (f t) -> p f t", t=P),
                            hid_free[q], hid_t_free[q])
                    if e < N_EXPERTS:
                        done = consumed_step(chunk, PE.do(lambda g, f=gate_up: f(g, 4, KT)))
                        s = act(silu[:, p, :], banks[4 + p][:, 0:FE], ACT.Silu, done, hid_ready[p])
                        gu_free[p] = hid_ready[p] = stt(hid[:, p, :], silu[:, p, :],
                                                        w_slot[:, grp, e % PER_GROUP:e % PER_GROUP + 1],
                                                        banks[4 + p][:, FE:2 * FE], ALU.mult, ALU.mult, s, hid_free[p])
                    if e > 0:
                        j = e - 1
                        q, grp = j % 2, j // PER_GROUP
                        w, landed, chunk = weight("down", l, j)
                        wv = w.rearrange("p (k n) -> p k n", k=2)

                        def down(g, q=q, j=j, wv=wv):
                            for f in range(2):
                                for c in range(2):
                                    ins = g.matmul(banks[c][:, :], hid_t[:, q, f, :],
                                                   wv[:, f, 512 * c:512 * (c + 1)],
                                                   start=(j % PER_GROUP == 0 and f == 0),
                                                   stop=(j % PER_GROUP == PER_GROUP - 1 and f == 1))
                            return ins
                        hid_t_free[q] = consumed_step(chunk, PE.do(down, landed, hid_t_ready[q], y_free))
                        if j % PER_GROUP == PER_GROUP - 1:
                            for c in range(2):
                                y_free = copy(V, y_slot[:, grp, 512 * c:512 * (c + 1)], banks[c][:, :],
                                                       hid_t_free[q])
                    beside_expert(e)
                ada.settle()
                PE.held = PE.held + [V.last()]
                def scatter(g):
                    for m in range(KT):
                        for n in range(N_GROUPS):
                            ins = g.matmul(banks[m // 2][:, (m % 2) * T:(m % 2 + 1) * T],
                                           y_slot[:, n, m * P:(m + 1) * P], pick_t[:, n, :],
                                           start=(n == 0), stop=(n == N_GROUPS - 1))
                    return ins
                PE.do(scatter, V.last())

            def dense_experts():
                a.at = base
                comb = a.take(N_EXPERTS, T)
                comb_t = a.take(T)
                def turn(g):
                    for b in range(2):
                        ins = g.transpose(banks[1][0:32, b * P:(b + 1) * P], cmb[:, b, :], ident)
                    return ins
                done = PE.do(turn)
                d = copy(V, comb_t[0:32, :], banks[1][0:32, 0:T], done)
                rot = Banks([2, 3])
                for e in range(0, N_EXPERTS, 2):
                    i, bank, free = rot.take()

                    def spread(g, e=e, bank=bank):
                        for j in range(2):
                            ins = g.matmul(bank[:, j * T:(j + 1) * T],
                                           ident[0:32, e + j:e + j + 1].broadcast_to([32, P]), comb_t[0:32, :],
                                           start=True, stop=True)
                        return ins
                    done = PE.do(spread, free, d)
                    rot.free[i] = copy(S, comb[:, e:e + 2, :], bank[:, :].rearrange("p (a t) -> p a t", t=T), done)
                join()
                PE.pad_to(pe_start + PRELUDE)

                silu, hid = a.take(2, 2, T), a.take(2, 2, T)
                hid_free, pair_free = [None, None], [None, None]
                hid_ready = [None, None]
                for e in range(N_EXPERTS + 1):
                    if e < N_EXPERTS:
                        p = e % 2
                        gate, up = banks[4], banks[5]
                        w, landed, chunk = weight("gate_up", l, e)
                        wv = w.rearrange("p (k n) -> p k n", k=KT)

                        def half(g, bank, base, wv=wv):
                            for m in range(2):
                                for k in range(KT):
                                    ins = g.matmul(bank[:, m * T:(m + 1) * T], wv[:, k, base + m * P:base + (m + 1) * P],
                                                   h[:, k, :], start=(k == 0), stop=(k == KT - 1))
                            return ins
                        done_g = PE.do(lambda g, gate=gate, half=half: half(g, gate, 0), landed, pair_free[1 - p])
                        s = act(silu[:, p, :, :], gate[:, :].rearrange("p (a t) -> p a t", t=T), ACT.Silu, done_g,
                                hid_ready[p])
                        if e > 0:
                            PE.pad_to(PE.count + 1)
                        done_u = PE.do(lambda g, up=up, half=half: half(g, up, FE))
                        consumed_step(chunk, done_u)
                        upv = up[:, :].rearrange("p (a t) -> p a t", t=T)
                        pair_free[p] = tt(V, silu[:, p, :, :], silu[:, p, :, :], upv, ALU.mult, done_u, s)
                        hid_ready[p] = tt(V, hid[:, p, :, :], silu[:, p, :, :],
                                          comb[:, e, :].unsqueeze(1).broadcast_to([P, 2, T]), ALU.mult, hid_free[p])
                    else:
                        PE.pad_to(PE.count + 1)
                    if e > 0:
                        q = (e - 1) % 2
                        w, landed, chunk = weight("down", l, e - 1)
                        wv = w.rearrange("p (k n) -> p k n", k=2)

                        def down(g, e=e - 1, q=q, wv=wv):
                            for f in range(2):
                                for m in range(KT):
                                    ins = g.matmul(banks[m // 2][:, (m % 2) * T:(m % 2 + 1) * T],
                                                   wv[:, f, m * P:(m + 1) * P], hid[:, q, f, :],
                                                   start=(e == 0 and f == 0 and m % 2 == 0),
                                                   stop=(e == N_EXPERTS - 1 and f == 1), skip_group_check=True)
                            return ins
                        hid_free[q] = consumed_step(chunk, PE.do(down, landed, hid_ready[q]))
                    beside_expert(e)
                ada.settle()

            pe_start, v_start = PE.count, V.count
            PRELUDE, V_PRELUDE, V_STEPS = 24, 40, 16
            ada_end = 12 * (l + 2)
            ada.settle()
            ada_start = ada.state()

            def beside_expert(e):
                V.pad_to(v_start + V_PRELUDE + V_STEPS * e)
                if ada.begun < ada_end and e % 2 == 1:
                    ada.step()
            first_chunk, starts = taken[0], [(e, e.count, e.steps, e.held) for e in (PE, V, S)]
            paths = []
            for path in (gathered_experts, dense_experts):
                taken[0] = first_chunk
                for e, n, _, held in starts:
                    e.count, e.steps, e.held = n, [], list(held)
                ada.restore(ada_start)
                ada.bank = banks[2 if path is gathered_experts else 6]
                path()
                paths.append([(e.count, e.steps) for e, _, _, _ in starts])
            for n, (e, _, before_branch, held) in enumerate(starts):
                top_count = max(paths[0][n][0], paths[1][n][0])
                for count_, steps in (paths[0][n], paths[1][n]):
                    e.count, e.steps = count_, steps
                    e.pad_to(top_count)
                e.steps, e.held = before_branch, []
                e.steps.append(([flagged] + held, ("branch", overflow[0:1, 0:1], paths[1][n][1], paths[0][n][1])))
            ada.bank, ada.acc_free, ada.bank_free = banks[2], [None, None], None
            join()
            scattered = PE.last()
            for m in range(KT):
                stt(x[:, m, :], banks[m // 2][:, (m % 2) * T:(m % 2 + 1) * T], mod[:, 40 + m:41 + m], x[:, m, :],
                    ALU.mult, ALU.add, scattered if m == 0 else None)
                x_squares.add(S, x, m, 1, V.last())

        def gated_residual(mod, y, gain, gate_at, norm_follows=True):
            col2 = small[:, 8:16]
            tt(V, col2, mod[:, gate_at:gate_at + 8], gain, ALU.mult)
            r = y_squares.inverse()
            for k in range(KT):
                stt(y[:, k, :], y[:, k, :], col2[:, k:k + 1], rstd, ALU.mult, ALU.mult, r)
                tt(V, x[:, k, :], x[:, k, :], y[:, k, :], ALU.add)
                if norm_follows:
                    x_squares.add(S, x, k, 1, V.last())

        def project_out(name, src, y):
            rot = Banks([0, 1, 2, 3])
            for c in range(2):
                def evacuate(m0, bank, done, c=c):
                    free = copy(S, y[:, 4 * c + m0:4 * c + m0 + 2, :], bank, done)
                    y_squares.add(V, y, 4 * c + m0, 2, free)
                    return free
                w, landed, chunk = weight(name, 0, c)
                features(rot, w, landed, chunk, 512, src, KT, evacuate)

        def rglru(l, h_ready):
            join()
            a = Arena()
            xc, gate = a.take(KT, T), a.take(KT, T)
            r_, i_, decay, mult = a.take(KT, T), a.take(KT, T), a.take(KT, T), a.take(KT, T)
            sp = small[:, 16:32]
            rot = Banks([0, 1, 2, 3])
            lam = col("rg_lambda", 0, KT)
            d = stt(sp[:, 0:8], lam, -1.0, lam, ALU.mult, ALU.max)
            act(sp[:, 0:8], sp[:, 0:8], ACT.Exp, d, scale=-1.0)
            d = act(sp[:, 0:8], sp[:, 0:8], ACT.Ln, bias=col("one"))
            ts(V, sp[:, 8:16], lam, -1.0, 0.0, ALU.mult, ALU.max, d)
            tt(V, sp[:, 8:16], sp[:, 8:16], sp[:, 0:8], ALU.add)
            ts(V, sp[:, 0:8], sp[:, 8:16], -RG_C, None, ALU.mult, None)
            ts(V, sp[:, 8:16], sp[:, 8:16], RG_C, None, ALU.mult, None)

            def convolve(m0, bank, done, c):
                m = 4 * c + m0
                return causal_conv(bank, [xc[:, m + j, :] for j in range(2)], done,
                                   lambda j, tap: col("rg_conv_w", tap * KT + m + j),
                                   lambda j: col("rg_conv_b", m + j), RG_CONV)
            for c in range(2):
                w, landed, chunk = weight("rg_in", 0, 2 + c)
                features(rot, w, landed, chunk, 512, h, KT,
                         lambda m0, bank, done, c=c: convolve(m0, bank, done, c), h_ready)
            conv_done = V.last()
            gw, g_landed, g_chunk = weight("rg_gates", 0, 0)
            gv = gw.rearrange("p (w b k n) -> p w b k n", w=2, b=RG_BLOCKS, k=2)
            for which, (dst, bias) in enumerate(((r_, "rg_ba"), (i_, "rg_bx"))):
                for b in range(RG_BLOCKS):
                    i, bank, free = rot.take()

                    def emit(g, which=which, b=b, bank=bank):
                        for m in range(2):
                            for k in range(2):
                                ins = g.matmul(bank[:, m * T:(m + 1) * T], gv[:, which, b, k, m * P:(m + 1) * P],
                                               xc[:, 2 * b + k, :], start=(k == 0), stop=(k == 1))
                        return ins
                    done = PE.do(emit, g_landed, conv_done, free)
                    for m in range(2):
                        rot.free[i] = act(dst[:, 2 * b + m, :], bank[:, m * T:(m + 1) * T], ACT.Sigmoid, done,
                                          bias=col(bias, 2 * b + m))
            consumed[g_chunk] = PE.last()
            gates_ready = S.last()
            for m in range(KT):
                act(decay[:, m, :], r_[:, m, :], ACT.Exp, scale=sp[:, m:m + 1])
                e = act(mult[:, m, :], r_[:, m, :], ACT.Tanh, scale=sp[:, 8 + m:9 + m])
            tt(V, i_[:, :, :], i_[:, :, :], xc[:, :, :], ALU.mult, e)
            d = ts(V, r_[:, :, :], mult[:, :, :], 2.0, TANH_FLOOR, ALU.mult, ALU.max, e)
            act(r_[:, :, :], r_[:, :, :], ACT.Ln, d)
            e = act(mult[:, :, :], mult[:, :, :], ACT.Ln, bias=col("one"))
            d = tt(V, mult[:, :, :], r_[:, :, :], mult[:, :, :], ALU.subtract, e)
            e = act(mult[:, :, :], mult[:, :, :], ACT.Exp, d, scale=0.5)
            tt(V, i_[:, :, :], i_[:, :, :], mult[:, :, :], ALU.mult, e)
            for m in range(KT):
                V.do(lambda g, m=m: g.tensor_tensor_scan(r_[:, m, :], decay[:, m, :], i_[:, m, :], 0.0,
                                                         ALU.mult, ALU.add))
            for c in range(2):
                def gated(m0, bank, done, c=c):
                    tiles = slice(4 * c + m0, 4 * c + m0 + 2)
                    free = act(gate[:, tiles, :], bank, ACT.Gelu_apprx_tanh, done)
                    tt(V, xc[:, tiles, :], gate[:, tiles, :], r_[:, tiles, :], ALU.mult, free)
                    return free
                run(chunk_features("rg_in", 0, c, rot, 512, h, KT, gated, gates_ready))
            join()
            project_out("rg_out", xc, decay)
            return decay

        def gla(l, h_ready):
            join()
            a = Arena()
            q, k, cum = a.take(4, T), a.take(4, T), a.take(4, T)
            v_tok, silu_r = a.take(2, D), a.take(KT, T)
            z = a.take(T)
            lgt = a.take(4, T)
            ones_row = a.take(T)
            rot = Banks([0, 1, 2, 3])
            V.do(lambda g: g.memset(ones_row, 1.0))
            w_z = col("gla_w_z", 0, KT * GLA_RANK).rearrange("p (k n) -> p k n", k=KT)

            def z_product(g):
                for kk in range(KT):
                    ins = g.matmul(banks[4][0:GLA_RANK, 0:T], w_z[:, kk, :], h[:, kk, :],
                                   start=(kk == 0), stop=(kk == KT - 1))
                return ins
            done = PE.do(z_product, h_ready)
            d = copy(V, z[0:GLA_RANK, :], banks[4][0:GLA_RANK, 0:T], done)

            def alpha(g):
                for m in range(4):
                    ins = g.matmul(banks[5 + m // 2][:, (m % 2) * T:(m % 2 + 1) * T],
                                   tab[0:GLA_RANK, OFFSET["gla_w_alpha"] + m * P:OFFSET["gla_w_alpha"] + (m + 1) * P],
                                   z[0:GLA_RANK, :], start=True, stop=True)
                return ins
            done = PE.do(alpha, d)
            for m in range(4):
                d = ts(V, lgt[:, m, :], banks[5 + m // 2][:, (m % 2) * T:(m % 2 + 1) * T],
                       col("gla_b_alpha", m), None, ALU.add, None, done)
            ab = a.take(4, T)
            d = stt(ab[:, :, :], lgt[:, :, :], -1.0, lgt[:, :, :], ALU.mult, ALU.max)
            act(ab[:, :, :], ab[:, :, :], ACT.Exp, d, scale=-1.0)
            d = act(ab[:, :, :], ab[:, :, :], ACT.Ln, bias=col("one"))
            stt(lgt[:, :, :], lgt[:, :, :], 0.0, ab[:, :, :], ALU.min, ALU.subtract, d)
            ts(V, lgt[:, :, :], lgt[:, :, :], 1.0 / GLA_TAU, None, ALU.mult, None)
            for m in range(4):
                V.do(lambda g, m=m: g.tensor_tensor_scan(cum[:, m, :], ones_row, lgt[:, m, :], 0.0,
                                                         ALU.mult, ALU.add))
            w, landed, chunk = weight("gla_in", 0, 1)
            features(rot, w, landed, chunk, 512, h, KT,
                     lambda m0, bank, done: copy(S, k[:, m0:m0 + 2, :], bank, done))
            w, landed, chunk = weight("gla_in", 0, 0)
            features(rot, w, landed, chunk, 512, h, KT,
                     lambda m0, bank, done: S.do(lambda g: g.activation(
                         q[:, m0:m0 + 2, :], bank, ACT.Copy, bias=0.0, scale=GLA_DK ** -0.5), done))
            beside = Background(*[chunk_tokens(
                "gla_in", 0, 2 + c, rot, h,
                lambda b, bank, done, c=c: copy(S, v_tok[:, b, 512 * c:512 * (c + 1)], bank, done))
                for c in range(2)], *[chunk_features(
                    "gla_in", 0, 4 + c, rot, 512, h, KT,
                    lambda m0, bank, done, c=c: copy(S, silu_r[:, 4 * c + m0:4 * c + m0 + 2, :], bank, done))
                    for c in range(2)])
            pair = Banks([6, 7])
            pair.free[6] = V.last()
            qk_ready = S.last()
            scores, done = leveled_scores(q, k, cum, [(n, 0, P) for n in range(4)], 4, a, pair,
                                          beside.step, qk_ready)
            beside.finish()
            o = h
            out_free = [S.last(), PE.last()]
            act(silu_r[:, :, :], silu_r[:, :, :], ACT.Silu)
            for n in range(GLA_HEADS):
                for j in range(2):
                    m = 2 * n + j
                    last = weighted_values(banks[m // 2], slice(0, P), j * T,
                                           [v_tok[:, b, m * P:(m + 1) * P] for b in range(2)],
                                           scores[:, n, :], done, *out_free)
                copy(S, o[:, 2 * n:2 * n + 2, :], banks[n][:, :].rearrange("p (a t) -> p a t", t=T), last)
            sq = v_tok.rearrange("p a b -> p (a b)").rearrange("p (a b) -> p a b", b=T)
            group_rstd, r = group_rms(o, GLA_HEADS, sq, [banks[4], banks[5]])
            tt(V, o[:, :, :], o[:, :, :], silu_r[:, :, :], ALU.mult)
            for n in range(GLA_HEADS):
                for j in range(2):
                    m = 2 * n + j
                    stt(o[:, m, :], o[:, m, :], col("gla_norm_g", j), group_rstd[:, n, :], ALU.mult, ALU.mult, r)
            join()
            y = arena[:, 0:2048].rearrange("p (a b) -> p a b", b=T)
            project_out("gla_out", o, y)
            return y

        def conv_ffn(l, h_ready):
            join()
            a = Arena()
            y = a.take(KT, T)
            act_t = a.take(FT, T)
            tmp = a.take(2, 4, T)
            rot = Banks([0, 1, 3, 5, 6, 7])
            buf_free = [None, None]
            for c in range(FT // 2):
                w, landed, chunk = weight("ffn_up", l, c)
                buf = tmp[:, c % 2, :, :]

                def convolve(m0, bank, done, c=c, buf=buf):
                    m = (0 if m0 == 0 else FT) + 2 * c
                    f = causal_conv(bank, [buf[:, m0 + j, :] for j in range(2)], done,
                                    lambda j, tap: col("ffn_conv_w", (l * FFN_CONV + tap) * 2 * FT + m + j),
                                    lambda j: col("ffn_conv_b", l * 2 * FT + m + j), FFN_CONV, buf_free[c % 2])
                    if m0 == 0:
                        act(buf[:, 0:2, :], buf[:, 0:2, :], ACT.Gelu_apprx_tanh, f)
                    else:
                        buf_free[c % 2] = tt(V, act_t[:, 2 * c:2 * c + 2, :], buf[:, 0:2, :], buf[:, 2:4, :],
                                             ALU.mult, S.last())
                    return f
                features(rot, w, landed, chunk, 512, h, KT, convolve, h_ready)
                ada.step()
            ready = V.last()
            for m in range(KT):
                w, landed, chunk = weight("ffn_down", l, m)

                def evacuate(m0, bank, done, m=m):
                    free = copy(S, y[:, m:m + 1, :], bank, done)
                    y_squares.add(V, y, m, 1, free)
                    return free
                features(rot, w, landed, chunk, P, act_t, FT, evacuate, ready)
            return y

        for which, name in ((0, "c"), (1, "c_2")):
            act(c_act[:, 8 * which:8 * which + 8], col(name, 0, 8), ACT.Silu, TABLE)
        lb, tmp4 = col("hgrn_lb", 0, 4), lower[:, 8:16]
        tt(V, tmp4[:, 0:2], lb[:, 0:2], lb[:, 2:4], ALU.max, TABLE)
        tt(V, lower[:, 0:2], lb[:, 0:2], tmp4[:, 0:2], ALU.subtract)
        d = tt(V, lower[:, 2:4], lb[:, 2:4], tmp4[:, 0:2], ALU.subtract)
        d = act(lower[:, 0:4], lower[:, 0:4], ACT.Exp, d)
        tt(V, tmp4[:, 0:2], lower[:, 0:2], lower[:, 2:4], ALU.add, d)
        recip(tmp4[:, 2:4], tmp4[:, 0:2])
        tt(V, lower[:, 0:2], lower[:, 0:2], tmp4[:, 2:4], ALU.mult)
        tt(V, lower[:, 2:4], lower[:, 2:4], tmp4[:, 2:4], ALU.mult)
        tt(V, lower[:, 2:4], lower[:, 0:2], lower[:, 2:4], ALU.add)
        tt(V, lower[:, 2:4], lower[:, 2:4], lower[:, 0:2], ALU.subtract)
        tt(V, lower[:, 0:2], lower[:, 0:2], lower[:, 0:2], ALU.subtract)
        ts(V, lower[:, 4:8], lower[:, 0:4], -1.0, 1.0, ALU.mult, ALU.add)
        x_squares = MeanSquare(banks[7])
        y_squares = MeanSquare(banks[4])
        while ada.begun < 4:
            ada.step()
        for k in range(KT):
            x_squares.add(S, x, k, 1, X_IN)
        x_squares.flush()

        for l in range(DEPTH):
            mod = mods[:, 48 * l:48 * l + 48]
            ada.through(l, 4)
            ready = modulated_norm(mod, col("norm_mix_g", 8 * l, 8), 0, 8)
            if l == 0:
                for e in (PE, V, S, G):
                    e.held = e.held + [TABLE_LATER]
            token_mixer(l, mod, ready)
            ada.through(l, 12)
            modulated_norm(mod, col("norm_ffn_g", 8 * l, 8), 24, 32)
            moe(l, mod)
        r = x_squares.inverse()
        for k in range(KT):
            stt(x[:, k, :], x[:, k, :], col("final_g", k), rstd, ALU.mult, ALU.mult, r)
            x_squares.add(S, x, k, 1, V.last())

        for l in range(DEPTH):
            mod = mods[:, 48 * (2 + l):48 * (2 + l) + 48]
            ada.through(2 + l, 12)
            ready = modulated_norm(mod, col("norm_g_2", (4 * l) * 8, 8), 0, 8)
            y = (rglru if l == 0 else gla)(l, ready)
            gated_residual(mod, y, col("norm_g_2", (4 * l + 1) * 8, 8), 16)
            ready = modulated_norm(mod, col("norm_g_2", (4 * l + 2) * 8, 8), 24, 32)
            y = conv_ffn(l, ready)
            gated_residual(mod, y, col("norm_g_2", (4 * l + 3) * 8, 8), 40, l + 1 < DEPTH)
        finished = V.last()
        assert taken[0] == len(order) == len(sizes)

        block = ctx.enter_context(nc.Block())

        @block.sync
        def _(sp):
            first = OFFSET[FIRST_LATER]
            sp.dma_start(tab[:, 0:first], table[:, 0:first]).then_inc(s_table, 16)
            for k, (start, n, off) in enumerate(where):
                if k == 4:
                    sp.dma_start(x.rearrange("p k t -> p (k t)"), x_in).then_inc(s_x, 16)
                    sp.dma_start(tab[:, first:], table[:, first:]).then_inc(s_later, 16)
                for j in reuse[k]:
                    sp.wait_ge(*consumed[j])
                sp.dma_start(ring[:, start:start + n],
                             weights[off:off + n * P].rearrange("(p n) -> p n", p=P)
                             ).then_inc(s_ring[k % RING_UNITS], 16)
            sp.wait_ge(*finished)
            sp.dma_start(out, x.rearrange("p k t -> p (k t)")).then_inc(s_out, 16)
            sp.wait_ge(s_out, 16)

        @block.tensor
        def _(eng):
            PE.play(eng)

        @block.vector
        def _(eng):
            V.play(eng)

        @block.scalar
        def _(eng):
            S.play(eng)

        @block.gpsimd
        def _(eng):
            G.play(eng)

    return order


def kernel(**inputs):
    import concourse.bacc as bacc
    from concourse.bass_utils import run_bass_kernel_spmd as run

    i = {name: np.asarray(a) for name, a in inputs.items()}

    def columns(a):
        return a.reshape(-1, P).T

    def chunk(w):
        return w.reshape(-1, P, w.shape[1]).transpose(1, 0, 2).reshape(P, -1)

    def wide(a):
        return np.pad(a, ((0, P - a.shape[0]), (0, 0)))

    s_, t_ = np.arange(P)[:, None], np.arange(T)[None, :]
    causal = np.concatenate([s_ <= t_, s_ + P <= t_[:, P:]], axis=1)
    lag = np.concatenate([t_ - s_, t_[:, P:] - s_ - P], axis=1)
    gamma = np.log1p(-np.exp2(-5.0 - np.arange(RET_HEADS)))
    decay = np.where(causal, np.exp(gamma[:, None, None] * lag * causal), 0.0) * HEAD ** -0.5
    half = HEAD // 2
    freq = (10000.0 ** (-np.arange(half, dtype=np.float32) / half)).astype(np.float32)
    angle = (np.arange(T, dtype=np.float32)[None, :] * np.tile(freq, 4)[:, None]).astype(np.float64)
    t1 = np.arange(P)[None, :]
    levels = [((s_ // (2 * n) == t1 // (2 * n)) & (s_ % (2 * n) < n) & (t1 % (2 * n) >= n)) for n in LEVELS]
    heads64 = (s_ // HEAD == t1 // HEAD)
    one = np.ones((P, 1))
    route = np.concatenate([i["w_grp"], i["w_exp"]], axis=2)
    b_route = np.concatenate([i["b_grp"], i["b_exp"]], axis=1)
    parts = {
        "c": columns(i["c"]), "c_2": columns(i["c_2"]), "final_g": columns(i["final_norm_g"]),
        "zero": np.zeros((P, 1)), "one": one, "eps": np.full((P, 1), EPS),
        "norm_mix_g": columns(i["norm_mix_g"]), "norm_ffn_g": columns(i["norm_ffn_g"]),
        "b_ada": columns(i["b_ada"]), "b_ada_2": columns(i["ada_b_2"]), "norm_g_2": columns(i["norm_g_2"]),
        "conv_w": columns(i["conv_w"]), "conv_b": columns(i["conv_b"]),
        "ssd_d": np.concatenate([columns(np.repeat(i["ssd_d"][l], HEAD)) for l in range(DEPTH)], axis=1),
        "ssd_norm_g": columns(i["ssd_norm_g"]),
        "dt_bias": wide(i["ssd_dt_bias"].T), "a_log": wide(i["ssd_a_log"].T),
        "hgrn_lb": columns(i["hgrn_lower_bounds"]), "hgrn_norm_g": columns(i["hgrn_norm_g"]),
        "b_route": np.broadcast_to(b_route.reshape(1, -1), (P, 36 * DEPTH)),
        "w_route": np.concatenate([chunk(route[l]) for l in range(DEPTH)], axis=1),
        "ffn_conv_w": columns(i["ffn_conv_w_2"]), "ffn_conv_b": columns(i["ffn_conv_b_2"]),
        "rg_conv_w": columns(i["rg_conv_w_2"]), "rg_conv_b": columns(i["rg_conv_b_2"]),
        "rg_ba": columns(i["rg_ba_2"]), "rg_bx": columns(i["rg_bx_2"]), "rg_lambda": columns(i["rg_lambda_2"]),
        "gla_b_alpha": columns(i["gla_b_alpha_2"]), "gla_norm_g": columns(i["gla_norm_g_2"]),
        "gla_w_z": chunk(i["gla_w_in_2"][0][:, 2 * 512 + 2 * D:]), "gla_w_alpha": wide(i["gla_w_alpha_2"][0]),
        "ident": np.eye(P), "ones": np.ones((P, P)),
        "mean_all": np.full((P, P), 1.0 / D), "mean_256": np.full((P, P), 1.0 / 256),
        "mean_head": heads64 / HEAD,
        "neg_mask": np.where(causal, 0.0, -BIG), "level_mask": np.concatenate(levels, axis=1),
        "cos": np.cos(angle), "sin": np.sin(angle),
        "ret_decay": np.concatenate(list(decay), axis=1),
        "rank4": np.broadcast_to(np.arange(4, 0, -1), (P, 4)), "rank8": np.broadcast_to(np.arange(8, 0, -1), (P, 8)),
        "before": s_ < t1, "slot_no": np.broadcast_to(np.arange(N_SLOTS), (P, N_SLOTS)),
        "group_base": np.broadcast_to(GROUP_SLOTS * np.arange(N_GROUPS), (P, N_GROUPS)),
    }
    for name, width in COLS.items():
        assert parts[name].shape == (P, width), (name, parts[name].shape, width)
    table = np.concatenate([np.asarray(parts[name], np.float32) for name in COLS], axis=1)

    off = np.cumsum([0, 512, 768, 8] + [256] * 8)
    z, xbc, dt, hq, hf, hi, hg, rq, rk, rv, rg = [np.arange(off[n], off[n + 1]) for n in range(11)]

    def by_halves(cols):
        return cols.reshape(RET_HEADS, 2, half).transpose(1, 0, 2).reshape(-1)
    in_cols = [xbc[:512], np.concatenate([xbc[512:], dt]), np.concatenate([hf, hq]), np.concatenate([hi, rv]),
               np.concatenate([by_halves(rq), by_halves(rk)]), z, np.concatenate([hg, rg])]

    def piece(name, l, n):
        span = slice(512 * n, 512 * n + 512)
        if name == "ada":
            return chunk(i["w_ada"][l][:, span])
        if name == "ada_2":
            return chunk(i["ada_w_2"][l][:, span])
        if name == "in":
            return chunk(i["w_in"][l][:, in_cols[n]])
        if name == "out":
            return chunk(i["w_out"][l][:, span])
        if name == "gate_up":
            return chunk(np.concatenate([i["w_gate"][l, n], i["w_up"][l, n]], axis=1))
        if name == "down":
            return chunk(i["w_down"][l, n])
        if name == "rg_in":
            return chunk(i["rg_w_in_2"][0][:, span])
        if name == "rg_gates":
            return np.concatenate([chunk(w[0, b]) for w in (i["rg_wa_2"], i["rg_wx_2"]) for b in range(RG_BLOCKS)],
                                  axis=1)
        if name == "rg_out":
            return chunk(i["rg_w_out_2"][0][:, span])
        if name == "gla_in":
            return chunk(i["gla_w_in_2"][0][:, span])
        if name == "gla_out":
            return chunk(i["gla_w_out_2"][0][:, span])
        if name == "ffn_up":
            w = i["ffn_w_up_2"][l]
            return chunk(np.concatenate([w[:, 256 * n:256 * n + 256], w[:, D_FF + 256 * n:D_FF + 256 * n + 256]],
                                        axis=1))
        return chunk(i["ffn_w_down_2"][l][:, P * n:P * n + P])

    x_t = np.ascontiguousarray(chunk(i["x"].reshape(T, D).T))

    nc = bacc.Bacc("TRN2", target_bir_lowering=False, num_devices=1)
    sizes = chunk_sizes()
    w_ap = nc.dram_tensor("weights", (P * sum(sizes.values()),), F32, kind="ExternalInput").ap()
    t_ap = nc.dram_tensor("table", table.shape, F32, kind="ExternalInput").ap()
    x_ap = nc.dram_tensor("x_t", x_t.shape, F32, kind="ExternalInput").ap()
    o_ap = nc.dram_tensor("y_t", (P, KT * T), F32, kind="ExternalOutput").ap()
    order = two_stacks_kernel(nc, w_ap, t_ap, x_ap, o_ap)
    stream = []
    for key in order:
        p = piece(*key)
        assert p.shape == (P, sizes[key]), (key, p.shape)
        stream.append(p.reshape(-1))
    stream = np.concatenate(stream)
    got = run(nc, [{"weights": stream, "table": table, "x_t": x_t}], core_ids=[0])
    y = got.results[0]["y_t"].reshape(P, KT, T)
    return np.ascontiguousarray(y.transpose(2, 1, 0)).reshape(1, T, D)
```
